# Optimizing a Trainium2 kernel written in Bass

```python
import math
import jax, jax.numpy as jnp
from jax import lax
import numpy as np

D_MODEL = 1024
BATCH = 1
SEQ = 256
DEPTH = 2

ATTN_HEADS = 4
HEAD_DIM = 64
ATTN_W = ATTN_HEADS * 2 * HEAD_DIM
ROT_DIM = HEAD_DIM // 4
ROPE_THETA = 500000.0
Q_BLOCK = 128
CONV_W = 512
CONV_K = 31
D_FF = ((int(math.ceil(8 * D_MODEL / 3)) + 255) // 256) * 256
N_BRANCH = 2
Q_OFF = 0
K_OFF = Q_OFF + ATTN_W
V_OFF = K_OFF + ATTN_W
C_OFF = V_OFF + ATTN_W
G_OFF = C_OFF + 2 * CONV_W
N_IN = G_OFF + N_BRANCH * D_MODEL
N_MOD = 6


def rms_norm(x, g, eps=1e-6):
    xf = x.astype(jnp.float32)
    y = xf * lax.rsqrt(jnp.mean(xf * xf, axis=-1, keepdims=True) + eps)
    return (y * g.astype(jnp.float32)).astype(x.dtype)

def layer_norm(x, g, b, eps=1e-5):
    xf = x.astype(jnp.float32)
    mu = jnp.mean(xf, axis=-1, keepdims=True)
    var = jnp.mean(jnp.square(xf - mu), axis=-1, keepdims=True)
    y = (xf - mu) * lax.rsqrt(var + eps)
    return (y * g.astype(jnp.float32) + b.astype(jnp.float32)).astype(x.dtype)

def partial_rope(t, cos, sin):
    half = ROT_DIM // 2
    x1 = t[..., :half]
    x2 = t[..., half:ROT_DIM]
    rot = jnp.concatenate([x1 * cos - x2 * sin, x2 * cos + x1 * sin], axis=-1)
    return jnp.concatenate([rot, t[..., ROT_DIM:]], axis=-1)

def diff_attention(q, k, v, lam):
    b, s, h, _, d = q.shape
    scale = 1.0 / math.sqrt(d)
    qt = q.transpose(0, 2, 3, 1, 4)
    kt = k.transpose(0, 2, 3, 1, 4)
    vt = v.transpose(0, 2, 1, 3)
    k_pos = jnp.arange(s)
    neg = jnp.finfo(jnp.float32).min

    def block(i):
        start = i * Q_BLOCK
        qb = lax.dynamic_slice_in_dim(qt, start, Q_BLOCK, axis=3)
        sc = jnp.einsum('bhcqd,bhckd->bhcqk', qb, kt).astype(jnp.float32) * scale
        q_pos = start + jnp.arange(Q_BLOCK)
        mask = q_pos[:, None] >= k_pos[None, :]
        sc = jnp.where(mask, sc, neg)
        p = jax.nn.softmax(sc, axis=-1)
        a = p[:, :, 0] - lam * p[:, :, 1]
        return jnp.einsum('bhqk,bhkv->bhqv', a.astype(vt.dtype), vt)

    out = lax.map(block, jnp.arange(s // Q_BLOCK))
    out = out.transpose(1, 0, 3, 2, 4)
    return out.reshape(b, s, h, 2 * d)

def causal_depthwise_conv(u, w, bias):
    y = lax.conv_general_dilated(
        u, w.astype(u.dtype), window_strides=(1,), padding=[(CONV_K - 1, 0)],
        dimension_numbers=('NWC', 'WIO', 'NWC'), feature_group_count=u.shape[-1])
    return y + bias

def first_inputs(seed: int = 0) -> dict:
    key = jax.random.key(seed)
    ks = jax.random.split(key, 24)
    f32 = jnp.float32

    def nrm(k, shape, s):
        return jax.random.normal(k, shape, f32) * s

    L = DEPTH
    return {
        "x": nrm(ks[0], (BATCH, SEQ, D_MODEL), 1.0),
        "c": nrm(ks[1], (BATCH, D_MODEL), 1.0),
        "positions": jnp.broadcast_to(jnp.arange(SEQ, dtype=jnp.int32)[None, :], (BATCH, SEQ)),
        "ada_w": nrm(ks[2], (L, D_MODEL, N_MOD * D_MODEL), 0.1 * D_MODEL ** -0.5),
        "ada_b": nrm(ks[3], (L, N_MOD * D_MODEL), 0.01),
        "norm1_g": 1.0 + nrm(ks[4], (L, D_MODEL), 0.01),
        "w_in": nrm(ks[5], (L, D_MODEL, N_IN), D_MODEL ** -0.5),
        "lambda_q1": nrm(ks[6], (L, HEAD_DIM), 0.1),
        "lambda_k1": nrm(ks[7], (L, HEAD_DIM), 0.1),
        "lambda_q2": nrm(ks[8], (L, HEAD_DIM), 0.1),
        "lambda_k2": nrm(ks[9], (L, HEAD_DIM), 0.1),
        "subln_g": 1.0 + nrm(ks[10], (L, 2 * HEAD_DIM), 0.01),
        "w_attn_o": nrm(ks[11], (L, ATTN_W, D_MODEL), ATTN_W ** -0.5),
        "dw_conv_w": nrm(ks[12], (L, CONV_K, 1, CONV_W), CONV_K ** -0.5),
        "dw_conv_b": nrm(ks[13], (L, CONV_W), 0.01),
        "conv_ln_g": 1.0 + nrm(ks[14], (L, CONV_W), 0.01),
        "conv_ln_b": nrm(ks[15], (L, CONV_W), 0.01),
        "w_conv_o": nrm(ks[16], (L, CONV_W, D_MODEL), CONV_W ** -0.5),
        "w_out": nrm(ks[17], (L, D_MODEL, D_MODEL), D_MODEL ** -0.5),
        "norm2_g": 1.0 + nrm(ks[18], (L, D_MODEL), 0.01),
        "w_ffn_in": nrm(ks[19], (L, D_MODEL, 2 * D_FF), D_MODEL ** -0.5),
        "w_ffn_out": nrm(ks[20], (L, D_FF, D_MODEL), D_FF ** -0.5),
        "final_g": 1.0 + nrm(ks[21], (D_MODEL,), 0.01),
    }

def first_block(x, c, positions, ada_w, ada_b, norm1_g, w_in, lambda_q1, lambda_k1,
              lambda_q2, lambda_k2, subln_g, w_attn_o, dw_conv_w, dw_conv_b,
              conv_ln_g, conv_ln_b, w_conv_o, w_out, norm2_g, w_ffn_in, w_ffn_out,
              final_g):
    b, s, _ = x.shape
    inv_freq = 1.0 / (ROPE_THETA ** (jnp.arange(0, ROT_DIM, 2, dtype=jnp.float32) / ROT_DIM))
    ang = positions.astype(jnp.float32)[..., None] * inv_freq
    cos = jnp.cos(ang)[:, :, None, None, :].astype(x.dtype)
    sin = jnp.sin(ang)[:, :, None, None, :].astype(x.dtype)
    c_act = jax.nn.silu(c)

    for l in range(DEPTH):
        mod = c_act @ ada_w[l] + ada_b[l]
        shift1, scale1, gate1, shift2, scale2, gate2 = [
            m[:, None, :] for m in jnp.split(mod, N_MOD, axis=-1)]

        h = rms_norm(x, norm1_g[l]) * (1.0 + scale1) + shift1
        z = h @ w_in[l]

        q = z[..., Q_OFF:K_OFF].reshape(b, s, ATTN_HEADS, 2, HEAD_DIM)
        k = z[..., K_OFF:V_OFF].reshape(b, s, ATTN_HEADS, 2, HEAD_DIM)
        v = z[..., V_OFF:C_OFF].reshape(b, s, ATTN_HEADS, 2 * HEAD_DIM)
        q = partial_rope(q, cos, sin)
        k = partial_rope(k, cos, sin)
        lambda_init = 0.8 - 0.6 * math.exp(-0.3 * l)
        lam = (jnp.exp(jnp.sum(lambda_q1[l].astype(jnp.float32) * lambda_k1[l].astype(jnp.float32)))
               - jnp.exp(jnp.sum(lambda_q2[l].astype(jnp.float32) * lambda_k2[l].astype(jnp.float32)))
               + lambda_init)
        o = diff_attention(q, k, v, lam)
        o = rms_norm(o, subln_g[l], eps=1e-5) * (1.0 - lambda_init)
        y_attn = o.reshape(b, s, ATTN_W) @ w_attn_o[l]

        ga, gb = jnp.split(z[..., C_OFF:G_OFF], 2, axis=-1)
        u = ga * jax.nn.sigmoid(gb)
        u = causal_depthwise_conv(u, dw_conv_w[l], dw_conv_b[l])
        u = jax.nn.silu(layer_norm(u, conv_ln_g[l], conv_ln_b[l]))
        y_conv = u @ w_conv_o[l]

        g_attn, g_conv = jnp.split(jax.nn.sigmoid(z[..., G_OFF:]), N_BRANCH, axis=-1)
        mixed = (g_attn * y_attn + g_conv * y_conv) @ w_out[l]
        x = x + (1.0 + gate1) * mixed

        h2 = rms_norm(x, norm2_g[l]) * (1.0 + scale2) + shift2
        f_gate, f_up = jnp.split(h2 @ w_ffn_in[l], 2, axis=-1)
        x = x + (1.0 + gate2) * ((jax.nn.silu(f_gate) * f_up) @ w_ffn_out[l])

    return rms_norm(x, final_g)


DEPTH_2 = 1

POOL_WIDTH = D_MODEL // 2
POOL_WINDOWS = (2, 4, 8, 16)
POOL_GROUPS = len(POOL_WINDOWS)
POOL_GC = POOL_WIDTH // POOL_GROUPS
ATTN_HEADS_2 = (D_MODEL // 2) // HEAD_DIM
ATTN_WIDTH = ATTN_HEADS_2 * HEAD_DIM
MOBA_BLOCK = 256
MOBA_TOPK = 3
QUERY_CHUNK = 64
ROT_DIM_2 = HEAD_DIM // 4
IN_WIDTH = 2 * POOL_WIDTH + 4 * ATTN_WIDTH + N_BRANCH * D_MODEL
EPS = 1e-6


def rms_norm_2(x, g):
    xf = x.astype(jnp.float32)
    y = xf * lax.rsqrt(jnp.mean(xf * xf, axis=-1, keepdims=True) + EPS)
    return (y * g.astype(jnp.float32)).astype(x.dtype)

def partial_rope_2(x):
    S_ = x.shape[1]
    half = ROT_DIM_2 // 2
    pos = jnp.arange(S_, dtype=jnp.float32)
    inv_freq = ROPE_THETA ** (-jnp.arange(0, ROT_DIM_2, 2, dtype=jnp.float32) / ROT_DIM_2)
    ang = pos[:, None] * inv_freq[None, :]
    cos = jnp.cos(ang)[None, :, None, :].astype(x.dtype)
    sin = jnp.sin(ang)[None, :, None, :].astype(x.dtype)
    x1 = x[..., :half]
    x2 = x[..., half:ROT_DIM_2]
    return jnp.concatenate([x1 * cos - x2 * sin, x2 * cos + x1 * sin, x[..., ROT_DIM_2:]], axis=-1)

def multiscale_pool(u, w_grp, scale):
    B_, S_, _ = u.shape
    ug = u.reshape(B_, S_, POOL_GROUPS, POOL_GC)
    uf = ug.astype(jnp.float32)
    cs = lax.cumsum(uf, axis=1)
    cs = jnp.concatenate([jnp.zeros_like(cs[:, :1]), cs], axis=1)
    t = jnp.arange(S_)
    means = []
    for g, w in enumerate(POOL_WINDOWS):
        hi = t + 1
        lo = jnp.maximum(t + 1 - w, 0)
        cnt = (hi - lo).astype(jnp.float32)[None, :, None]
        means.append((cs[:, hi, g] - cs[:, lo, g]) / cnt)
    d = (jnp.stack(means, axis=2) - uf).astype(u.dtype)
    y = jnp.einsum('bsgc,gcd->bsgd', d, w_grp).reshape(B_, S_, POOL_WIDTH)
    return y * scale

def moba_attention(q, k, v):
    B_, S_, H, Dh = q.shape
    q = q.transpose(0, 2, 1, 3)
    k = k.transpose(0, 2, 1, 3)
    v = v.transpose(0, 2, 1, 3)
    nb = -(-S_ // MOBA_BLOCK)
    s_pad = nb * MOBA_BLOCK
    pad = ((0, 0), (0, 0), (0, s_pad - S_), (0, 0))
    kb = jnp.pad(k, pad).reshape(B_, H, nb, MOBA_BLOCK, Dh)
    vb = jnp.pad(v, pad).reshape(B_, H, nb, MOBA_BLOCK, Dh)
    kmean = jnp.mean(kb.astype(jnp.float32), axis=3)
    n_sel = min(MOBA_TOPK, nb)
    nq = S_ // QUERY_CHUNK
    q_chunks = q.reshape(B_, H, nq, QUERY_CHUNK, Dh).transpose(2, 0, 1, 3, 4)
    scale = Dh ** -0.5
    bi = jnp.arange(B_)[:, None, None, None]
    hi = jnp.arange(H)[None, :, None, None]
    blk_ids = jnp.arange(nb)
    kr = jnp.arange(MOBA_BLOCK)

    def one_chunk(args):
        ci, qc = args
        q0 = ci * QUERY_CHUNK
        qblk = q0 // MOBA_BLOCK
        qpos = q0 + jnp.arange(QUERY_CHUNK)
        gate = jnp.einsum('bhqd,bhnd->bhqn', qc.astype(jnp.float32), kmean)
        gate = jnp.where(blk_ids < qblk, gate, -jnp.inf)
        _, sel = lax.top_k(gate, n_sel)
        sel_ok = sel < qblk
        ksel = kb[bi, hi, sel]
        vsel = vb[bi, hi, sel]
        s_sel = jnp.einsum('bhqd,bhqkjd->bhqkj', qc, ksel).astype(jnp.float32) * scale
        s_sel = jnp.where(sel_ok[..., None], s_sel, -jnp.inf)
        s_sel = s_sel.reshape(B_, H, QUERY_CHUNK, n_sel * MOBA_BLOCK)
        kown = lax.dynamic_index_in_dim(kb, qblk, axis=2, keepdims=False)
        vown = lax.dynamic_index_in_dim(vb, qblk, axis=2, keepdims=False)
        kpos = qblk * MOBA_BLOCK + kr
        s_own = jnp.einsum('bhqd,bhjd->bhqj', qc, kown).astype(jnp.float32) * scale
        s_own = jnp.where(kpos[None, :] <= qpos[:, None], s_own, -jnp.inf)
        p = jax.nn.softmax(jnp.concatenate([s_sel, s_own], axis=-1), axis=-1).astype(v.dtype)
        p_sel = p[..., :n_sel * MOBA_BLOCK].reshape(B_, H, QUERY_CHUNK, n_sel, MOBA_BLOCK)
        p_own = p[..., n_sel * MOBA_BLOCK:]
        return (jnp.einsum('bhqkj,bhqkjd->bhqd', p_sel, vsel)
                + jnp.einsum('bhqj,bhjd->bhqd', p_own, vown))

    out = lax.map(one_chunk, (jnp.arange(nq), q_chunks))
    return out.transpose(1, 0, 3, 2, 4).reshape(B_, S_, H * Dh)

def second_inputs(seed: int = 0) -> dict:
    key = jax.random.key(seed)
    ks = jax.random.split(key, 14)
    D = D_MODEL
    nrm = jax.random.normal
    return {
        "x": nrm(ks[0], (BATCH, SEQ, D), jnp.float32),
        "c": nrm(ks[1], (BATCH, D), jnp.float32),
        "w_ada": nrm(ks[2], (DEPTH_2, D, 3 * D), jnp.float32) * (0.3 * D ** -0.5),
        "b_ada": nrm(ks[3], (DEPTH_2, 3 * D), jnp.float32) * 0.01,
        "g_norm": 1.0 + 0.05 * nrm(ks[4], (DEPTH_2, D), jnp.float32),
        "w_in": nrm(ks[5], (DEPTH_2, D, IN_WIDTH), jnp.float32) * D ** -0.5,
        "w_pool_grp": nrm(ks[6], (DEPTH_2, POOL_GROUPS, POOL_GC, POOL_GC), jnp.float32) * POOL_GC ** -0.5,
        "pool_scale": 1.0 + 0.1 * nrm(ks[7], (DEPTH_2, POOL_WIDTH), jnp.float32),
        "w_pool_up": nrm(ks[8], (DEPTH_2, POOL_WIDTH, D), jnp.float32) * POOL_WIDTH ** -0.5,
        "w_attn_up": nrm(ks[9], (DEPTH_2, ATTN_WIDTH, D), jnp.float32) * ATTN_WIDTH ** -0.5,
        "w_out": nrm(ks[10], (DEPTH_2, D, D), jnp.float32) * D ** -0.5,
        "g_final": 1.0 + 0.05 * nrm(ks[11], (D,), jnp.float32),
    }

def second_block(x, c, w_ada, b_ada, g_norm, w_in, w_pool_grp, pool_scale, w_pool_up, w_attn_up, w_out, g_final):
    B_, S_, D = x.shape
    splits = np.cumsum([POOL_WIDTH, POOL_WIDTH, ATTN_WIDTH, ATTN_WIDTH, ATTN_WIDTH, ATTN_WIDTH, D_MODEL]).tolist()
    for l in range(DEPTH_2):
        mod = c @ w_ada[l] + b_ada[l]
        shift, scl, gate = jnp.split(mod, 3, axis=-1)
        h = rms_norm_2(x, g_norm[l]) * (1.0 + scl[:, None, :]) + shift[:, None, :]
        proj = h @ w_in[l]
        u_pool, z_pool, q, k, v, z_attn, m_pool, m_attn = jnp.split(proj, splits, axis=-1)
        y_pool = multiscale_pool(u_pool, w_pool_grp[l], pool_scale[l]) * jax.nn.silu(z_pool)
        y_pool = y_pool @ w_pool_up[l]
        q = partial_rope_2(q.reshape(B_, S_, ATTN_HEADS_2, HEAD_DIM))
        k = partial_rope_2(k.reshape(B_, S_, ATTN_HEADS_2, HEAD_DIM))
        v = v.reshape(B_, S_, ATTN_HEADS_2, HEAD_DIM)
        y_attn = moba_attention(q, k, v) * jax.nn.silu(z_attn)
        y_attn = y_attn @ w_attn_up[l]
        merged = jax.nn.sigmoid(m_pool) * y_pool + jax.nn.sigmoid(m_attn) * y_attn
        x = x + gate[:, None, :] * (merged @ w_out[l])
    return rms_norm_2(x, g_final)


CHUNK = 64
D_MIX = D_MODEL
CONV_GROUPS = 8
CONV_GROUP_DIM = 64
W_CONV = CONV_GROUPS * CONV_GROUP_DIM
CONV_K_3 = 3
LRU_HEADS = 8
LRU_HEAD_DIM = 64
W_LRU = LRU_HEADS * LRU_HEAD_DIM
LRU_CONV_K = 4
RG_C = 8.0
D_IN_TOT = 3 * W_CONV + 2 * W_LRU
D_FF_3 = 3584
N_EXPERTS = 8
TOP_K = 2
N_DENSE = (DEPTH + 1) // 2
N_MOE = DEPTH // 2


def rms_norm_3(x, g):
    xf = x.astype(jnp.float32)
    y = xf * lax.rsqrt(jnp.mean(xf * xf, axis=-1, keepdims=True) + EPS)
    return (y * g.astype(jnp.float32)).astype(x.dtype)

def causal_depthwise_conv_3(x, w):
    k = w.shape[0]
    c = x.shape[-1]
    return lax.conv_general_dilated(
        x, w[:, None, :].astype(x.dtype), window_strides=(1,), padding=[(k - 1, 0)],
        dimension_numbers=("NWC", "WIO", "NWC"), feature_group_count=c)

def chunked_linear_scan(a, b):
    bsz, s, w = a.shape
    nc = s // CHUNK
    a_c = a.reshape(bsz, nc, CHUNK, w).transpose(1, 0, 2, 3)
    b_c = b.reshape(bsz, nc, CHUNK, w).transpose(1, 0, 2, 3)

    def combine(left, right):
        al, bl = left
        ar, br = right
        return al * ar, ar * bl + br

    def step(h_prev, ab):
        ac, bc = ab
        a_cum, b_cum = lax.associative_scan(combine, (ac, bc), axis=1)
        h = a_cum * h_prev[:, None, :] + b_cum
        return h[:, -1, :], h

    h0 = jnp.zeros((bsz, w), jnp.float32)
    _, hs = lax.scan(step, h0, (a_c, b_c))
    return hs.transpose(1, 0, 2, 3).reshape(bsz, s, w)

def rg_lru(x, wa, ba, wx, bx, lam):
    bsz, s, _ = x.shape
    xh = x.reshape(bsz, s, LRU_HEADS, LRU_HEAD_DIM)
    r = jax.nn.sigmoid((jnp.einsum("bshi,hij->bshj", xh, wa).reshape(bsz, s, W_LRU) + ba).astype(jnp.float32))
    i = jax.nn.sigmoid((jnp.einsum("bshi,hij->bshj", xh, wx).reshape(bsz, s, W_LRU) + bx).astype(jnp.float32))
    log_a = -RG_C * r * jax.nn.softplus(-lam.astype(jnp.float32))
    a = jnp.exp(log_a)
    b = jnp.sqrt(-jnp.expm1(2.0 * log_a)) * (i * x.astype(jnp.float32))
    return chunked_linear_scan(a, b).astype(x.dtype)

def hybrid_mixer(h, w_in, conv_w, lru_conv_w, lru_conv_b, wa, ba, wx, bx, lam, w_out):
    p = h @ w_in
    c_gate, b_gate, v, u, g = jnp.split(
        p, [W_CONV, 2 * W_CONV, 3 * W_CONV, 3 * W_CONV + W_LRU], axis=-1)
    y_a = b_gate * causal_depthwise_conv_3(c_gate * v, conv_w)
    uc = causal_depthwise_conv_3(u, lru_conv_w) + lru_conv_b
    y_b = rg_lru(uc, wa, ba, wx, bx, lam) * jax.nn.gelu(g)
    return jnp.concatenate([y_a, y_b], axis=-1) @ w_out

def swiglu(x, wg, wu, wd):
    return (jax.nn.silu(x @ wg) * (x @ wu)) @ wd

def moe_swiglu(h, w_router, wg, wu, wd):
    bsz, s, d = h.shape
    xt = h.reshape(-1, d)
    logits = (xt @ w_router).astype(jnp.float32)
    top_v, top_i = lax.top_k(logits, TOP_K)
    gates = jax.nn.softmax(top_v, axis=-1)
    comb = jnp.sum(jax.nn.one_hot(top_i, N_EXPERTS, dtype=jnp.float32) * gates[..., None], axis=1)
    comb = comb.astype(h.dtype)
    y = jnp.zeros_like(xt)
    for e in range(N_EXPERTS):
        y = y + comb[:, e:e + 1] * swiglu(xt, wg[e], wu[e], wd[e])
    return y.reshape(bsz, s, d)

def third_inputs(seed: int = 0) -> dict:
    key = jax.random.key(seed)
    ks = jax.random.split(key, 24)
    f32 = jnp.float32
    nrm = lambda k, shape, fan_in: jax.random.normal(k, shape, f32) * (fan_in ** -0.5)
    u = jax.random.uniform(ks[11], (DEPTH, W_LRU), f32, minval=0.9, maxval=0.999)
    a0 = u ** (1.0 / RG_C)
    lam = jnp.log(a0) - jnp.log1p(-a0)
    return {
        "x": jax.random.normal(ks[0], (BATCH, SEQ, D_MODEL), f32),
        "norm_mix": 1.0 + 0.02 * jax.random.normal(ks[1], (DEPTH, D_MODEL), f32),
        "norm_ffn": 1.0 + 0.02 * jax.random.normal(ks[2], (DEPTH, D_MODEL), f32),
        "norm_final": 1.0 + 0.02 * jax.random.normal(ks[3], (D_MODEL,), f32),
        "w_in": nrm(ks[4], (DEPTH, D_MODEL, D_IN_TOT), D_MODEL),
        "conv_w": nrm(ks[5], (DEPTH, CONV_K_3, W_CONV), CONV_K_3),
        "lru_conv_w": nrm(ks[6], (DEPTH, LRU_CONV_K, W_LRU), LRU_CONV_K),
        "lru_conv_b": 0.02 * jax.random.normal(ks[7], (DEPTH, W_LRU), f32),
        "lru_wa": nrm(ks[8], (DEPTH, LRU_HEADS, LRU_HEAD_DIM, LRU_HEAD_DIM), LRU_HEAD_DIM),
        "lru_ba": 0.02 * jax.random.normal(ks[9], (DEPTH, W_LRU), f32),
        "lru_wx": nrm(ks[10], (DEPTH, LRU_HEADS, LRU_HEAD_DIM, LRU_HEAD_DIM), LRU_HEAD_DIM),
        "lru_bx": 0.02 * jax.random.normal(ks[12], (DEPTH, W_LRU), f32),
        "lru_lambda": lam,
        "w_out": nrm(ks[13], (DEPTH, D_MIX, D_MODEL), D_MIX),
        "ffn_w_gate": nrm(ks[14], (N_DENSE, D_MODEL, D_FF_3), D_MODEL),
        "ffn_w_up": nrm(ks[15], (N_DENSE, D_MODEL, D_FF_3), D_MODEL),
        "ffn_w_down": nrm(ks[16], (N_DENSE, D_FF_3, D_MODEL), D_FF_3),
        "w_router": nrm(ks[17], (N_MOE, D_MODEL, N_EXPERTS), D_MODEL),
        "moe_w_gate": nrm(ks[18], (N_MOE, N_EXPERTS, D_MODEL, D_FF_3), D_MODEL),
        "moe_w_up": nrm(ks[19], (N_MOE, N_EXPERTS, D_MODEL, D_FF_3), D_MODEL),
        "moe_w_down": nrm(ks[20], (N_MOE, N_EXPERTS, D_FF_3, D_MODEL), D_FF_3),
    }

def third_block(x, norm_mix, norm_ffn, norm_final, w_in, conv_w, lru_conv_w, lru_conv_b,
              lru_wa, lru_ba, lru_wx, lru_bx, lru_lambda, w_out,
              ffn_w_gate, ffn_w_up, ffn_w_down,
              w_router, moe_w_gate, moe_w_up, moe_w_down):
    for l in range(DEPTH):
        h = rms_norm_3(x, norm_mix[l])
        x = x + hybrid_mixer(h, w_in[l], conv_w[l], lru_conv_w[l], lru_conv_b[l],
                             lru_wa[l], lru_ba[l], lru_wx[l], lru_bx[l], lru_lambda[l], w_out[l])
        h = rms_norm_3(x, norm_ffn[l])
        j = l // 2
        if l % 2 == 0:
            x = x + swiglu(h, ffn_w_gate[j], ffn_w_up[j], ffn_w_down[j])
        else:
            x = x + moe_swiglu(h, w_router[j], moe_w_gate[j], moe_w_up[j], moe_w_down[j])
    return rms_norm_3(x, norm_final)


def setup_inputs(seed=0):
    out = dict(first_inputs(seed))
    for name, value in second_inputs(seed + 1).items():
        if name != "x":
            out[name + "_2"] = value
    for name, value in third_inputs(seed + 2).items():
        if name != "x":
            out[name + "_3"] = value
    return out


def reference(
    x, c, positions, ada_w, ada_b, norm1_g, w_in, lambda_q1, lambda_k1, lambda_q2, lambda_k2,
    subln_g, w_attn_o, dw_conv_w, dw_conv_b, conv_ln_g, conv_ln_b, w_conv_o, w_out, norm2_g,
    w_ffn_in, w_ffn_out, final_g, c_2, w_ada_2, b_ada_2, g_norm_2, w_in_2, w_pool_grp_2,
    pool_scale_2, w_pool_up_2, w_attn_up_2, w_out_2, g_final_2, norm_mix_3, norm_ffn_3,
    norm_final_3, w_in_3, conv_w_3, lru_conv_w_3, lru_conv_b_3, lru_wa_3, lru_ba_3, lru_wx_3,
    lru_bx_3, lru_lambda_3, w_out_3, ffn_w_gate_3, ffn_w_up_3, ffn_w_down_3, w_router_3,
    moe_w_gate_3, moe_w_up_3, moe_w_down_3,
):
    x = first_block(
        x, c, positions, ada_w, ada_b, norm1_g, w_in, lambda_q1, lambda_k1, lambda_q2,
        lambda_k2, subln_g, w_attn_o, dw_conv_w, dw_conv_b, conv_ln_g, conv_ln_b, w_conv_o,
        w_out, norm2_g, w_ffn_in, w_ffn_out, final_g,
    )
    x = second_block(
        x, c_2, w_ada_2, b_ada_2, g_norm_2, w_in_2, w_pool_grp_2, pool_scale_2, w_pool_up_2,
        w_attn_up_2, w_out_2, g_final_2,
    )
    return third_block(
        x, norm_mix_3, norm_ffn_3, norm_final_3, w_in_3, conv_w_3, lru_conv_w_3, lru_conv_b_3,
        lru_wa_3, lru_ba_3, lru_wx_3, lru_bx_3, lru_lambda_3, w_out_3, ffn_w_gate_3, ffn_w_up_3,
        ffn_w_down_3, w_router_3, moe_w_gate_3, moe_w_up_3, moe_w_down_3,
    )


_drawn_inputs = setup_inputs


def setup_inputs(seed=0):
    import zlib

    import numpy as np

    out = dict(_drawn_inputs(seed))
    spreads = {}
    factors = {'conv_ln_g': 3.943,
     'b_ada_2': 3.833,
     'norm_final_3': 8.089,
     'lru_ba_3': 18.063,
     'lru_bx_3': 3.463,
     'lambda_q2': 2.707,
     'subln_g': 5.196,
     'conv_ln_b': 6.854,
     'norm2_g': 2.85,
     'g_norm_2': 3.162,
     'pool_scale_2': 2.843}
    for name, (base, spread) in spreads.items():
        noise = np.random.default_rng([zlib.crc32(name.encode()), seed]).standard_normal(out[name].shape)
        drawn = base * np.exp(spread * noise) if base else spread * noise
        out[name] = __import__('jax').numpy.asarray(drawn.astype(out[name].dtype))
    for name, factor in factors.items():
        out[name] = (out[name] * factor).astype(out[name].dtype)
    return out
```

```python
import math
from contextlib import ExitStack

import concourse.bass as bass
from concourse import mybir

ALU = mybir.AluOpType
ACT = mybir.ActivationFunctionType
AX = mybir.AxisListType
F32 = mybir.dt.float32
F32R = mybir.dt.float32r
I32 = mybir.dt.int32

P = 128
D = 1024
KD = D // P
S = 256
T = S // P
W = 512
KW = W // P
NT = 512
RAW = 6
SPL = 3
AHEAD = 2
FB = 256
F1 = 2816
F3 = 3584
E = 8
CONV_K = 31
PI = math.pi


PARAM_ROWS = [
    ("norm1_g", 16), ("norm2_g", 16), ("g_norm_2", 8), ("norm_mix_3", 16), ("norm_ffn_3", 16),
    ("subln_g", 2), ("dw_conv_b", 8), ("conv_ln_g", 8), ("conv_ln_b", 8), ("pool_scale_2", 4),
    ("lru_conv_b_3", 8), ("lru_ba_3", 8), ("lru_bx_3", 8), ("lru_lambda_3", 8), ("c", 8), ("c_2", 8),
    ("conv_w_3", 24), ("lru_conv_w_3", 32), ("dw_conv_w", 248),
]


def param_columns():
    at, n, loads = {}, 0, []
    for name, rows in PARAM_ROWS:
        at[name] = n
        r = 0
        while r < rows:
            k = min(rows - r, P - n % P)
            loads.append((name, r, n, k))
            r += k
            n += k
    return at, loads, -(-n // P)


COL, PARAM_LOADS, PARAM_TILES = param_columns()


def shape_constants():
    import numpy as np
    ident = np.eye(P, dtype=np.float32)
    rot = np.zeros((P, P), np.float32)
    for b in (0, 64):
        for d in range(8):
            rot[b + d + 8, b + d] = -1.0
            rot[b + d, b + d + 8] = 1.0
    tri = np.where(np.arange(P)[:, None] >= np.arange(P)[None, :], 0.0, -3.0e38).astype(np.float32)
    before = (np.arange(P)[:, None] < np.arange(P)[None, :]).astype(np.float32)
    iota = np.broadcast_to(np.arange(P, dtype=np.float32), (P, P))
    freq = np.zeros((P, 2), np.float32)
    e = np.arange(0, 16, 2, dtype=np.float32) / np.float32(16)
    f1 = (np.float32(1.0) / np.power(np.float32(500000.0), e)).astype(np.float32)
    f2 = np.power(np.float32(500000.0), -e).astype(np.float32)
    for p in range(P):
        if p % 64 < 16:
            freq[p, 0], freq[p, 1] = f1[p % 8], f2[p % 8]
    misc = np.zeros((P, P), np.float32)
    misc[:, 0:2] = freq
    square = np.stack([ident, rot, tri, before, iota, misc], 1).reshape(P, 6 * P)
    t = np.arange(S, dtype=np.float32)
    row = [1.0 / np.minimum(t + 1, w) for w in (2, 4, 8, 16)] + [t]
    return np.ascontiguousarray(square), np.ascontiguousarray(np.stack(row).astype(np.float32))


class Plan:

    def __init__(self):
        self.chunks = []
        self.jobs = {}
        self.order = []
        self.count = {"act": 0, "dve": 0}
        self.splits = {}

    def job(self, name, evac, sources=()):
        self.count[evac] += 1
        n = len(self.order)
        self.jobs[name] = (n, len(self.chunks), len(sources), evac, self.count[evac])
        self.order.append(name)
        self.chunks += sources

    def split(self, name):
        self.splits[name] = len(self.splits) + 1

    def before(self, name):
        n = self.jobs[name][0]
        return self.jobs[self.order[n - 3]][3:5] if n >= 3 else None


def tiles(w):
    return w.rearrange("(c p) n -> p c n", p=P)


def halves(src, width):
    rows = src.shape[1]
    h = rows // 2
    return [(slice(0, h * width), src[:, 0:h, :]), (slice(h * width, 2 * h * width), src[:, h:rows, :])]


def column_chunks(w, n0, rows=KD, r0=0):
    t = tiles(w)
    return [halves(t[:, k:k + 4, n0:n0 + NT], NT) for k in range(r0, r0 + rows, 4)]


def build(nc, a, out):
    plan = Plan()
    at3 = {}
    counts_at = {}
    n_norm = [0]

    def plan_norm():
        n = n_norm[0]
        n_norm[0] += 1
        plan.job(f"norm{n}.0", "dve")
        plan.job(f"norm{n}.1", "dve")
        plan.split(f"norm{n}.0")
        plan.split(f"norm{n}.1")

    def plan_linear(name, w, cols, evac, n0=0, rows=KD):
        for j in range(cols // NT):
            plan.job(f"{name}.{j}", evac, column_chunks(w, n0 + j * NT, rows))

    def plan_mod(k, w, slices):
        for j in range(slices):
            plan.job(f"mod{k}.{j}", "act", column_chunks(w, j * D) + column_chunks(w, j * D + NT))
            if j in (2, 5):
                plan.job(f"gate{k}.{j}", "dve")

    def plan_attention(k):
        for part in ("rotq", "rotk"):
            plan.job(f"{part}{k}", "dve")
        for q in ("score0", "score1a", "score1b"):
            plan.job(f"{q}.{k}", "act")
        maps = 4 if k < 2 else 8
        for j in range(3 * maps // 8 if k == 2 else 2):
            plan.job(f"turn{k}.{j}", "act")
        plan.job(f"pv{k}", "act")

    def ffn_sources(gate, up, down, steps):
        def gu(s, k):
            return [(slice(0, 1024), tiles(gate)[:, k:k + 4, s * FB:(s + 1) * FB]),
                    (slice(1024, 2048), tiles(up)[:, k:k + 4, s * FB:(s + 1) * FB])]

        def dn(s):
            return halves(tiles(down)[:, 2 * s:2 * s + 2, :], D)
        res = [gu(0, 0), gu(0, 4)]
        for s in range(steps - 1):
            res += [gu(s + 1, 0), gu(s + 1, 4), dn(s)]
        return res + [dn(steps - 1)]

    def plan_ffn(k, gate, up, down, steps):
        at3[k] = len(plan.chunks)
        counts_at[k] = dict(plan.count)
        plan.chunks += ffn_sources(gate, up, down, steps)

    for l in range(2):
        plan_mod(l, a["ada_w"][l], 6)
        plan_norm()
        w = a["w_in"][l]
        plan_linear(f"ga{l}", w, 512, "act", 1536)
        plan_linear(f"gb{l}", w, 512, "act", 2048)
        plan_linear(f"q{l}", w, 512, "act", 0)
        plan_linear(f"k{l}", w, 512, "act", 512)
        plan_linear(f"v{l}", w, 512, "act", 1024)
        plan_linear(f"gates{l}", w, 2048, "act", 2560)
        plan_attention(l)
        plan.job(f"subln{l}", "dve")
        plan.split(f"attn{l}")
        plan_linear(f"yattn{l}", a["w_attn_o"][l], 1024, "dve", rows=KW)
        plan.job(f"lnmean{l}", "dve")
        plan.job(f"lnvar{l}", "dve")
        plan.split(f"conv{l}")
        plan_linear(f"yconv{l}", a["w_conv_o"][l], 1024, "dve", rows=KW)
        plan.job(f"mix{l}.0", "act")
        plan.job(f"mix{l}.1", "act")
        plan.split(f"mix{l}.0")
        plan.split(f"mix{l}.1")
        plan_linear(f"wout{l}", a["w_out"][l], 1024, "dve")
        plan_norm()
        wf = a["w_ffn_in"][l]
        plan_ffn(l, wf[:, 0:F1], wf[:, F1:2 * F1], a["w_ffn_out"][l], F1 // FB)
    plan_mod(2, a["w_ada_2"][0], 3)
    plan_norm()
    w = a["w_in_2"][0]
    plan_linear("up", w, 512, "act", 0)
    plan_linear("zp", w, 512, "act", 512)
    plan_linear("q2", w, 512, "act", 1024)
    plan_linear("k2", w, 512, "act", 1536)
    plan_linear("v2", w, 512, "act", 2048)
    plan_linear("gates2", w, 2048, "act", 3072)
    plan_linear("za", w, 512, "act", 2560)
    plan.job("pool", "dve")
    plan.split("conv2")
    plan_linear("yconv2", a["w_pool_up_2"][0], 1024, "dve", rows=KW)
    plan_attention(2)
    plan.split("attn2")
    plan_linear("yattn2", a["w_attn_up_2"][0], 1024, "dve", rows=KW)
    plan.job("mix2.0", "act")
    plan.job("mix2.1", "act")
    plan.split("mix2.0")
    plan.split("mix2.1")
    plan_linear("wout2", a["w_out_2"][0], 1024, "dve")
    for l in range(2):
        plan_norm()
        w = a["w_in_3"][l]
        for j, name in enumerate(("cg", "bg", "vv", "uu", "gg")):
            plan_linear(f"{name}{l}", w, 512, "dve" if name == "vv" else "act", j * 512)
        plan.job(f"lrur{l}", "act")
        plan.job(f"lrui{l}", "act")
        plan.split(f"lru{l}.0")
        plan.split(f"lru{l}.1")
        plan_linear(f"wout{3 + l}", a["w_out_3"][l], 1024, "dve")
        plan_norm()
        if l == 0:
            plan_ffn(2, a["ffn_w_gate_3"][0], a["ffn_w_up_3"][0], a["ffn_w_down_3"][0], F3 // FB)
    MOE0 = len(plan.chunks)
    STEPS3 = F3 // FB
    PER = 3 * STEPS3
    assert PER % RAW == 0 and PER % SPL == 0

    ctx = ExitStack()
    with ctx:
        def sb(name, shape, dt=F32):
            return ctx.enter_context(nc.sbuf_tensor(name, shape, dt))

        sems = {}

        def sem(name):
            if name not in sems:
                sems[name] = ctx.enter_context(nc.semaphore(name))
            return sems[name]

        raw = sb("raw", [P, RAW, 2048])
        head = sb("head", [P, SPL, 2048], F32R)
        rest = sb("rest", [P, SPL, 2048], F32R)
        x = sb("x", [P, T, D])
        xn = sb("xn", [P, T, D])
        hT = sb("hT", [P, KD, S])
        hTh = sb("hTh", [P, KD, S], F32R)
        hTl = sb("hTl", [P, KD, S], F32R)
        cst = sb("cst", [P, 6, P])
        ident, rot, tri, before, iota = (cst[:, i, :] for i in range(5))
        freq = cst[:, 5, 0:2]
        ones = sb("ones", [P, P])
        prm = sb("prm", [P, PARAM_TILES * P])
        trig = sb("trig", [P, 2, S])
        gbc = sb("gbc", [P, 2, D])
        aTh = sb("aTh", [P, 2, S], F32R)
        aTl = sb("aTl", [P, 2, S], F32R)
        qkv = sb("qkv", [P, 3, 1024])
        gat = sb("gat", [P, T, 2048])
        upad = sb("upad", [P, KW, 30 + S])
        aw = sb("aw", [P, 3072])
        oT = sb("oT", [P, KW, S])
        sm = sb("sm", [P, 288])
        cHL = sb("cHL", [P, 2 * KD + 64], F32R)
        pair = [ctx.enter_context(nc.psum_tensor(f"pair{i}", [P, 2, 512], F32)) for i in range(3)]
        tb = [ctx.enter_context(nc.psum_tensor(f"tb{i}", [P, 512], F32)) for i in range(2)]

        qT = qkv[:, 0, :].rearrange("p (g s) -> p g s", s=S)
        kT = qkv[:, 1, :].rearrange("p (g s) -> p g s", s=S)
        vt = qkv[:, 2, :].rearrange("p (t n) -> p t n", t=T)
        conv = aw[:, 2048:3072].rearrange("p (g s) -> p g s", s=S)
        modrow = gat[0:3, 1, 0:1024]
        gateA, gateB = gat[:, :, 0:D], gat[:, :, D:2 * D]
        sg = qkv[:, 0, 0:512].rearrange("p (t f) -> p t f", t=T)
        act_ = qkv[:, 1, 0:512].rearrange("p (t f) -> p t f", t=T)
        ss, rstd = sm[:, 0:2], sm[:, 2:4]
        gs, sh = sm[:, 8:24], sm[:, 24:40]
        lamc = sm[:, 40:44]
        mx, su = sm[:, 228:244], sm[:, 244:260]
        rs = sm[:, 260:276]
        cact = sm[:, 72:80]
        sub = sm[:, 80:81]
        sp8 = sm[:, 276:284]
        tmp8 = sm[:, 88:120]
        lam4 = sm[0:1, 120:124]
        pos = sm[:, 128:144].rearrange("p (t e) -> p t e", t=T)
        comb = sm[:, 144:160].rearrange("p (t e) -> p t e", t=T)
        sel = sm[:, 160:176].rearrange("p (t e) -> p t e", t=T)
        lg = sm[:, 176:192].rearrange("p (t e) -> p t e", t=T)
        w8 = sm[:, 192:208].rearrange("p (t e) -> p t e", t=T)
        o8 = sm[:, 208:224].rearrange("p (t e) -> p t e", t=T)
        m2 = sm[:, 224:226]
        m1 = sm[:, 226:228]
        wins = sb("wins", [1, 1], I32)
        posi = aw[:, 0:S].bitcast(I32)


        class Ops:

            def __init__(self, eng, name):
                self.eng, self.sem, self.n = eng, sem(name), 0

            def did(self, ins):
                self.n += 1
                ins.then_inc(self.sem, 1)

            def now(self):
                self.eng.wait_ge(self.sem, self.n)

        class At:

            def __init__(self, k, turn=0, per=0):
                self.k, self.turn, self.per = k, turn, per
                self.raw, self.split = k % RAW, k % SPL

            def next(self, d=1):
                return At(self.k + d, self.turn, self.per)

            def count(self, d=0):
                return self.turn * self.per + (self.k + 1 + d)

            def landed(self):
                return self.turn * (32 * self.per // RAW) + 32 * (self.k // RAW + 1)

        def wait(eng, s, value):
            if not (isinstance(value, int) and value <= 0):
                eng.wait_ge(s, value)

        landed = [sem(f"chunk_landed{i}") for i in range(RAW)]
        heads_done, rests_done, chunk_used = sem("heads_done"), sem("rests_done"), sem("chunk_used")
        job_done, evac = sem("job_done"), {"act": sem("evac_act"), "dve": sem("evac_dve")}
        hth_ready, htl_ready = sem("hth_ready"), sem("htl_ready")
        act_ready, turned = sem("act_ready"), sem("act_turned")
        ath_ready, atl_ready = sem("ath_ready"), sem("atl_ready")

        def pcol(name, i=0, n=1):
            return prm[:, COL[name] + i:COL[name] + i + n]

        def col8(name, l):
            return pcol(name, 8 * l, 8)

        def jobs_done(name):
            n = plan.jobs[name][0]
            return sum(1 for m in plan.order[:n + 1] if not plan.jobs[m][2])

        def last_chunk(name):
            return plan.jobs[name][1] + plan.jobs[name][2] - 1

        def bank(name):
            return pair[plan.jobs[name][0] % 3]

        def flat4(t):
            return t[:, :, :].rearrange("p b (h s) -> p (b h) s", s=S)

        def over(ap, shape, axis):
            return ap.unsqueeze(axis).to_broadcast(shape)

        DENSE = [(0, F1 // FB), (1, F1 // FB), (2, F3 // FB)]
        STEP0 = {0: 0, 1: F1 // FB, 2: 2 * (F1 // FB), 3: 2 * (F1 // FB) + F3 // FB}
        POOLBUF = (oT, aw[:, 0:1024].rearrange("p (g s) -> p g s", s=S))
        dpool = aw[:, 1024:2048].rearrange("p (g s) -> p g s", s=S)
        invcnt = aw[:, 2048:3072].rearrange("p (g s) -> p g s", s=S)
        wgrp = gbc[:, 1, 0:512].rearrange("p (g s) -> p g s", s=P)
        wbd = gbc[:, 0, :].rearrange("p (a g n) -> p a g n", a=2, g=KW)
        wrt = oT[:, 0, 0:64].rearrange("p (k e) -> p k e", e=E)
        sc0 = hT[:, 0:4, :].rearrange("p k s -> p (k s)").rearrange("p (m s) -> p m s", s=P)
        sc1 = xn[:, :, :].rearrange("p t n -> p (t n)").rearrange("p (m s) -> p m s", s=S)
        aT = aw[:, :].rearrange("p (c n) -> p c n", n=512)
        G = gat[:, :, :].rearrange("p t n -> p (t n)")
        upu = G[:, 0:KW * (3 + S)].rearrange("p (g s) -> p g s", s=3 + S)
        lru_a = G[:, 1036:2060].rearrange("p (g s) -> p g s", s=S)
        aw4 = [aw[:, i * 1024:(i + 1) * 1024].rearrange("p (g s) -> p g s", s=S) for i in range(3)]
        kq = [qkv[:, i, :].rearrange("p (g s) -> p g s", s=S) for i in range(3)]
        praw = aw[:, 1024:1024 + PARAM_TILES * P].rearrange("p (c n) -> p c n", n=P)
        lamrow = xn[0:1, 0, 0:512].rearrange("p (a l n) -> p a l n", a=4, l=2)
        angle = aw[:, S:2 * S]
        ptok = aw[:, 0:256].rearrange("p (t n) -> p t n", t=T)
        pcomb = aw[:, 256:512].rearrange("p (t n) -> p t n", t=T)
        pslot = aw[:, 512:768]
        ysb = aw[:, 1024:2048]
        xe = G[:, 0:1024].rearrange("p (k s) -> p k s", s=P)
        PADS = 30
        lam_init = [0.8 - 0.6 * math.exp(-0.3 * l) for l in range(2)]
        mods = [(0, 6, 0), (1, 6, 6), (2, 3, 12)]

        block = ctx.enter_context(nc.Block())

        @block.sync
        def _(sp):
            sp.dma_start(cst[:, :, :], a["square"].rearrange("p (c n) -> p c n", n=P)).then_inc(sem("const_landed"), 16)
            sp.dma_start(x[:, :, :], a["x"][0].rearrange("(t p) n -> p t n", p=P)).then_inc(sem("x_landed"), 16)

            def load(c, parts):
                wait(sp, rests_done, c.count(-RAW))
                for part, src in parts:
                    dst = raw[:, c.raw, part]
                    if len(src.shape) == 3:
                        dst = dst.rearrange("p (k n) -> p k n", n=src.shape[2])
                    sp.dma_start(dst, src).then_inc(landed[c.raw], 16)

            def load_ffn_loop(k, gate, up, down, steps):
                g, u, d = tiles(gate), tiles(up), tiles(down)
                c0 = at3[k] + 5
                with sp.Fori(0, (steps - 2) // 2) as i:
                    for j in range(2):
                        s = 1 + j
                        cols = bass.ds(i * (2 * FB) + (s + 1) * FB, FB)
                        for r in range(2):
                            load(At(c0 + 3 * j + r, i, RAW), [(slice(0, 1024), g[:, 4 * r:4 * r + 4, cols]),
                                                             (slice(1024, 2048), u[:, 4 * r:4 * r + 4, cols])])
                        load(At(c0 + 3 * j + 2, i, RAW),
                             [(slice(0, D), d[:, bass.ds(i * 4 + 2 * s, 1), :]),
                              (slice(D, 2 * D), d[:, bass.ds(i * 4 + 2 * s + 1, 1), :])])
                return c0 + RAW * ((steps - 2) // 2)

            loops = {
                at3[0] + 5: (0, a["w_ffn_in"][0][:, 0:F1], a["w_ffn_in"][0][:, F1:2 * F1], a["w_ffn_out"][0], F1 // FB),
                at3[1] + 5: (1, a["w_ffn_in"][1][:, 0:F1], a["w_ffn_in"][1][:, F1:2 * F1], a["w_ffn_out"][1], F1 // FB),
                at3[2] + 5: (2, a["ffn_w_gate_3"][0], a["ffn_w_up_3"][0], a["ffn_w_down_3"][0], F3 // FB)}
            c = 0
            while c < MOE0:
                if c in loops:
                    c = load_ffn_loop(*loops[c])
                else:
                    load(At(c), plan.chunks[c])
                    c += 1
            eg = a["moe_w_gate_3"][0].rearrange("e (c p) n -> p (e c) n", p=P)
            eu = a["moe_w_up_3"][0].rearrange("e (c p) n -> p (e c) n", p=P)
            ed = a["moe_w_down_3"][0].rearrange("e (c p) n -> p (e c) n", p=P)
            KF = F3 // P

            def load_expert(it, e):
                def gu(k, s, r):
                    cols = slice(s * FB, (s + 1) * FB)
                    load(At(MOE0 + k, it, PER), [(slice(0, 1024), eg[:, bass.ds(e * KD + 4 * r, 4), cols]),
                                                 (slice(1024, 2048), eu[:, bass.ds(e * KD + 4 * r, 4), cols])])

                def dn(k, s):
                    load(At(MOE0 + k, it, PER), [(slice(0, D), ed[:, bass.ds(e * KF + 2 * s, 1), :]),
                                                 (slice(D, 2 * D), ed[:, bass.ds(e * KF + 2 * s + 1, 1), :])])
                gu(0, 0, 0)
                gu(1, 0, 1)
                for s in range(STEPS3 - 1):
                    gu(2 + 3 * s, s + 1, 0)
                    gu(3 + 3 * s, s + 1, 1)
                    dn(4 + 3 * s, s)
                dn(PER - 1, STEPS3 - 1)

            with sp.Fori(0, E) as e:
                load_expert(e, e)
            sp.wait_ge(sem("windows_ready"), 1)
            more = sp.value_load(wins[0:1, 0:1], min_val=0, max_val=1)
            with sp.If(more):
                with sp.Fori(0, E) as e:
                    load_expert(e + E, e)
            for k in range(2):
                sp.wait_ge(rests_done, more * (E * PER) + (MOE0 + E * PER + k + 1 - RAW))
                for j in range(2):
                    sp.dma_start(raw[:, (MOE0 + k) % RAW, 8 * j:8 * j + 8], a["square"][:, 8 * j:8 * j + 8]).then_inc(landed[(MOE0 + k) % RAW], 16)

        @block.gpsimd
        def _(pool):
            own = Ops(pool, "pool_own")
            own.did(pool.memset(praw, 0.0))
            pool.memset(ones[:, :], 1.0).then_inc(sem("ones_ready"), 1)
            own.did(pool.memset(upad[:, :, :], 0.0))
            own.now()
            for name, r, n, k in PARAM_LOADS:
                pool.dma_start(praw[n % P:n % P + k, n // P, :], a["p_" + name][r:r + k, :]).then_inc(sem("params_landed"), 16)
            for i, name in enumerate(("lambda_q1", "lambda_k1", "lambda_q2", "lambda_k2")):
                pool.dma_start(lamrow[:, i, :, 0:64], a[name].unsqueeze(0)).then_inc(sem("lambdas_landed"), 16)
            pool.dma_start(posi, a["positions"][0:1, :].to_broadcast([P, S])).then_inc(sem("positions_landed"), 16)

            def bias_rows(k, slices, before_):
                src = a["ada_b"][k:k + 1, :] if k < 2 else a["b_ada_2"][0:1, :]
                for j in range(slices):
                    wait(pool, sem("modrow_used"), before_ + j)
                    pool.dma_start(modrow[2:3, :], src[:, j * D:(j + 1) * D]).then_inc(sem("bias_row"), 16)

            bias_rows(*mods[0])
            pool.wait_ge(evac["dve"], plan.jobs["norm1.1"][4])
            bias_rows(*mods[1])
            pool.wait_ge(evac["dve"], plan.jobs["norm3.1"][4])
            pool.dma_start(gbc[:, 0, :], a["final_g"].unsqueeze(0).to_broadcast([P, D])).then_inc(sem("final_g_landed"), 16)
            pool.wait_ge(sem("block_done"), 1)
            pool.dma_start(invcnt, a["rows"][0:4, :].unsqueeze(0).to_broadcast([P, 4, S])).then_inc(sem("pool_landed"), 16)
            pool.dma_start(angle, a["rows"][4:5, :].to_broadcast([P, S])).then_inc(sem("pool_landed"), 16)
            pool.dma_start(wgrp, a["w_pool_grp_2"][0].rearrange("g c d -> c g d")).then_inc(sem("pool_landed"), 16)
            bias_rows(*mods[2])
            pool.wait_ge(job_done, jobs_done("pool"))
            pool.dma_start(gbc[:, 1, :], a["g_final_2"].unsqueeze(0).to_broadcast([P, D])).then_inc(sem("final_g_landed"), 16)
            pool.wait_ge(sem("block_done"), 2)
            pool.dma_start(gbc[:, 1, :], a["norm_final_3"].unsqueeze(0).to_broadcast([P, D])).then_inc(sem("final_g_landed"), 16)
            own.did(pool.memset(gbc[:, 0, :], 0.0))
            own.now()
            for l in range(2):
                if l == 1:
                    pool.wait_ge(job_done, jobs_done("lrui0"))
                for i, name in enumerate(("lru_wa_3", "lru_wx_3")):
                    src = a[name][l].rearrange("(g h) i j -> h i g j", h=2)
                    for h in range(2):
                        pool.dma_start(wbd[64 * h:64 * h + 64, i, :, 64 * h:64 * h + 64], src[h]).then_inc(sem("lru_landed"), 16)
            pool.wait_ge(evac["dve"], plan.jobs["norm8.1"][4])
            pool.dma_start(wrt, a["w_router_3"][0].rearrange("(k p) e -> p k e", p=P)).then_inc(sem("router_landed"), 16)
            pool.wait_ge(sem("block_done"), 3)
            pool.dma_start(out[0].rearrange("(t p) n -> p t n", p=P), xn[:, :, :]).then_inc(sem("out_stored"), 16)
            pool.wait_ge(sem("out_stored"), 16)

        @block.scalar
        def _(act):
            own = Ops(act, "act_own")
            fed = [0]

            def make_head(c):
                act.wait_ge(landed[c.raw], c.landed())
                wait(act, chunk_used, c.count(-SPL))
                act.activation(head[:, c.split, :], raw[:, c.raw, :], ACT.Copy).then_inc(heads_done, 1)

            def feed(upto):
                while fed[0] < min(upto, MOE0 + 2):
                    make_head(At(fed[0]))
                    fed[0] += 1

            def job(name):
                feed(last_chunk(name) + 1 + AHEAD)
                act.wait_ge(chunk_used, last_chunk(name) + 1)
                return bank(name)

            def split(name, lo, hi, ready=None):
                act.wait_ge(sem("hT_ready"), plan.splits[name])
                act.activation(hTh[:, lo:hi, :], hT[:, lo:hi, :], ACT.Copy).then_inc(hth_ready, 1)

            def sqrt_rows(n):
                act.wait_ge(sem("mean_square"), n)
                act.activation(rstd, ss, ACT.Sqrt).then_inc(sem("root"), 1)

            def norm(n):
                for j in range(2):
                    split(f"norm{n}.{j}", 4 * j, 4 * j + 4)

            def sines(k):
                act.wait_ge(sem("angles_ready"), k + 1)
                act.activation(trig[:, 1, :], aw[:, 2 * S:3 * S], ACT.Sin)
                act.activation(trig[:, 0, :], aw[:, 3 * S:4 * S], ACT.Sin).then_inc(sem("trig_ready"), 1)

            def mod(k, slices, before_):
                act.wait_ge(sem("cond_ready"), k // 2 + 1)
                if k != 1:
                    if k == 0:
                        own.did(act.activation(cact, pcol("c", 0, 8), ACT.Silu))
                        own.now()
                    act.activation(cHL[:, 0:2 * KD:2], cact if k == 0 else pcol("c_2", 0, 8), ACT.Copy).then_inc(sem("cond_head"), 1)
                for j in range(slices):
                    ps = job(f"mod{k}.{j}")
                    wait(act, sem("modrow_used"), before_ + j)
                    act.activation(modrow[0:2, :].rearrange("p (b n) -> p b n", b=2), ps[0:2, :, :], ACT.Copy).then_inc(evac["act"], 1)

            def copy_job(name, dst, func=ACT.Copy, turn=True, scale=1.0):
                ps = job(name)
                act.activation(dst, flat4(ps) if turn else ps[:, :, :], func, scale=scale).then_inc(evac["act"], 1)

            def attention(k):
                act.wait_ge(job_done, jobs_done(f"score0.{k}"))
                act.activation(sc0, bank(f"score0.{k}")[:, :, :].rearrange("p r (g n) -> p (r g) n", n=P), ACT.Copy,
                               scale=0.125).then_inc(evac["act"], 1)
                for h, part in enumerate("ab"):
                    name = f"score1{part}.{k}"
                    act.wait_ge(job_done, jobs_done(name))
                    dst = sc1.rearrange("p (r g) s -> p r g s", r=2)[:, :, 2 * h:2 * h + 2, :]
                    act.activation(dst, bank(name)[:, :, :].rearrange("p r (g s) -> p r g s", s=S), ACT.Copy,
                                   scale=0.125).then_inc(evac["act"], 1)
                for q, sc in enumerate((sc0, sc1)):
                    act.wait_ge(sem("max_ready"), 2 * k + q + 1)
                    for m in range(8):
                        ins = act.activation(sc[:, m, :], sc[:, m, :], ACT.Exp, bias=mx[:, 8 * q + m:8 * q + m + 1],
                                             accum_out=su[:, 8 * q + m:8 * q + m + 1])
                    ins.then_inc(sem("exp_ready"), 1)
                for j in range(2 if k < 2 else 3):
                    act.wait_ge(job_done, jobs_done(f"turn{k}.{j}"))
                    n = 1 if k < 2 and j == 1 else 2
                    act.activation(aT[:, 2 * j:2 * j + n, :], bank(f"turn{k}.{j}")[:, 0:n, :], ACT.Copy).then_inc(evac["act"], 1)
                act.wait_ge(job_done, jobs_done(f"pv{k}"))
                act.activation(oT[:, :, :], flat4(bank(f"pv{k}")), ACT.Copy).then_inc(evac["act"], 1)

            def mix(k):
                for j in range(2):
                    act.wait_ge(job_done, jobs_done(f"mix{k}.{j}"))
                    act.activation(hT[:, 4 * j:4 * j + 4, :], flat4(bank(f"mix{k}.{j}")), ACT.Copy).then_inc(evac["act"], 1)
                    act.wait_ge(evac["act"], plan.jobs[f"mix{k}.{j}"][4])
                    act.activation(hTh[:, 4 * j:4 * j + 4, :], hT[:, 4 * j:4 * j + 4, :], ACT.Copy).then_inc(hth_ready, 1)

            def silu_gate(c, s, nt, b=0):
                act.wait_ge(chunk_used, c.count())
                src = pair[0][:, 0:T, 0:FB] if nt == T else pair[0][:, b:b + 1, 0:FB]
                act.activation(sg[:, 0:nt, :], src, ACT.Silu).then_inc(sem("silu_ready"), 1)

            def turned_head(s, nt):
                act.wait_ge(turned, s + 1)
                act.activation(aTh[:, :, 0:nt * P], tb[0][:, :].rearrange("p (k s) -> p k s", k=2)[:, :, 0:nt * P],
                               ACT.Copy).then_inc(ath_ready, 1)

            def ffn_step(c, s, nt, b=0):
                make_head(c.next(2))
                turned_head(s, nt)
                make_head(c.next(3))
                make_head(c.next(4))
                silu_gate(c.next(1), s + 1, nt, b)

            def ffn(k, steps):
                c0, s0 = at3[k], STEP0[k]
                feed(c0 + 2 + AHEAD)
                silu_gate(At(c0 + 1), s0, T)
                ffn_step(At(c0 + 2), s0, T)
                with act.Fori(0, (steps - 2) // 2) as i:
                    for j in range(2):
                        ffn_step(At(c0 + 5 + 3 * j, i, RAW), i * 2 + (s0 + 1 + j), T)
                done = 1 + 2 * ((steps - 2) // 2)
                for s in range(done, steps - 1):
                    ffn_step(At(c0 + 2 + 3 * s), s0 + s, T)
                fed[0] = c0 + 2 + 3 * (steps - 1) + AHEAD
                turned_head(s0 + steps - 1, T)

            act.wait_ge(sem("lam_dots"), 1)
            act.activation(lam4, lam4, ACT.Exp).then_inc(sem("lam_exp"), 1)
            act.wait_ge(sem("params_ready"), 1)
            act.wait_ge(sem("lru_decay_in"), 1)
            act.activation(tmp8[:, 8:16], tmp8[:, 0:8], ACT.Exp, scale=-1.0).then_inc(sem("lru_decay_exp"), 1)
            sines(0)
            nn = 0
            for l in range(2):
                mod(*mods[l])
                sqrt_rows(nn + 1)
                norm(nn)
                nn += 1
                copy_job(f"ga{l}.0", upad[:, :, PADS:PADS + S])
                copy_job(f"gb{l}.0", oT[:, :, :], ACT.Sigmoid)
                copy_job(f"q{l}.0", qT)
                copy_job(f"k{l}.0", kT)
                copy_job(f"v{l}.0", vt, turn=False)
                for j in range(4):
                    copy_job(f"gates{l}.{j}", gat[:, :, j * NT:(j + 1) * NT], ACT.Sigmoid, turn=False)
                attention(l)
                act.wait_ge(sem("sub_var"), l + 1)
                act.activation(kq[1], kq[1], ACT.Sqrt).then_inc(sem("sub_root"), 1)
                split(f"attn{l}", 0, 4)
                feed(last_chunk(f"yattn{l}.0") + 1 + AHEAD)
                feed(last_chunk(f"yattn{l}.1") + 1 + AHEAD)
                act.wait_ge(sem("ln_var"), l + 1)
                act.activation(kq[1][:, 0, :], kq[1][:, 0, :], ACT.Sqrt).then_inc(sem("ln_root"), 1)
                act.wait_ge(sem("ln_ready"), l + 1)
                for g in range(KW):
                    own.did(act.activation(hT[:, 4 + g, :], conv[:, g, :], ACT.Silu,
                                           scale=pcol("conv_ln_g", 4 * l + g), bias=pcol("conv_ln_b", 4 * l + g)))
                own.now()
                act.activation(hTh[:, 4:8, :], hT[:, 4:8, :], ACT.Copy).then_inc(hth_ready, 1)
                feed(last_chunk(f"yconv{l}.1") + 1 + AHEAD)
                mix(l)
                feed(last_chunk(f"wout{l}.0") + 1 + AHEAD)
                feed(last_chunk(f"wout{l}.1") + 1 + AHEAD)
                sqrt_rows(nn + 1)
                norm(nn)
                nn += 1
                ffn(*DENSE[l])
            roots = nn + 1
            sqrt_rows(roots)
            sines(1)
            mod(*mods[2])
            roots += 1
            sqrt_rows(roots)
            norm(nn)
            nn += 1
            copy_job("up.0", upad[:, :, PADS:PADS + S])
            copy_job("zp.0", xn[:, 0, :].rearrange("p (g s) -> p g s", s=S), ACT.Silu)
            copy_job("q2.0", qT)
            copy_job("k2.0", kT)
            copy_job("v2.0", vt, turn=False)
            for j in range(4):
                copy_job(f"gates2.{j}", gat[:, :, j * NT:(j + 1) * NT], ACT.Sigmoid, turn=False)
            act.wait_ge(sem("pool_ready"), 1)
            copy_job("za.0", upad[:, :, PADS:PADS + S], ACT.Silu)
            split("conv2", 4, 8)
            feed(last_chunk("yconv2.1") + 1 + AHEAD)
            attention(2)
            split("attn2", 0, 4)
            feed(last_chunk("yattn2.1") + 1 + AHEAD)
            mix(2)
            feed(last_chunk("wout2.1") + 1 + AHEAD)
            roots += 1
            sqrt_rows(roots)
            for l in range(2):
                roots += 1
                sqrt_rows(roots)
                norm(nn)
                nn += 1
                copy_job(f"cg{l}.0", kq[0])
                copy_job(f"bg{l}.0", kq[1])
                feed(last_chunk(f"vv{l}.0") + 1 + AHEAD)
                act.wait_ge(sem("upu_zero"), 1)
                copy_job(f"uu{l}.0", upu[:, :, 3:3 + S])
                copy_job(f"gg{l}.0", kq[2], ACT.Gelu_apprx_tanh)
                for i, (name, bias) in enumerate((("lrur", "lru_ba_3"), ("lrui", "lru_bx_3"))):
                    act.wait_ge(job_done, jobs_done(f"{name}{l}"))
                    for g in range(KW):
                        ins = act.activation(aw4[i][:, g, :], flat4(bank(f"{name}{l}"))[:, g, :], ACT.Sigmoid,
                                             bias=pcol(bias, 4 * l + g))
                    ins.then_inc(evac["act"], 1)
                act.wait_ge(sem("log_a"), l + 1)
                act.activation(aw4[2], aw4[0], ACT.Tanh)
                act.activation(lru_a, aw4[0], ACT.Exp).then_inc(sem("lru_exp"), 1)
                act.wait_ge(sem("b_square"), l + 1)
                act.activation(aw4[2], aw4[0], ACT.Sqrt).then_inc(sem("b_root"), 1)
                split(f"lru{l}.0", 0, 4)
                split(f"lru{l}.1", 4, 8)
                feed(last_chunk(f"wout{3 + l}.1") + 1 + AHEAD)
                roots += 1
                sqrt_rows(roots)
                norm(nn)
                nn += 1
                if l == 0:
                    ffn(*DENSE[2])
            act.wait_ge(sem("gap_ready"), 1)
            act.activation(m2, m2, ACT.Exp).then_inc(sem("gap_exp"), 1)
            feed(MOE0 + 2)

            def expert(it):
                s0 = it * STEPS3 + STEP0[3]
                act.wait_ge(sem("combine_turned"), it + 1)
                act.activation(pslot, tb[1][:, 0:256], ACT.Copy).then_inc(sem("combine_ready"), 1)
                act.wait_ge(sem("gathered"), it + 1)
                act.activation(hTh[:, :, 0:P], xe, ACT.Copy).then_inc(sem("xe_head"), 1)
                at = At(MOE0, it, PER)
                make_head(at.next(2))
                make_head(at.next(3))
                silu_gate(at.next(1), s0, 1, 0)
                for s in range(STEPS3 - 1):
                    ffn_step(at.next(2 + 3 * s), s0 + s, 1, (s + 1) % 2)
                turned_head(s0 + (STEPS3 - 1), 1)
                make_head(at.next(PER + 1))
                act.wait_ge(chunk_used, at.next(PER - 1).count())
                act.activation(ysb.rearrange("p (b n) -> p b n", b=2), pair[1][:, :, :], ACT.Copy).then_inc(sem("y_ready"), 1)

            with act.Fori(0, E) as e:
                expert(e)
            act.wait_ge(sem("windows_ready"), 1)
            more = act.value_load(wins[0:1, 0:1], min_val=0, max_val=1)
            with act.If(more):
                with act.Fori(0, E) as e:
                    expert(e + E)
            act.wait_ge(sem("last_mean_square"), 1)
            act.activation(rstd, ss, ACT.Sqrt).then_inc(sem("last_root"), 1)

        @block.vector
        def _(dve):
            own = Ops(dve, "dve_own")
            did, now = own.did, own.now
            fed = [0]
            roots = [0]

            def make_rest(c):
                dve.wait_ge(heads_done, c.count())
                dve.tensor_tensor(rest[:, c.split, :], raw[:, c.raw, :], head[:, c.split, :].bitcast(F32),
                                  ALU.subtract).then_inc(rests_done, 1)

            def feed(upto):
                while fed[0] < min(upto, MOE0 + 2):
                    make_rest(At(fed[0]))
                    fed[0] += 1

            def job(name):
                feed(last_chunk(name) + 1 + AHEAD)
                dve.wait_ge(chunk_used, last_chunk(name) + 1)
                return bank(name)

            def split_rest(name, lo, hi):
                dve.wait_ge(hth_ready, plan.splits[name])
                dve.tensor_tensor(hTl[:, lo:hi, :], hT[:, lo:hi, :], hTh[:, lo:hi, :].bitcast(F32),
                                  ALU.subtract).then_inc(htl_ready, 1)

            def rms(eps=1e-6):
                now()
                for t in range(T):
                    did(dve.tensor_tensor_reduce(xn[:, t, :], x[:, t, :], x[:, t, :], 1.0, 0.0, ALU.mult, ALU.add, ss[:, t:t + 1]))
                now()
                dve.tensor_scalar(ss, ss, 1.0 / D, eps, ALU.mult, ALU.add).then_inc(sem("mean_square"), 1)
                roots[0] += 1
                dve.wait_ge(sem("root"), roots[0])
                did(dve.reciprocal(rstd, rstd))
                now()

            def norm(n, scale, shift=None):
                rms()
                for t in range(T):
                    ins = dve.tensor_scalar(xn[:, t, :], x[:, t, :], rstd[:, t:t + 1], None, ALU.mult)
                ins.then_inc(sem("xn_ready"), 1)
                for j in range(2):
                    dve.wait_ge(job_done, jobs_done(f"norm{n}.{j}"))
                    ps = flat4(bank(f"norm{n}.{j}"))
                    for i in range(4):
                        k = 4 * j + i
                        if shift is None:
                            ins = dve.tensor_scalar(hT[:, k, :], ps[:, i, :], scale[:, k:k + 1], None, ALU.mult)
                        else:
                            ins = dve.tensor_scalar(hT[:, k, :], ps[:, i, :], scale[:, k:k + 1], shift[:, k:k + 1], ALU.mult, ALU.add)
                        if i < 3:
                            did(ins)
                    ins.then_inc(evac["dve"], 1)
                    dve.wait_ge(evac["dve"], plan.jobs[f"norm{n}.{j}"][4])
                    dve.sem_inc(sem("hT_ready"), 1)
                    split_rest(f"norm{n}.{j}", 4 * j, 4 * j + 4)

            def last_norm(src_row, dst):
                rms()
                dve.wait_ge(sem("final_g_landed"), 16 * (src_row[0] + 1))
                for t in range(T):
                    ins = dve.scalar_tensor_tensor(out=dst[:, t, :], in0=x[:, t, :], scalar=rstd[:, t:t + 1],
                                                   in1=gbc[:, src_row[1], :], op0=ALU.mult, op1=ALU.mult)
                ins.then_inc(sem("block_done"), 1)
                dve.wait_ge(sem("block_done"), src_row[0] + 1)

            def angles(k):
                r, c_, m, n_int = aw[:, 2 * S:3 * S], aw[:, 3 * S:4 * S], aw[:, 0:S], posi
                did(dve.tensor_scalar(r, angle, freq[:, k:k + 1], None, ALU.mult))
                now()
                did(dve.tensor_scalar(n_int, r, 1.0 / (2 * PI), None, ALU.mult))
                now()
                did(dve.tensor_copy(c_, n_int))
                now()
                for part in (6.28125, 2 * PI - 6.28125):
                    did(dve.scalar_tensor_tensor(out=r, in0=c_, scalar=-part, in1=r, op0=ALU.mult, op1=ALU.add))
                    now()

                def fold(v):
                    for cmp, lim, step in ((ALU.is_gt, PI, -2 * PI), (ALU.is_lt, -PI, 2 * PI)):
                        did(dve.tensor_scalar(m, v, lim, step, cmp, ALU.mult))
                        now()
                        did(dve.tensor_tensor(v, v, m, ALU.add))
                        now()
                    did(dve.tensor_scalar(v, v, 3.1415925, -3.1415925, ALU.min, ALU.max))
                    now()
                fold(r)
                did(dve.tensor_scalar(c_, r, PI / 2, None, ALU.add))
                now()
                fold(c_)
                dve.sem_inc(sem("angles_ready"), 1)

            def mod(k, slices, before_):
                now()
                dve.sem_inc(sem("cond_ready"), 1) if k != 1 else None
                if k != 1:
                    dve.wait_ge(sem("cond_head"), k // 2 + 1)
                    dve.tensor_tensor(cHL[:, 1:2 * KD:2], cact if k == 0 else pcol("c_2", 0, 8),
                                      cHL[:, 0:2 * KD:2].bitcast(F32), ALU.subtract).then_inc(sem("cond_split"), 1)
                for j in range(slices):
                    feed(last_chunk(f"mod{k}.{j}") + 1 + AHEAD)
                    if j in (2, 5):
                        dve.wait_ge(sem("modrow_used"), before_ + j + 1)
                        dve.tensor_scalar(gbc[:, j // 3, :], bank(f"gate{k}.{j}")[:, :, :].rearrange("p b n -> p (b n)"),
                                          1.0 if k < 2 else 0.0, None, ALU.add).then_inc(evac["dve"], 1)
                for i in range(slices // 3):
                    g = col8("norm1_g" if i == 0 else "norm2_g", k) if k < 2 else pcol("g_norm_2", 0, 8)
                    if i == 0:
                        dve.wait_ge(sem("modrow_used"), before_ + slices)
                    did(dve.tensor_copy(sh[:, 8 * i:8 * i + 8], tb[1][:, 24 * i:24 * i + 8]))
                    did(dve.scalar_tensor_tensor(out=gs[:, 8 * i:8 * i + 8], in0=tb[1][:, 24 * i + 8:24 * i + 16], scalar=1.0,
                                                 in1=g, op0=ALU.add, op1=ALU.mult))
                now()
                dve.sem_inc(sem("modcols_read"), 1)

            def conv_taps(l, ks):
                for k in ks:
                    now()
                    for g in range(KW):
                        w_ = pcol("dw_conv_w", 124 * l + 4 * k + g)
                        if k == 0:
                            did(dve.tensor_scalar(conv[:, g, :], upad[:, g, 0:S], w_, pcol("dw_conv_b", 4 * l + g), ALU.mult, ALU.add))
                        else:
                            did(dve.scalar_tensor_tensor(out=conv[:, g, :], in0=upad[:, g, k:k + S], scalar=w_, in1=conv[:, g, :],
                                                         op0=ALU.mult, op1=ALU.add))

            def rope(k):
                tmp = aw4[0]
                for i, (name, buf) in enumerate((("rotq", qT), ("rotk", kT))):
                    dve.wait_ge(job_done, jobs_done(f"{name}{k}"))
                    dve.tensor_tensor(tmp, flat4(bank(f"{name}{k}")), over(trig[:, 1, :], [P, KW, S], 1), ALU.mult).then_inc(evac["dve"], 1)
                    did(dve.tensor_tensor(buf, buf, over(trig[:, 0, :], [P, KW, S], 1), ALU.mult))
                    now()
                    dve.wait_ge(evac["dve"], plan.jobs[f"{name}{k}"][4])
                    did(dve.tensor_tensor(buf, buf, tmp, ALU.add))
                    now()
                    dve.sem_inc(sem("roped"), 1)

            def attention(k):
                rope(k)
                for q, sc in enumerate((sc0, sc1)):
                    L = P * (q + 1)
                    name = f"score0.{k}" if q == 0 else f"score1b.{k}"
                    dve.wait_ge(evac["act"], plan.jobs[name][4])
                    diag = sc[:, :, q * P:(q + 1) * P]
                    did(dve.tensor_tensor(diag, diag, over(tri, [P, 8, P], 1), ALU.add))
                    now()
                    did(dve.tensor_reduce(mx[:, 8 * q:8 * q + 8], sc[:, :, 0:L], AX.X, ALU.max))
                    now()
                    dve.tensor_scalar(mx[:, 8 * q:8 * q + 8], mx[:, 8 * q:8 * q + 8], -1.0, None, ALU.mult).then_inc(sem("max_ready"), 1)
                for q, sc in enumerate((sc0, sc1)):
                    dve.wait_ge(sem("exp_ready"), 2 * k + q + 1)
                    did(dve.reciprocal(rs[:, 0:8], su[:, 8 * q:8 * q + 8]))
                    now()
                    if k < 2:
                        did(dve.tensor_scalar(rs[:, 4:8], rs[:, 4:8], lamc[:, k:k + 1], None, ALU.mult))
                        now()
                    for m in range(4 if k < 2 else 8):
                        did(dve.tensor_scalar(sc[:, m, :], sc[:, m, :], rs[:, m:m + 1], None, ALU.mult))
                    now()
                    if k < 2:
                        for h in range(4):
                            did(dve.scalar_tensor_tensor(out=sc[:, h, :], in0=sc[:, 4 + h, :], scalar=rs[:, 4 + h:5 + h], in1=sc[:, h, :],
                                                         op0=ALU.mult, op1=ALU.add))
                        now()
                    dve.sem_inc(sem("probs_ready"), 1)

            def column_mean_job(name, buf, n, eps=None):
                dve.wait_ge(job_done, jobs_done(name))
                src = flat4(bank(name)) if len(buf.shape) == 3 else bank(name)[:, 0, 0:S]
                if eps is None:
                    dve.tensor_scalar(buf, src, 1.0 / n, None, ALU.mult).then_inc(evac["dve"], 1)
                else:
                    dve.tensor_scalar(buf, src, 1.0 / n, eps, ALU.mult, ALU.add).then_inc(evac["dve"], 1)
                dve.wait_ge(evac["dve"], plan.jobs[name][4])

            def gate_product(name, gate):
                for j in range(2):
                    ps = job(f"{name}.{j}")
                    part = gate[:, :, j * NT:(j + 1) * NT]
                    dve.tensor_tensor(part, part, ps[:, :, :], ALU.mult).then_inc(evac["dve"], 1)

            def merge(k):
                dve.wait_ge(evac["dve"], max(plan.jobs[f"{n}{k}.1"][4] for n in ("yconv", "yattn")))
                dve.tensor_tensor(gateA, gateA, gateB, ALU.add).then_inc(sem("merged"), 1)
                for j in range(2):
                    split_rest(f"mix{k}.{j}", 4 * j, 4 * j + 4)

            def add_product(name, gate):
                for j in range(2):
                    ps = job(f"{name}.{j}")
                    part = x[:, :, j * NT:(j + 1) * NT]
                    if gate is None:
                        dve.tensor_tensor(part, part, ps[:, :, :], ALU.add).then_inc(evac["dve"], 1)
                    else:
                        tmp = gateB[:, :, j * NT:(j + 1) * NT]
                        dve.tensor_tensor(tmp, ps[:, :, :], over(gate[:, j * NT:(j + 1) * NT], [P, T, NT], 1),
                                          ALU.mult).then_inc(evac["dve"], 1)
                        dve.wait_ge(evac["dve"], plan.jobs[f"{name}.{j}"][4])
                        did(dve.tensor_tensor(part, part, tmp, ALU.add))
                dve.wait_ge(evac["dve"], plan.jobs[f"{name}.1"][4])

            def gated_hidden(s, nt, b=0):
                dve.wait_ge(sem("silu_ready"), s + 1)
                up = pair[0][:, 0:T, FB:2 * FB] if nt == T else pair[0][:, b:b + 1, FB:2 * FB]
                dve.tensor_tensor(act_[:, 0:nt, :], sg[:, 0:nt, :], up, ALU.mult).then_inc(act_ready, 1)

            def turned_rest(s, nt):
                dve.wait_ge(ath_ready, s + 1)
                dve.tensor_tensor(aTl[:, :, 0:nt * P], tb[0][:, :].rearrange("p (k s) -> p k s", k=2)[:, :, 0:nt * P],
                                  aTh[:, :, 0:nt * P].bitcast(F32), ALU.subtract).then_inc(atl_ready, 1)

            def ffn_step(c, s, nt, b=0):
                make_rest(c.next(2))
                turned_rest(s, nt)
                make_rest(c.next(3))
                make_rest(c.next(4))
                gated_hidden(s + 1, nt, b)

            def ffn(k, steps, gate):
                c0, s0 = at3[k], STEP0[k]
                feed(c0 + 2 + AHEAD)
                gated_hidden(s0, T)
                ffn_step(At(c0 + 2), s0, T)
                with dve.Fori(0, (steps - 2) // 2) as i:
                    for j in range(2):
                        ffn_step(At(c0 + 5 + 3 * j, i, RAW), i * 2 + (s0 + 1 + j), T)
                done = 1 + 2 * ((steps - 2) // 2)
                for s in range(done, steps - 1):
                    ffn_step(At(c0 + 2 + 3 * s), s0 + s, T)
                fed[0] = c0 + 2 + 3 * (steps - 1) + AHEAD
                turned_rest(s0 + steps - 1, T)
                dve.wait_ge(chunk_used, c0 + 3 * steps)
                for t in range(T):
                    y = pair[1 + t][:, :, :].rearrange("p b n -> p (b n)")
                    if gate is None:
                        did(dve.tensor_tensor(x[:, t, :], x[:, t, :], y, ALU.add))
                    else:
                        did(dve.tensor_tensor(xn[:, t, :], y, gate, ALU.mult))
                now()
                dve.sem_inc(sem("ffn_read"), 1)
                if gate is not None:
                    did(dve.tensor_tensor(x[:, :, :], x[:, :, :], xn[:, :, :], ALU.add))

            dve.wait_ge(sem("lambdas_landed"), 64)
            for l in range(2):
                for i in range(2):
                    did(dve.tensor_tensor_reduce(lamrow[:, 2 * i, l, 0:64], lamrow[:, 2 * i, l, 0:64], lamrow[:, 2 * i + 1, l, 0:64],
                                                 1.0, 0.0, ALU.mult, ALU.add, lam4[:, 2 * i + l:2 * i + l + 1]))
            now()
            dve.sem_inc(sem("lam_dots"), 1)
            dve.wait_ge(sem("lam_exp"), 1)
            did(dve.tensor_tensor(lam4[:, 0:2], lam4[:, 2:4], lam4[:, 0:2], ALU.subtract))
            now()
            for l in range(2):
                did(dve.tensor_scalar(lam4[:, l:l + 1], lam4[:, l:l + 1], -lam_init[l], None, ALU.add))
            now()
            dve.sem_inc(sem("lam_rows"), 1)
            dve.wait_ge(sem("lam_spread"), 1)
            did(dve.tensor_copy(lamc[:, 0:2], tb[1][:, 0:2]))
            dve.wait_ge(sem("params_turned"), 1)
            did(dve.tensor_copy(prm[:, :], tb[0][:, :]))
            dve.wait_ge(sem("positions_landed"), 16)
            did(dve.tensor_copy(angle, posi))
            now()
            dve.sem_inc(sem("params_ready"), 1)
            for l in range(2):
                did(dve.tensor_scalar(lamc[:, 2 + l:3 + l], pcol("subln_g", l), 1.0 - lam_init[l], None, ALU.mult))
            lam = pcol("lru_lambda_3", 0, 8)
            az, ez, s_, s2, p_ = (tmp8[:, 8 * i:8 * i + 8] for i in (0, 1, 2, 3, 0))
            did(dve.tensor_scalar(s2, lam, -1.0, None, ALU.mult))
            now()
            did(dve.tensor_tensor(az, s2, lam, ALU.max))
            now()
            dve.sem_inc(sem("lru_decay_in"), 1)
            dve.wait_ge(sem("lru_decay_exp"), 1)
            did(dve.tensor_scalar(s_, ez, 2.0, None, ALU.add))
            now()
            did(dve.reciprocal(s_, s_))
            now()
            did(dve.tensor_tensor(s_, s_, ez, ALU.mult))
            now()
            did(dve.tensor_tensor(s2, s_, s_, ALU.mult))
            now()
            did(dve.tensor_scalar(p_, s2, 1.0 / 17, 1.0 / 15, ALU.mult, ALU.add))
            for n in (13, 11, 9, 7, 5, 3, 1):
                now()
                did(dve.tensor_tensor(p_, p_, s2, ALU.mult))
                now()
                did(dve.tensor_scalar(p_, p_, 1.0 / n, None, ALU.add))
            now()
            did(dve.tensor_tensor(p_, p_, s_, ALU.mult))
            did(dve.tensor_scalar(s2, lam, -1.0, 0.0, ALU.mult, ALU.max))
            now()
            did(dve.scalar_tensor_tensor(out=p_, in0=p_, scalar=2.0, in1=s2, op0=ALU.mult, op1=ALU.add))
            now()
            did(dve.tensor_scalar(sp8, p_, -8.0, None, ALU.mult))
            did(dve.memset(cHL[:, :].bitcast(F32), 0.0))
            angles(0)
            dve.wait_ge(sem("x_landed"), 16)
            nn = 0
            for l in range(2):
                mod(*mods[l])
                norm(nn, gs[:, 0:8], sh[:, 0:8])
                nn += 1
                feed(last_chunk(f"gb{l}.0") + 1 + AHEAD)
                dve.wait_ge(evac["act"], plan.jobs[f"gb{l}.0"][4])
                did(dve.tensor_tensor(upad[:, :, PADS:], upad[:, :, PADS:], oT[:, :, :], ALU.mult))
                k = 0
                for name in (f"q{l}.0", f"k{l}.0", f"v{l}.0") + tuple(f"gates{l}.{j}" for j in range(4)):
                    feed(last_chunk(name) + AHEAD)
                    conv_taps(l, range(k, min(k + 3, CONV_K)))
                    k += 3
                    feed(last_chunk(name) + 1 + AHEAD)
                conv_taps(l, range(k, CONV_K))
                attention(l)
                dve.wait_ge(evac["act"], plan.jobs[f"pv{l}"][4])
                did(dve.tensor_tensor(kq[0], oT[:, :, :], oT[:, :, :], ALU.mult))
                now()
                dve.sem_inc(sem("squares_ready"), 1)
                column_mean_job(f"subln{l}", kq[1], P, 1e-5)
                dve.sem_inc(sem("sub_var"), 1)
                dve.wait_ge(sem("sub_root"), l + 1)
                did(dve.reciprocal(kq[1], kq[1]))
                now()
                did(dve.scalar_tensor_tensor(out=hT[:, 0:4, :].rearrange("p k s -> p (k s)"), in0=oT[:, :, :].rearrange("p k s -> p (k s)"),
                                             scalar=lamc[:, 2 + l:3 + l], in1=qkv[:, 1, :], op0=ALU.mult, op1=ALU.mult))
                now()
                dve.sem_inc(sem("hT_ready"), 1)
                split_rest(f"attn{l}", 0, 4)
                gate_product(f"yattn{l}", gateA)
                column_mean_job(f"lnmean{l}", kq[0][:, 0, :], W)
                did(dve.tensor_tensor(conv, conv, over(kq[0][:, 0, :], [P, KW, S], 1), ALU.subtract))
                now()
                did(dve.tensor_tensor(kq[2], conv, conv, ALU.mult))
                now()
                dve.sem_inc(sem("squares_ready"), 1)
                column_mean_job(f"lnvar{l}", kq[1][:, 0, :], W, 1e-5)
                dve.sem_inc(sem("ln_var"), 1)
                dve.wait_ge(sem("ln_root"), l + 1)
                did(dve.reciprocal(kq[1][:, 0, :], kq[1][:, 0, :]))
                now()
                did(dve.tensor_tensor(conv, conv, over(kq[1][:, 0, :], [P, KW, S], 1), ALU.mult))
                now()
                dve.sem_inc(sem("ln_ready"), 1)
                dve.sem_inc(sem("hT_ready"), 1)
                split_rest(f"conv{l}", 4, 8)
                gate_product(f"yconv{l}", gateB)
                merge(l)
                dve.sem_inc(sem("hT_ready"), 1)
                dve.sem_inc(sem("hT_ready"), 1)
                add_product(f"wout{l}", gbc[:, 0, :])
                norm(nn, gs[:, 8:16], sh[:, 8:16])
                nn += 1
                ffn(*DENSE[l], gbc[:, 1, :])
            last_norm((0, 0), x)
            dve.wait_ge(sem("pool_landed"), 48)
            angles(1)
            mod(*mods[2])
            norm(nn, gs[:, 0:8], sh[:, 0:8])
            nn += 1
            for name in ("up.0", "zp.0", "q2.0", "k2.0", "v2.0"):
                feed(last_chunk(name) + 1 + AHEAD)
            dve.wait_ge(evac["act"], plan.jobs["zp.0"][4])
            src = upad[:, :, PADS:]
            for level in range(4):
                dst, h = POOLBUF[level % 2], 2 ** level
                did(dve.tensor_copy(dst[:, level:, 0:h], src[:, level:, 0:h]))
                did(dve.tensor_tensor(dst[:, level:, h:], src[:, level:, h:], src[:, level:, 0:S - h], ALU.add))
                now()
                src = dst
            for g in range(4):
                did(dve.tensor_tensor(dpool[:, g, :], POOLBUF[g % 2][:, g, :], invcnt[:, g, :], ALU.mult))
            now()
            did(dve.tensor_tensor(dpool, dpool, upad[:, :, PADS:], ALU.subtract))
            now()
            dve.sem_inc(sem("pool_ready"), 1)
            for name in ["gates2.0", "gates2.1", "gates2.2", "gates2.3", "za.0"]:
                feed(last_chunk(name) + 1 + AHEAD)
            dve.wait_ge(job_done, jobs_done("pool"))
            for g in range(KW):
                ins = dve.scalar_tensor_tensor(out=hT[:, 4 + g, :], in0=flat4(bank("pool"))[:, g, :], scalar=pcol("pool_scale_2", g),
                                               in1=xn[:, 0, g * S:(g + 1) * S], op0=ALU.mult, op1=ALU.mult)
            ins.then_inc(evac["dve"], 1)
            dve.wait_ge(evac["dve"], plan.jobs["pool"][4])
            dve.sem_inc(sem("hT_ready"), 1)
            split_rest("conv2", 4, 8)
            gate_product("yconv2", gateA)
            attention(2)
            dve.wait_ge(evac["act"], plan.jobs["pv2"][4])
            did(dve.tensor_tensor(hT[:, 0:4, :], oT[:, :, :], upad[:, :, PADS:], ALU.mult))
            now()
            dve.sem_inc(sem("hT_ready"), 1)
            split_rest("attn2", 0, 4)
            gate_product("yattn2", gateB)
            merge(2)
            dve.sem_inc(sem("hT_ready"), 1)
            dve.sem_inc(sem("hT_ready"), 1)
            add_product("wout2", gbc[:, 0, :])
            last_norm((1, 1), x)
            did(dve.memset(upu[:, :, 0:3], 0.0))
            now()
            dve.sem_inc(sem("upu_zero"), 1)
            for l in range(2):
                norm(nn, col8("norm_mix_3", l))
                nn += 1
                feed(last_chunk(f"bg{l}.0") + 1 + AHEAD)
                ps = job(f"vv{l}.0")
                dve.wait_ge(evac["act"], plan.jobs[f"cg{l}.0"][4])
                dve.tensor_tensor(upad[:, :, PADS:], flat4(ps), kq[0], ALU.mult).then_inc(evac["dve"], 1)
                dve.wait_ge(evac["dve"], plan.jobs[f"vv{l}.0"][4])
                feed(last_chunk(f"uu{l}.0") + 1 + AHEAD)
                y = hT[:, 0:4, :]
                ya = aw4[2]
                for k in range(3):
                    now()
                    for g in range(KW):
                        w_, src = pcol("conv_w_3", 12 * l + 4 * k + g), upad[:, g, PADS - 2 + k:PADS - 2 + k + S]
                        if k == 0:
                            did(dve.tensor_scalar(ya[:, g, :], src, w_, None, ALU.mult))
                        else:
                            did(dve.scalar_tensor_tensor(out=ya[:, g, :], in0=src, scalar=w_, in1=ya[:, g, :], op0=ALU.mult, op1=ALU.add))
                now()
                feed(last_chunk(f"gg{l}.0") + 1 + AHEAD)
                dve.wait_ge(evac["act"], plan.jobs[f"uu{l}.0"][4])
                did(dve.tensor_tensor(y, ya, kq[1], ALU.mult))
                for k in range(4):
                    now()
                    for g in range(KW):
                        w_, src = pcol("lru_conv_w_3", 16 * l + 4 * k + g), upu[:, g, k:k + S]
                        if k == 0:
                            did(dve.tensor_scalar(oT[:, g, :], src, w_, pcol("lru_conv_b_3", 4 * l + g), ALU.mult, ALU.add))
                        else:
                            did(dve.scalar_tensor_tensor(out=oT[:, g, :], in0=src, scalar=w_, in1=oT[:, g, :], op0=ALU.mult, op1=ALU.add))
                now()
                dve.sem_inc(sem("uc_ready"), 1)
                dve.sem_inc(sem("hT_ready"), 1)
                dve.wait_ge(evac["act"], plan.jobs[f"lrui{l}"][4])
                for g in range(KW):
                    did(dve.tensor_scalar(aw4[0][:, g, :], aw4[0][:, g, :], sp8[:, 4 * l + g:4 * l + g + 1], None, ALU.mult))
                now()
                dve.sem_inc(sem("log_a"), 1)
                did(dve.tensor_tensor(aw4[1], aw4[1], oT[:, :, :], ALU.mult))
                dve.wait_ge(sem("lru_exp"), l + 1)
                did(dve.tensor_scalar(aw4[0], aw4[2], -1.0, 1.0, ALU.mult, ALU.add))
                now()
                did(dve.reciprocal(aw4[0], aw4[0]))
                now()
                did(dve.scalar_tensor_tensor(out=aw[:, 0:1024], in0=aw[:, 2048:3072], scalar=-2.0, in1=aw[:, 0:1024], op0=ALU.mult, op1=ALU.mult))
                now()
                dve.sem_inc(sem("b_square"), 1)
                dve.wait_ge(sem("b_root"), l + 1)
                did(dve.tensor_tensor(aw4[1], aw4[1], aw4[2], ALU.mult))
                now()
                for g in range(KW):
                    did(dve.tensor_tensor_scan(oT[:, g, :], lru_a[:, g, :], aw4[1][:, g, :], 0.0, ALU.mult, ALU.add))
                now()
                dve.wait_ge(evac["act"], plan.jobs[f"gg{l}.0"][4])
                did(dve.tensor_tensor(hT[:, 4:8, :], oT[:, :, :], kq[2], ALU.mult))
                now()
                dve.sem_inc(sem("hT_ready"), 1)
                split_rest(f"lru{l}.0", 0, 4)
                split_rest(f"lru{l}.1", 4, 8)
                add_product(f"wout{3 + l}", None)
                norm(nn, col8("norm_ffn_3", l))
                nn += 1
                if l == 0:
                    ffn(*DENSE[2], None)
            dve.wait_ge(sem("logits_done"), 1)
            for t in range(T):
                did(dve.tensor_copy(lg[:, t, :], tb[1][:, 8 * t:8 * t + 8]))
            now()
            i8 = iota[:, 0:E]
            picks = ((m1, sel), (m2, o8))
            for n, (m, pick) in enumerate(picks):
                did(dve.tensor_reduce(m, lg, AX.X, ALU.max))
                now()
                did(dve.tensor_tensor(w8, lg, over(m, [P, T, E], 2), ALU.is_equal))
                now()
                did(dve.scalar_tensor_tensor(out=w8, in0=w8, scalar=-99.0, in1=over(i8, [P, T, E], 1), op0=ALU.mult, op1=ALU.add))
                now()
                did(dve.tensor_reduce(rstd, w8, AX.X, ALU.min))
                now()
                did(dve.tensor_tensor(pick, w8, over(rstd, [P, T, E], 2), ALU.is_equal))
                now()
                if n == 0:
                    did(dve.scalar_tensor_tensor(out=lg, in0=pick, scalar=-3.0e38, in1=lg, op0=ALU.mult, op1=ALU.add))
                    now()
            did(dve.tensor_tensor(m2, m2, m1, ALU.subtract))
            now()
            dve.sem_inc(sem("gap_ready"), 1)
            dve.wait_ge(sem("gap_exp"), 1)
            did(dve.tensor_scalar(m1, m2, 1.0, None, ALU.add))
            now()
            did(dve.reciprocal(m1, m1))
            now()
            did(dve.tensor_tensor(m2, m2, m1, ALU.mult))
            now()
            for t in range(T):
                did(dve.tensor_scalar(comb[:, t, :], sel[:, t, :], m1[:, t:t + 1], None, ALU.mult))
            now()
            for t in range(T):
                did(dve.scalar_tensor_tensor(out=comb[:, t, :], in0=o8[:, t, :], scalar=m2[:, t:t + 1], in1=comb[:, t, :], op0=ALU.mult, op1=ALU.add))
            did(dve.tensor_tensor(sel, sel, o8, ALU.add))
            now()
            dve.sem_inc(sem("chosen"), 1)
            dve.wait_ge(sem("ranks_done"), 1)
            did(dve.tensor_copy(pos.rearrange("p t e -> p (t e)"), tb[1][:, 32:48]))
            did(dve.tensor_reduce(rstd[:, 0:1], tb[1][:, 48:56], AX.X, ALU.max))
            now()
            did(dve.tensor_scalar(wins[0:1, 0:1], rstd[0:1, 0:1], float(P), None, ALU.is_gt))
            now()
            dve.sem_inc(sem("windows_ready"), 1)
            feed(MOE0 + 2)

            def expert(it, e):
                s0 = it * STEPS3 + STEP0[3]
                for t in range(T):
                    rank = pos[:, t, bass.ds(e, 1)]
                    dve.tensor_scalar(pcomb[:, t, :], iota, rank, comb[:, t, bass.ds(e, 1)], ALU.is_equal, ALU.mult)
                    ins = dve.tensor_scalar(ptok[:, t, :], iota, rank, sel[:, t, bass.ds(e, 1)], ALU.is_equal, ALU.mult)
                ins.then_inc(sem("picks_ready"), 1)
                dve.wait_ge(sem("gather_done"), it + 1)
                dve.tensor_tensor(xe, pair[2][:, :, :].rearrange("p b (k s) -> p (b k) s", s=P),
                                  over(col8("norm_ffn_3", 1), [P, KD, P], 2), ALU.mult).then_inc(sem("gathered"), 1)
                dve.wait_ge(sem("xe_head"), it + 1)
                dve.tensor_tensor(hTl[:, :, 0:P], xe, hTh[:, :, 0:P].bitcast(F32), ALU.subtract).then_inc(sem("xe_rest"), 1)
                at = At(MOE0, it, PER)
                make_rest(at.next(2))
                make_rest(at.next(3))
                gated_hidden(s0, 1, 0)
                for s in range(STEPS3 - 1):
                    ffn_step(at.next(2 + 3 * s), s0 + s, 1, (s + 1) % 2)
                turned_rest(s0 + (STEPS3 - 1), 1)
                make_rest(at.next(PER + 1))
                for t in range(T):
                    dve.wait_ge(sem("scattered"), it * 2 + (t + 1))
                    dve.tensor_tensor(x[:, t, :], x[:, t, :], pair[2 - t][:, :, :].rearrange("p b n -> p (b n)"),
                                      ALU.add).then_inc(sem("scatter_added"), 1)

            with dve.Fori(0, E) as e:
                expert(e, e)
            more = dve.value_load(wins[0:1, 0:1], min_val=0, max_val=1)
            with dve.If(more):
                dve.wait_ge(sem("scatter_added"), 2 * E)
                dve.tensor_scalar(pos.rearrange("p t e -> p (t e)"), pos.rearrange("p t e -> p (t e)"), -float(P), None,
                                  ALU.add).then_inc(sem("window_moved"), 1)
                dve.wait_ge(sem("window_moved"), 1)
                with dve.Fori(0, E) as e:
                    expert(e + E, e)
            dve.wait_ge(sem("scatter_added"), more * (2 * E) + 2 * E)
            for t in range(T):
                did(dve.tensor_tensor_reduce(xn[:, t, :], x[:, t, :], x[:, t, :], 1.0, 0.0, ALU.mult, ALU.add, ss[:, t:t + 1]))
            now()
            dve.tensor_scalar(ss, ss, 1.0 / D, 1e-6, ALU.mult, ALU.add).then_inc(sem("last_mean_square"), 1)
            dve.wait_ge(sem("last_root"), 1)
            did(dve.reciprocal(rstd, rstd))
            now()
            dve.wait_ge(sem("final_g_landed"), 48)
            for t in range(T):
                ins = dve.scalar_tensor_tensor(out=xn[:, t, :], in0=x[:, t, :], scalar=rstd[:, t:t + 1], in1=gbc[:, 1, :],
                                               op0=ALU.mult, op1=ALU.mult)
            ins.then_inc(sem("block_done"), 1)

        @block.tensor
        def _(pe):
            def free(name):
                b = plan.before(name)
                if b:
                    pe.wait_ge(evac[b[0]], b[1])

            def three(out_, lh, ll, rh, rl, start, stop):
                pe.matmul(out_, lh, rh, start=start, stop=False, skip_group_check=True)
                pe.matmul(out_, lh, rl, start=False, stop=False, skip_group_check=True)
                return pe.matmul(out_, ll, rh, start=False, stop=stop, skip_group_check=True)

            def linear(name, cols, k0=0, turn=False):
                for j in range(cols // NT):
                    n, c0, nch = plan.jobs[f"{name}.{j}"][0:3]
                    free(f"{name}.{j}")
                    ps = pair[n % 3]
                    for ch in range(nch):
                        c = At(c0 + ch)
                        pe.wait_ge(rests_done, c.count())
                        for k in range(4):
                            kk = k0 + 4 * ch + k
                            first, last = ch == 0 and k == 0, ch == nch - 1 and k == 3
                            if turn:
                                for i in range(4):
                                    wcols = slice(k * NT + i * P, k * NT + (i + 1) * P)
                                    ins = three(flat4(ps)[:, i, :], head[:, c.split, wcols], rest[:, c.split, wcols],
                                                hTh[:, kk, :], hTl[:, kk, :], first and i % 2 == 0, last)
                            else:
                                wcols = slice(k * NT, (k + 1) * NT)
                                for t in range(T):
                                    toks = slice(t * P, (t + 1) * P)
                                    ins = three(ps[:, t, :], hTh[:, kk, toks], hTl[:, kk, toks],
                                                head[:, c.split, wcols], rest[:, c.split, wcols], first, last)
                        ins.then_inc(chunk_used, 1)

            def mod(k, slices, before_):
                pe.wait_ge(sem("cond_split"), k // 2 + 1)
                for j in range(slices):
                    n, c0, nch = plan.jobs[f"mod{k}.{j}"][0:3]
                    free(f"mod{k}.{j}")
                    ps = pair[n % 3]
                    for ch in range(nch):
                        c = At(c0 + ch)
                        pe.wait_ge(rests_done, c.count())
                        for i in range(4):
                            kk = 4 * (ch % 2) + i
                            for w_ in (head, rest):
                                ins = pe.matmul(ps[0:66, ch // 2, :], cHL[:, 2 * kk:2 * kk + 66], w_[:, c.split, i * NT:(i + 1) * NT],
                                                start=kk == 0 and w_ is head, stop=kk == 7 and w_ is rest)
                        ins.then_inc(chunk_used, 1)
                    pe.wait_ge(evac["act"], plan.jobs[f"mod{k}.{j}"][4])
                    pe.wait_ge(sem("bias_row"), 16 * (before_ + j + 1))
                    if j in (2, 5):
                        free(f"gate{k}.{j}")
                        for b in range(2):
                            ins = pe.matmul(bank(f"gate{k}.{j}")[:, b, :], ones[0:3, :], modrow[0:3, b * NT:(b + 1) * NT], start=True, stop=True)
                    else:
                        if j == 0 and k > 0:
                            pe.wait_ge(sem("modcols_read"), k)
                        if j == 0 and k == 0:
                            pe.wait_ge(sem("params_ready"), 1)
                        for i in range(KD):
                            ins = pe.matmul(tb[1][:, 8 * j + i:8 * j + i + 1], modrow[0:3, i * P:(i + 1) * P], ones[0:3, 0:1], start=True, stop=True)
                    ins.then_inc(sem("modrow_used"), 1)
                    if j in (2, 5):
                        pe.wait_ge(sem("modrow_used"), before_ + j + 1)
                        pe.sem_inc(job_done, 1)

            def turn4(name, src):
                free(name)
                for i in range(4):
                    for t in range(T):
                        ins = pe.transpose(flat4(bank(name))[:, i, t * P:(t + 1) * P], src(i, t), ident)
                ins.then_inc(job_done, 1)

            def norm(n):
                pe.wait_ge(sem("xn_ready"), n + 1)
                for j in range(2):
                    turn4(f"norm{n}.{j}", lambda i, t: xn[:, t, (4 * j + i) * P:(4 * j + i + 1) * P])

            def ready(name):
                pe.wait_ge(htl_ready, plan.splits[name])

            combos = ((0, 0), (1, 0), (1, 1))

            def attention(k):
                pe.wait_ge(sem("trig_ready"), 1 if k < 2 else 2)
                for name, job_, buf in (("rotq", f"q{k}.0", qT), ("rotk", f"k{k}.0", kT)):
                    free(f"{name}{k}")
                    pe.wait_ge(evac["act"], plan.jobs[job_][4])
                    for g in range(KW):
                        ins = pe.matmul(flat4(bank(f"{name}{k}"))[:, g, :], rot, buf[:, g, :], start=True, stop=True)
                    ins.then_inc(job_done, 1)
                pe.wait_ge(sem("roped"), 2 * k + 2)
                for name, q, gg in ((f"score0.{k}", 0, range(4)), (f"score1a.{k}", 1, (0, 1)), (f"score1b.{k}", 1, (2, 3))):
                    free(name)
                    L = P * (q + 1)
                    for i, g in enumerate(gg):
                        for r in range(2):
                            rows = slice(64 * r, 64 * r + 64)
                            ins = pe.matmul(bank(name)[:, r, i * L:(i + 1) * L], qT[rows, g, q * P:(q + 1) * P], kT[rows, g, 0:L],
                                            start=True, stop=True)
                    ins.then_inc(job_done, 1)
                groups = [(ci, r) for ci in range(3) for r in range(1 if k < 2 else 2)]
                for j in range(2 if k < 2 else 3):
                    free(f"turn{k}.{j}")
                    for b, (ci, r) in enumerate(groups[2 * j:2 * j + 2]):
                        q, kt = combos[ci]
                        pe.wait_ge(sem("probs_ready"), 2 * k + q + 1)
                        for h in range(4):
                            ins = pe.transpose(bank(f"turn{k}.{j}")[:, b, h * P:(h + 1) * P], (sc0, sc1)[q][:, 4 * r + h, kt * P:(kt + 1) * P], ident)
                    ins.then_inc(job_done, 1)
                free(f"pv{k}")
                pe.wait_ge(evac["act"], plan.jobs[f"turn{k}.{1 if k < 2 else 2}"][4])
                ps = flat4(bank(f"pv{k}"))
                for g in range(4):
                    for r in range(1 if k < 2 else 2):
                        rows = slice(0, P) if k < 2 else slice(64 * r, 64 * r + 64)
                        vcols = slice(g * P, (g + 1) * P) if k < 2 else slice((2 * g + r) * 64, (2 * g + r + 1) * 64)
                        for ci, (q, kt) in enumerate(combos):
                            src = aT[:, ci if k < 2 else 2 * ci + r, g * P:(g + 1) * P]
                            ins = pe.matmul(ps[rows, g, q * P:(q + 1) * P], vt[:, kt, vcols], src, start=kt == 0, stop=kt == q)
                ins.then_inc(job_done, 1)

            def mix(k):
                pe.wait_ge(sem("merged"), k + 1)
                for j in range(2):
                    turn4(f"mix{k}.{j}", lambda i, t: gateA[:, t, (4 * j + i) * P:(4 * j + i + 1) * P])
                ready(f"mix{k}.1")
                linear(f"wout{k}", D)

            def gate_up(c, s, half, nt, b, wait_for):
                if half == 0:
                    wait(pe, act_ready, wait_for)
                pe.wait_ge(rests_done, c.count())
                wh = head[:, c.split, :].rearrange("p (m k n) -> p m k n", m=2, k=4)
                wl = rest[:, c.split, :].rearrange("p (m k n) -> p m k n", m=2, k=4)
                for k in range(4):
                    for t in range(nt):
                        toks = slice(t * P, (t + 1) * P)
                        ins = three(pair[0][:, b + t, :].rearrange("p (m n) -> p m n", m=2), hTh[:, 4 * half + k, toks], hTl[:, 4 * half + k, toks],
                                    wh[:, :, k, :], wl[:, :, k, :], half == 0 and k == 0, half == 1 and k == 3)
                        if k == 3 and t == nt - 1:
                            ins.then_inc(chunk_used, 1)

            def turn_hidden(s, nt):
                pe.wait_ge(act_ready, s + 1)
                wait(pe, atl_ready, s)
                for t in range(nt):
                    for k in range(2):
                        ins = pe.transpose(tb[0][:, k * S + t * P:k * S + (t + 1) * P], act_[:, t, k * P:(k + 1) * P], ident)
                ins.then_inc(turned, 1)

            def down(c, s, nt, first, last):
                pe.wait_ge(rests_done, c.count())
                pe.wait_ge(atl_ready, s + 1)
                for k in range(2):
                    for t in range(nt):
                        toks = slice(t * P, (t + 1) * P)
                        for n in range(2):
                            wcols = slice(k * D + n * NT, k * D + (n + 1) * NT)
                            ins = three(pair[1 + t][:, n, :], aTh[:, k, toks], aTl[:, k, toks], head[:, c.split, wcols],
                                        rest[:, c.split, wcols], first and k == 0, last and k == 1)
                ins.then_inc(chunk_used, 1)

            def ffn_step(c, s, nt, first, b=0, lag=0):
                gate_up(c, s + 1, 0, nt, b, s + 1 - lag)
                turn_hidden(s, nt)
                gate_up(c.next(1), s + 1, 1, nt, b, None)
                down(c.next(2), s, nt, first, False)

            def ffn(k, steps):
                c0, s0 = at3[k], STEP0[k]
                for eng in ("act", "dve"):
                    pe.wait_ge(evac[eng], counts_at[k][eng])
                gate_up(At(c0), s0, 0, T, 0, s0)
                gate_up(At(c0 + 1), s0, 1, T, 0, None)
                ffn_step(At(c0 + 2), s0, T, True)
                with pe.Fori(0, (steps - 2) // 2) as i:
                    for j in range(2):
                        ffn_step(At(c0 + 5 + 3 * j, i, RAW), i * 2 + (s0 + 1 + j), T, False)
                done = 1 + 2 * ((steps - 2) // 2)
                for s in range(done, steps - 1):
                    ffn_step(At(c0 + 2 + 3 * s), s0 + s, T, False)
                turn_hidden(s0 + steps - 1, T)
                c = At(c0 + 2 + 3 * (steps - 1))
                down(c, s0 + steps - 1, T, False, True)
                pe.wait_ge(sem("ffn_read"), k + 1)

            def sum_over_partitions(name, buf, n):
                free(name)
                if n == 1:
                    for b in range(2):
                        ins = pe.matmul(bank(name)[:, b, :], ones[:, :], buf[:, b * NT:(b + 1) * NT], start=True, stop=True)
                else:
                    for g in range(n):
                        ins = pe.matmul(bank(name)[:, 0, 0:S], ones[:, :], buf[:, g, :], start=g == 0, stop=g == n - 1)
                ins.then_inc(job_done, 1)

            pe.wait_ge(sem("const_landed"), 16)
            pe.wait_ge(sem("ones_ready"), 1)
            pe.wait_ge(sem("lam_rows"), 1)
            pe.matmul(tb[1][:, 0:2], ones[0:1, :], lam4[:, 0:2], start=True, stop=True).then_inc(sem("lam_spread"), 1)
            pe.wait_ge(sem("params_landed"), 16 * len(PARAM_LOADS))
            for i in range(PARAM_TILES):
                ins = pe.transpose(tb[0][:, i * P:(i + 1) * P], praw[:, i, :], ident)
            ins.then_inc(sem("params_turned"), 1)
            nn = 0
            for l in range(2):
                mod(*mods[l])
                norm(nn)
                ready(f"norm{nn}.1")
                nn += 1
                linear(f"ga{l}", 512, turn=True)
                linear(f"gb{l}", 512, turn=True)
                linear(f"q{l}", 512, turn=True)
                linear(f"k{l}", 512, turn=True)
                linear(f"v{l}", 512)
                linear(f"gates{l}", 2048)
                attention(l)
                pe.wait_ge(sem("squares_ready"), 2 * l + 1)
                sum_over_partitions(f"subln{l}", qkv[:, 0, :], 1)
                ready(f"attn{l}")
                linear(f"yattn{l}", D)
                sum_over_partitions(f"lnmean{l}", conv, KW)
                pe.wait_ge(sem("squares_ready"), 2 * l + 2)
                sum_over_partitions(f"lnvar{l}", kq[2], KW)
                ready(f"conv{l}")
                linear(f"yconv{l}", D, k0=4)
                mix(l)
                norm(nn)
                ready(f"norm{nn}.1")
                nn += 1
                ffn(*DENSE[l])
            mod(*mods[2])
            norm(nn)
            ready(f"norm{nn}.1")
            nn += 1
            for name in ("up", "zp", "q2", "k2"):
                linear(name, 512, turn=True)
            linear("v2", 512)
            linear("gates2", 2048)
            linear("za", 512, turn=True)
            pe.wait_ge(sem("pool_ready"), 1)
            pe.wait_ge(sem("pool_landed"), 48)
            free("pool")
            for g in range(KW):
                ins = pe.matmul(flat4(bank("pool"))[:, g, :], wgrp[:, g, :], dpool[:, g, :], start=True, stop=True)
            ins.then_inc(job_done, 1)
            ready("conv2")
            linear("yconv2", D, k0=4)
            attention(2)
            ready("attn2")
            linear("yattn2", D)
            mix(2)
            for l in range(2):
                norm(nn)
                ready(f"norm{nn}.1")
                nn += 1
                for name in ("cg", "bg", "vv", "uu", "gg"):
                    linear(f"{name}{l}", 512, turn=True)
                pe.wait_ge(sem("uc_ready"), l + 1)
                pe.wait_ge(sem("lru_landed"), 64 * (l + 1))
                for i, name in enumerate(("lrur", "lrui")):
                    free(f"{name}{l}")
                    for g in range(KW):
                        ins = pe.matmul(flat4(bank(f"{name}{l}"))[:, g, :], wbd[:, i, g, :], oT[:, g, :], start=True, stop=True)
                    ins.then_inc(job_done, 1)
                ready(f"lru{l}.1")
                linear(f"wout{3 + l}", D)
                norm(nn)
                if l == 0:
                    ready(f"norm{nn}.1")
                    nn += 1
                    ffn(*DENSE[2])
            pe.wait_ge(evac["dve"], plan.jobs["norm8.1"][4])
            pe.wait_ge(sem("router_landed"), 16)
            for t in range(T):
                for k in range(KD):
                    ins = pe.matmul(tb[1][:, E * t:E * t + E], hT[:, k, t * P:(t + 1) * P], wrt[:, k, :], start=k == 0, stop=k == KD - 1)
            ins.then_inc(sem("logits_done"), 1)
            pe.wait_ge(sem("chosen"), 1)
            pe.matmul(tb[1][:, 32:40], before, sel[:, 0, :], start=True, stop=True)
            pe.matmul(tb[1][:, 40:48], ones[:, :], sel[:, 0, :], start=True, stop=False)
            pe.matmul(tb[1][:, 40:48], before, sel[:, 1, :], start=False, stop=True)
            pe.matmul(tb[1][:, 48:56], ones[:, :], sel[:, 0, :], start=True, stop=False)
            pe.matmul(tb[1][:, 48:56], ones[:, :], sel[:, 1, :], start=False, stop=True).then_inc(sem("ranks_done"), 1)
            pe.wait_ge(htl_ready, plan.splits["norm8.1"])
            pe.wait_ge(sem("windows_ready"), 1)

            def expert(it, wait_scatter=True):
                s0 = it * STEPS3 + STEP0[3]
                pe.wait_ge(sem("picks_ready"), it + 1)
                for k in range(KD):
                    for t in range(T):
                        ins = pe.matmul(pair[2][:, k // 4, (k % 4) * P:(k % 4 + 1) * P], xn[:, t, k * P:(k + 1) * P], ptok[:, t, :],
                                        start=t == 0, stop=t == 1)
                ins.then_inc(sem("gather_done"), 1)
                for t in range(T):
                    ins = pe.transpose(tb[1][:, t * P:(t + 1) * P], pcomb[:, t, :], ident)
                ins.then_inc(sem("combine_turned"), 1)
                pe.wait_ge(sem("xe_rest"), it + 1)
                at = At(MOE0, it, PER)
                gate_up(at, s0, 0, 1, 0, s0 - 1)
                gate_up(at.next(1), s0, 1, 1, 0, None)
                for s in range(STEPS3 - 1):
                    ffn_step(at.next(2 + 3 * s), s0 + s, 1, s == 0, (s + 1) % 2, 1)
                turn_hidden(s0 + (STEPS3 - 1), 1)
                c = at.next(PER - 1)
                down(c, s0 + (STEPS3 - 1), 1, False, True)
                pe.wait_ge(sem("y_ready"), it + 1)
                for t in range(T):
                    for n in range(2):
                        ins = pe.matmul(pair[2 - t][:, n, :], pslot[:, t * P:(t + 1) * P], ysb[:, n * NT:(n + 1) * NT], start=True, stop=True)
                    ins.then_inc(sem("scattered"), 1)
                pe.wait_ge(sem("scatter_added"), it * 2 + 2)

            with pe.Fori(0, E) as e:
                expert(e)
            more = pe.value_load(wins[0:1, 0:1], min_val=0, max_val=1)
            with pe.If(more):
                with pe.Fori(0, E) as e:
                    expert(e + E)


INPUTS = ["x", "positions", "ada_w", "ada_b", "w_in", "lambda_q1", "lambda_k1", "lambda_q2", "lambda_k2",
          "w_attn_o", "w_conv_o", "w_out", "w_ffn_in", "w_ffn_out", "final_g", "w_ada_2", "b_ada_2", "w_in_2",
          "w_pool_grp_2", "w_pool_up_2", "w_attn_up_2", "w_out_2", "g_final_2", "norm_final_3", "w_in_3",
          "lru_wa_3", "lru_wx_3", "w_out_3", "ffn_w_gate_3", "ffn_w_up_3", "ffn_w_down_3", "w_router_3",
          "moe_w_gate_3", "moe_w_up_3", "moe_w_down_3"]


def kernel(**inputs):
    import numpy as np
    import concourse.bacc as bacc
    from concourse.bass_utils import run_bass_kernel_spmd as run

    nc = bacc.Bacc("TRN2", target_bir_lowering=False, num_devices=1)
    square, rows = shape_constants()
    given = {name: np.ascontiguousarray(inputs[name]) for name in INPUTS}
    for name, _ in PARAM_ROWS:
        given["p_" + name] = np.ascontiguousarray(inputs[name]).reshape(-1, P)
    given["square"], given["rows"] = square, rows
    arrays = {f"in_{name}": v for name, v in given.items()}
    a = {name: nc.dram_tensor(f"in_{name}", v.shape, mybir.dt.from_np(v.dtype), kind="ExternalInput").ap()
         for name, v in given.items()}
    out = nc.dram_tensor("result", (1, S, D), F32, kind="ExternalOutput").ap()
    build(nc, a, out)
    r = run(nc, [arrays], core_ids=[0])
    return r.results[0]["result"]
```

```python
import math
from contextlib import ExitStack

import concourse.bass as bass
from concourse import mybir

ALU = mybir.AluOpType
ACT = mybir.ActivationFunctionType
AX = mybir.AxisListType
F32 = mybir.dt.float32
F32R = mybir.dt.float32r
I32 = mybir.dt.int32

P = 128
D = 1024
KD = D // P
S = 256
T = S // P
W = 512
KW = W // P
NT = 512
RAW = 6
SPL = 3
AHEAD = 2
FB = 256
F1 = 2816
F3 = 3584
E = 8
CONV_K = 31
PI = math.pi


PARAM_ROWS = [
    ("norm1_g", 16), ("norm2_g", 16), ("g_norm_2", 8), ("norm_mix_3", 16), ("norm_ffn_3", 16),
    ("subln_g", 2), ("dw_conv_b", 8), ("conv_ln_g", 8), ("conv_ln_b", 8), ("pool_scale_2", 4),
    ("lru_conv_b_3", 8), ("lru_ba_3", 8), ("lru_bx_3", 8), ("lru_lambda_3", 8), ("c", 8), ("c_2", 8),
    ("conv_w_3", 24), ("lru_conv_w_3", 32), ("dw_conv_w", 248),
]


COL = {}
for _name, _rows in PARAM_ROWS:
    COL[_name] = sum(COL_ROWS for _, COL_ROWS in PARAM_ROWS[:len(COL)])
PARAM_TILES = -(-sum(_rows for _, _rows in PARAM_ROWS) // P)


def shape_constants():
    import numpy as np
    ident = np.eye(P, dtype=np.float32)
    rot = np.zeros((P, P), np.float32)
    for b in (0, 64):
        for d in range(8):
            rot[b + d + 8, b + d] = -1.0
            rot[b + d, b + d + 8] = 1.0
    tri = np.where(np.arange(P)[:, None] >= np.arange(P)[None, :], 0.0, -3.0e38).astype(np.float32)
    before = (np.arange(P)[:, None] < np.arange(P)[None, :]).astype(np.float32)
    iota = np.broadcast_to(np.arange(P, dtype=np.float32), (P, P))
    freq = np.zeros((P, 2), np.float32)
    e = np.arange(0, 16, 2, dtype=np.float32) / np.float32(16)
    f1 = (np.float32(1.0) / np.power(np.float32(500000.0), e)).astype(np.float32)
    f2 = np.power(np.float32(500000.0), -e).astype(np.float32)
    for p in range(P):
        if p % 64 < 16:
            freq[p, 0], freq[p, 1] = f1[p % 8], f2[p % 8]
    misc = np.zeros((P, P), np.float32)
    misc[:, 0:2] = freq
    square = np.stack([ident, rot, tri, before, iota, misc], 1).reshape(P, 6 * P)
    t = np.arange(S, dtype=np.float32)
    row = [1.0 / np.minimum(t + 1, w) for w in (2, 4, 8, 16)] + [t]
    return np.ascontiguousarray(square), np.ascontiguousarray(np.stack(row).astype(np.float32))


class Plan:

    def __init__(self):
        self.chunks = []
        self.jobs = {}
        self.order = []
        self.count = {"act": 0, "dve": 0}
        self.splits = {}

    def job(self, name, evac, sources=()):
        self.count[evac] += 1
        n = len(self.order)
        self.jobs[name] = (n, len(self.chunks), len(sources), evac, self.count[evac])
        self.order.append(name)
        self.chunks += sources

    def split(self, name):
        self.splits[name] = len(self.splits) + 1

    def before(self, name):
        n = self.jobs[name][0]
        return self.jobs[self.order[n - 3]][3:5] if n >= 3 else None


def tiles(w):
    return w.rearrange("(c p) n -> p c n", p=P)


def halves(src, width):
    rows = src.shape[1]
    h = rows // 2
    return [(slice(0, h * width), src[:, 0:h, :]), (slice(h * width, 2 * h * width), src[:, h:rows, :])]


def column_chunks(w, n0, rows=KD, r0=0):
    t = tiles(w)
    return [halves(t[:, k:k + 4, n0:n0 + NT], NT) for k in range(r0, r0 + rows, 4)]


def build(nc, a, out):
    plan = Plan()
    at3 = {}
    counts_at = {}
    n_norm = [0]

    def plan_norm():
        n = n_norm[0]
        n_norm[0] += 1
        plan.job(f"norm{n}.0", "dve")
        plan.job(f"norm{n}.1", "dve")
        plan.split(f"norm{n}.0")
        plan.split(f"norm{n}.1")

    def plan_linear(name, w, cols, evac, n0=0, rows=KD):
        for j in range(cols // NT):
            plan.job(f"{name}.{j}" if cols > NT else name, evac, column_chunks(w, n0 + j * NT, rows))

    def plan_mod(k, w, slices):
        for j in range(slices):
            plan.job(f"mod{k}.{j}", "act", column_chunks(w, j * D) + column_chunks(w, j * D + NT))
            if j in (2, 5):
                plan.job(f"gate{k}.{j}", "dve")

    def plan_rotate(k):
        for part in ("rotq", "rotk"):
            plan.job(f"{part}{k}", "dve")

    def plan_scores(k):
        for q in ("score0", "score1a", "score1b"):
            plan.job(f"{q}.{k}", "act")

    def plan_apply(k):
        for j in range(3 if k == 2 else 2):
            plan.job(f"turn{k}.{j}", "act")
        plan.job(f"pv{k}", "act")

    def ffn_sources(gate, up, down, steps):
        def gu(s, k):
            return [(slice(0, 1024), tiles(gate)[:, k:k + 4, s * FB:(s + 1) * FB]),
                    (slice(1024, 2048), tiles(up)[:, k:k + 4, s * FB:(s + 1) * FB])]

        def dn(s):
            return halves(tiles(down)[:, 2 * s:2 * s + 2, :], D)
        res = [gu(0, 0), gu(0, 4)]
        for s in range(steps - 1):
            res += [gu(s + 1, 0), gu(s + 1, 4), dn(s)]
        return res + [dn(steps - 1)]

    def plan_ffn(k, gate, up, down, steps):
        at3[k] = len(plan.chunks)
        counts_at[k] = dict(plan.count)
        plan.chunks += ffn_sources(gate, up, down, steps)

    for l in range(2):
        plan_mod(l, a["ada_w"][l], 6)
        plan_norm()
        w = a["w_in"][l]
        plan_linear(f"ga{l}", w, 512, "act", 1536)
        plan_linear(f"gb{l}", w, 512, "act", 2048)
        plan_linear(f"q{l}", w, 512, "act", 0)
        plan_linear(f"k{l}", w, 512, "act", 512)
        plan_rotate(l)
        plan_linear(f"v{l}", w, 512, "act", 1024)
        plan_scores(l)
        plan_linear(f"gates{l}.0", w, NT, "act", 2560)
        plan_linear(f"gates{l}.1", w, NT, "act", 2560 + NT)
        plan_apply(l)
        plan_linear(f"gates{l}.2", w, NT, "act", 2560 + 2 * NT)
        plan.job(f"subln{l}", "dve")
        plan_linear(f"gates{l}.3", w, NT, "act", 2560 + 3 * NT)
        plan.split(f"attn{l}")
        plan.job(f"lnmean{l}", "dve")
        plan_linear(f"yattn{l}.0", a["w_attn_o"][l], NT, "dve", rows=KW)
        plan.job(f"lnvar{l}", "dve")
        plan_linear(f"yattn{l}.1", a["w_attn_o"][l], NT, "dve", NT, rows=KW)
        plan.split(f"conv{l}")
        plan_linear(f"yconv{l}", a["w_conv_o"][l], 1024, "dve", rows=KW)
        plan.job(f"mix{l}.0", "act")
        plan.job(f"mix{l}.1", "act")
        plan.split(f"mix{l}.0")
        plan.split(f"mix{l}.1")
        plan_linear(f"wout{l}", a["w_out"][l], 1024, "dve")
        plan_norm()
        wf = a["w_ffn_in"][l]
        plan_ffn(l, wf[:, 0:F1], wf[:, F1:2 * F1], a["w_ffn_out"][l], F1 // FB)
    plan_mod(2, a["w_ada_2"][0], 3)
    plan_norm()
    w = a["w_in_2"][0]
    plan_linear("up", w, 512, "act", 0)
    plan_linear("zp", w, 512, "act", 512)
    plan_linear("q2", w, 512, "act", 1024)
    plan_linear("k2", w, 512, "act", 1536)
    plan_rotate(2)
    plan_linear("v2", w, 512, "act", 2048)
    for j in range(4):
        plan_linear(f"gates2.{j}", w, NT, "act", 3072 + j * NT)
    plan_linear("za", w, 512, "act", 2560)
    plan.job("pool", "dve")
    plan.split("conv2")
    plan_linear("yconv2", a["w_pool_up_2"][0], 1024, "dve", rows=KW)
    plan_scores(2)
    plan_apply(2)
    plan.split("attn2")
    plan_linear("yattn2", a["w_attn_up_2"][0], 1024, "dve", rows=KW)
    plan.job("mix2.0", "act")
    plan.job("mix2.1", "act")
    plan.split("mix2.0")
    plan.split("mix2.1")
    plan_linear("wout2", a["w_out_2"][0], 1024, "dve")
    for l in range(2):
        plan_norm()
        w = a["w_in_3"][l]
        for j, name in enumerate(("cg", "bg", "vv", "uu", "gg")):
            plan_linear(f"{name}{l}", w, 512, "dve" if name == "vv" else "act", j * 512)
        plan.job(f"lrur{l}", "act")
        plan.job(f"lrui{l}", "act")
        plan.split(f"lru{l}.0")
        plan.split(f"lru{l}.1")
        plan_linear(f"wout{3 + l}", a["w_out_3"][l], 1024, "dve")
        plan_norm()
        if l == 0:
            plan_ffn(2, a["ffn_w_gate_3"][0], a["ffn_w_up_3"][0], a["ffn_w_down_3"][0], F3 // FB)
    MOE0 = len(plan.chunks)
    STEPS3 = F3 // FB
    PER = 3 * STEPS3
    assert PER % RAW == 0 and PER % SPL == 0

    ctx = ExitStack()
    with ctx:
        def sb(name, shape, dt=F32):
            return ctx.enter_context(nc.sbuf_tensor(name, shape, dt))

        sems = {}

        def sem(name):
            if name not in sems:
                sems[name] = ctx.enter_context(nc.semaphore(name))
            return sems[name]

        raw = sb("raw", [P, RAW, 2048])
        head = sb("head", [P, SPL, 2048], F32R)
        rest = sb("rest", [P, SPL, 2048], F32R)
        x = sb("x", [P, T, D])
        xn = sb("xn", [P, T, D])
        hT = sb("hT", [P, KD, S])
        hTh = sb("hTh", [P, KD, S], F32R)
        hTl = sb("hTl", [P, KD, S], F32R)
        cst = sb("cst", [P, 6, P])
        ident, rot, tri, before, iota = (cst[:, i, :] for i in range(5))
        freq = cst[:, 5, 0:2]
        ones = sb("ones", [P, P])
        prm = sb("prm", [P, PARAM_TILES * P])
        trig = sb("trig", [P, 2, S])
        gbc = sb("gbc", [P, 2, D])
        aTh = sb("aTh", [P, 2, S], F32R)
        aTl = sb("aTl", [P, 2, S], F32R)
        qkv = sb("qkv", [P, 3, 1024])
        gat = sb("gat", [P, T, 2048])
        upad = sb("upad", [P, KW, 30 + S])
        aw = sb("aw", [P, 3072])
        oT = sb("oT", [P, KW, S])
        sm = sb("sm", [P, 288])
        cHL = sb("cHL", [P, 2 * KD + 64], F32R)
        pair = [ctx.enter_context(nc.psum_tensor(f"pair{i}", [P, 2, 512], F32)) for i in range(3)]
        tb = [ctx.enter_context(nc.psum_tensor(f"tb{i}", [P, 512], F32)) for i in range(2)]

        qT = qkv[:, 0, :].rearrange("p (g s) -> p g s", s=S)
        kT = qkv[:, 1, :].rearrange("p (g s) -> p g s", s=S)
        vt = qkv[:, 2, :].rearrange("p (t n) -> p t n", t=T)
        conv = aw[:, 2048:3072].rearrange("p (g s) -> p g s", s=S)
        modrow = gat[0:3, 1, 0:1024]
        gateA, gateB = gat[:, :, 0:D], gat[:, :, D:2 * D]
        sg = qkv[:, 0, 0:512].rearrange("p (t f) -> p t f", t=T)
        act_ = qkv[:, 1, 0:512].rearrange("p (t f) -> p t f", t=T)
        ss, rstd = sm[:, 0:2], sm[:, 2:4]
        gs, sh = sm[:, 8:24], sm[:, 24:40]
        lamc = sm[:, 40:44]
        mx, su = sm[:, 228:244], sm[:, 244:260]
        rs = sm[:, 260:276]
        cact = sm[:, 72:80]
        sub = sm[:, 80:81]
        sp8 = sm[:, 276:284]
        tmp8 = sm[:, 88:120]
        lam4 = sm[0:1, 120:124]
        pos = sm[:, 128:144].rearrange("p (t e) -> p t e", t=T)
        comb = sm[:, 144:160].rearrange("p (t e) -> p t e", t=T)
        sel = sm[:, 160:176].rearrange("p (t e) -> p t e", t=T)
        lg = sm[:, 192:208].rearrange("p (t e) -> p t e", t=T)
        w8 = sm[:, 176:192].rearrange("p (t e) -> p t e", t=T)
        o8 = sm[:, 208:224].rearrange("p (t e) -> p t e", t=T)
        m2 = sm[:, 224:226]
        m1 = sm[:, 226:228]
        wins = sb("wins", [1, 1], I32)
        posi = aw[:, 0:S].bitcast(I32)


        class Ops:

            def __init__(self, eng, name):
                self.eng, self.sem, self.n = eng, sem(name), 0

            def did(self, ins):
                self.n += 1
                ins.then_inc(self.sem, 1)

            def now(self):
                self.eng.wait_ge(self.sem, self.n)

        class At:

            def __init__(self, k, turn=0, per=0):
                self.k, self.turn, self.per = k, turn, per
                self.raw, self.split = k % RAW, k % SPL

            def next(self, d=1):
                return At(self.k + d, self.turn, self.per)

            def count(self, d=0):
                return self.turn * self.per + (self.k + 1 + d)

            def landed(self):
                return self.turn * (32 * self.per // RAW) + 32 * (self.k // RAW + 1)

        def wait(eng, s, value):
            if not (isinstance(value, int) and value <= 0):
                eng.wait_ge(s, value)

        landed = [sem(f"chunk_landed{i}") for i in range(RAW)]
        heads_done, rests_done, chunk_used = sem("heads_done"), sem("rests_done"), sem("chunk_used")
        job_done, evac = sem("job_done"), {"act": sem("evac_act"), "dve": sem("evac_dve")}
        hth_ready, htl_ready = sem("hth_ready"), sem("htl_ready")
        act_ready, turned = sem("act_ready"), sem("act_turned")
        ath_ready, atl_ready = sem("ath_ready"), sem("atl_ready")

        def pcol(name, i=0, n=1):
            return prm[:, COL[name] + i:COL[name] + i + n]

        def col8(name, l):
            return pcol(name, 8 * l, 8)

        def jobs_done(name):
            n = plan.jobs[name][0]
            return sum(1 for m in plan.order[:n + 1] if not plan.jobs[m][2])

        def last_chunk(name):
            return plan.jobs[name][1] + plan.jobs[name][2] - 1

        def bank(name):
            return pair[plan.jobs[name][0] % 3]

        def flat4(t):
            return t[:, :, :].rearrange("p b (h s) -> p (b h) s", s=S)

        def over(ap, shape, axis):
            return ap.unsqueeze(axis).to_broadcast(shape)

        DENSE = [(0, F1 // FB), (1, F1 // FB), (2, F3 // FB)]
        STEP0 = {0: 0, 1: F1 // FB, 2: 2 * (F1 // FB), 3: 2 * (F1 // FB) + F3 // FB}
        POOLBUF = (oT, aw[:, 0:1024].rearrange("p (g s) -> p g s", s=S))
        tap = aw[:, 1536:2048].rearrange("p (g s) -> p g s", s=S)
        dpool = aw[:, 1024:2048].rearrange("p (g s) -> p g s", s=S)
        invcnt = aw[:, 2048:3072].rearrange("p (g s) -> p g s", s=S)
        wgrp = gbc[:, 1, 0:512].rearrange("p (g s) -> p g s", s=P)
        wbd = gbc[:, 0, :].rearrange("p (a g n) -> p a g n", a=2, g=KW)
        wrt = oT[:, 0, 0:64].rearrange("p (k e) -> p k e", e=E)
        sc0 = hT[:, 0:4, :].rearrange("p k s -> p (k s)").rearrange("p (m s) -> p m s", s=P)
        sc1 = xn[:, :, :].rearrange("p t n -> p (t n)").rearrange("p (m s) -> p m s", s=S)
        aT = aw[:, :].rearrange("p (c n) -> p c n", n=512)
        G = gat[:, :, :].rearrange("p t n -> p (t n)")
        upu = G[:, 0:KW * (3 + S)].rearrange("p (g s) -> p g s", s=3 + S)
        lru_a = G[:, 1036:2060].rearrange("p (g s) -> p g s", s=S)
        aw4 = [aw[:, i * 1024:(i + 1) * 1024].rearrange("p (g s) -> p g s", s=S) for i in range(3)]
        kq = [qkv[:, i, :].rearrange("p (g s) -> p g s", s=S) for i in range(3)]
        praw = aw[:, 1024:1024 + PARAM_TILES * P].rearrange("p (c n) -> p c n", n=P)
        lamrow = xn[0:1, 0, 0:512].rearrange("p (a l n) -> p a l n", a=4, l=2)
        angle = aw[:, S:2 * S]
        ptok = aw[:, 0:256].rearrange("p (t n) -> p t n", t=T)
        pcomb = aw[:, 256:512].rearrange("p (t n) -> p t n", t=T)
        pslot = aw[:, 512:768]
        ysb = aw[:, 1024:2048]
        xe = G[:, 0:1024].rearrange("p (k s) -> p k s", s=P)
        PADS = 30
        lam_init = [0.8 - 0.6 * math.exp(-0.3 * l) for l in range(2)]
        mods = [(0, 6, 0), (1, 6, 6), (2, 3, 12)]

        block = ctx.enter_context(nc.Block())

        @block.sync
        def _(sp):
            sp.dma_start(praw, a["params"].rearrange("(c p) n -> p c n", p=P)).then_inc(sem("params_landed"), 16)
            sp.dma_start(cst[:, :, :], a["square"].rearrange("p (c n) -> p c n", n=P)).then_inc(sem("const_landed"), 16)

            def load(c, parts):
                wait(sp, rests_done, c.count(-RAW))
                for part, src in parts:
                    dst = raw[:, c.raw, part]
                    if len(src.shape) == 3:
                        dst = dst.rearrange("p (k n) -> p k n", n=src.shape[2])
                    sp.dma_start(dst, src).then_inc(landed[c.raw], 16)

            def load_ffn_loop(k, gate, up, down, steps):
                g, u, d = tiles(gate), tiles(up), tiles(down)
                c0 = at3[k] + 5
                with sp.Fori(0, (steps - 2) // 2) as i:
                    for j in range(2):
                        s = 1 + j
                        cols = bass.ds(i * (2 * FB) + (s + 1) * FB, FB)
                        for r in range(2):
                            load(At(c0 + 3 * j + r, i, RAW), [(slice(0, 1024), g[:, 4 * r:4 * r + 4, cols]),
                                                             (slice(1024, 2048), u[:, 4 * r:4 * r + 4, cols])])
                        load(At(c0 + 3 * j + 2, i, RAW),
                             [(slice(0, D), d[:, bass.ds(i * 4 + 2 * s, 1), :]),
                              (slice(D, 2 * D), d[:, bass.ds(i * 4 + 2 * s + 1, 1), :])])
                return c0 + RAW * ((steps - 2) // 2)

            loops = {
                at3[0] + 5: (0, a["w_ffn_in"][0][:, 0:F1], a["w_ffn_in"][0][:, F1:2 * F1], a["w_ffn_out"][0], F1 // FB),
                at3[1] + 5: (1, a["w_ffn_in"][1][:, 0:F1], a["w_ffn_in"][1][:, F1:2 * F1], a["w_ffn_out"][1], F1 // FB),
                at3[2] + 5: (2, a["ffn_w_gate_3"][0], a["ffn_w_up_3"][0], a["ffn_w_down_3"][0], F3 // FB)}
            c = 0
            while c < MOE0:
                if c == RAW:
                    sp.dma_start(x[:, :, :], a["x"][0].rearrange("(t p) n -> p t n", p=P)).then_inc(sem("x_landed"), 16)
                if c in loops:
                    c = load_ffn_loop(*loops[c])
                else:
                    load(At(c), plan.chunks[c])
                    c += 1
            eg = a["moe_w_gate_3"][0].rearrange("e (c p) n -> p (e c) n", p=P)
            eu = a["moe_w_up_3"][0].rearrange("e (c p) n -> p (e c) n", p=P)
            ed = a["moe_w_down_3"][0].rearrange("e (c p) n -> p (e c) n", p=P)
            KF = F3 // P

            def load_expert(it, e):
                def gu(k, s, r):
                    cols = slice(s * FB, (s + 1) * FB)
                    load(At(MOE0 + k, it, PER), [(slice(0, 1024), eg[:, bass.ds(e * KD + 4 * r, 4), cols]),
                                                 (slice(1024, 2048), eu[:, bass.ds(e * KD + 4 * r, 4), cols])])

                def dn(k, s):
                    load(At(MOE0 + k, it, PER), [(slice(0, D), ed[:, bass.ds(e * KF + 2 * s, 1), :]),
                                                 (slice(D, 2 * D), ed[:, bass.ds(e * KF + 2 * s + 1, 1), :])])
                gu(0, 0, 0)
                gu(1, 0, 1)
                for s in range(STEPS3 - 1):
                    gu(2 + 3 * s, s + 1, 0)
                    gu(3 + 3 * s, s + 1, 1)
                    dn(4 + 3 * s, s)
                dn(PER - 1, STEPS3 - 1)

            with sp.Fori(0, E) as e:
                load_expert(e, e)
            sp.wait_ge(sem("windows_ready"), 1)
            more = sp.value_load(wins[0:1, 0:1], min_val=0, max_val=1)
            with sp.If(more):
                with sp.Fori(0, E) as e:
                    load_expert(e + E, e)
            for k in range(2):
                sp.wait_ge(rests_done, more * (E * PER) + (MOE0 + E * PER + k + 1 - RAW))
                for j in range(2):
                    sp.dma_start(raw[:, (MOE0 + k) % RAW, 8 * j:8 * j + 8], a["square"][:, 8 * j:8 * j + 8]).then_inc(landed[(MOE0 + k) % RAW], 16)

        @block.gpsimd
        def _(pool):
            own = Ops(pool, "pool_own")
            pool.memset(ones[:, :], 1.0).then_inc(sem("ones_ready"), 1)
            own.did(pool.memset(upad[:, :, :], 0.0))
            own.now()
            pool.sem_inc(sem("pads_zero"), 1)
            for i, name in enumerate(("lambda_q1", "lambda_k1", "lambda_q2", "lambda_k2")):
                pool.dma_start(lamrow[:, i, :, 0:64], a[name].unsqueeze(0)).then_inc(sem("lambdas_landed"), 16)
            pool.dma_start(posi, a["positions"][0:1, :].to_broadcast([P, S])).then_inc(sem("positions_landed"), 16)

            def bias_rows(k, slices, before_):
                src = a["ada_b"][k:k + 1, :] if k < 2 else a["b_ada_2"][0:1, :]
                for j in range(slices):
                    wait(pool, sem("modrow_used"), before_ + j)
                    pool.dma_start(modrow[2:3, :], src[:, j * D:(j + 1) * D]).then_inc(sem("bias_row"), 16)

            def conv_half(l):
                half = slice(KW // 2, KW)
                pool.wait_ge(sem("u_ready"), l + 1)
                for k in range(CONV_K):
                    w_ = pcol("dw_conv_w", 124 * l + 4 * k + KW // 2, KW // 2)
                    own.now()
                    own.did(pool.tensor_tensor(tap, upad[:, half, k:k + S], over(w_, [P, KW // 2, S], 2), ALU.mult))
                    own.now()
                    bias = over(pcol("dw_conv_b", 4 * l + KW // 2, KW // 2), [P, KW // 2, S], 2)
                    own.did(pool.tensor_tensor(conv[:, half, :], tap, bias if k == 0 else conv[:, half, :], ALU.add))
                own.now()
                pool.sem_inc(sem("conv_half_done"), 1)

            bias_rows(*mods[0])
            conv_half(0)
            pool.wait_ge(evac["dve"], plan.jobs["norm1.1"][4])
            bias_rows(*mods[1])
            conv_half(1)
            pool.wait_ge(evac["dve"], plan.jobs["norm3.1"][4])
            pool.dma_start(gbc[:, 0, :], a["final_g"].unsqueeze(0).to_broadcast([P, D])).then_inc(sem("final_g_landed"), 16)
            pool.wait_ge(sem("block_done"), 1)
            pool.dma_start(invcnt, a["rows"][0:4, :].unsqueeze(0).to_broadcast([P, 4, S])).then_inc(sem("pool_landed"), 16)
            pool.dma_start(angle, a["rows"][4:5, :].to_broadcast([P, S])).then_inc(sem("pool_landed"), 16)
            pool.dma_start(wgrp, a["w_pool_grp_2"][0].rearrange("g c d -> c g d")).then_inc(sem("pool_landed"), 16)
            bias_rows(*mods[2])
            pool.wait_ge(job_done, jobs_done("pool"))
            pool.dma_start(gbc[:, 1, :], a["g_final_2"].unsqueeze(0).to_broadcast([P, D])).then_inc(sem("final_g_landed"), 16)
            pool.wait_ge(sem("block_done"), 2)
            pool.dma_start(gbc[:, 1, :], a["norm_final_3"].unsqueeze(0).to_broadcast([P, D])).then_inc(sem("final_g_landed"), 16)
            own.did(pool.memset(gbc[:, 0, :], 0.0))
            own.now()
            for l in range(2):
                if l == 1:
                    pool.wait_ge(job_done, jobs_done("lrui0"))
                for i, name in enumerate(("lru_wa_3", "lru_wx_3")):
                    src = a[name][l].rearrange("(g h) i j -> h i g j", h=2)
                    for h in range(2):
                        pool.dma_start(wbd[64 * h:64 * h + 64, i, :, 64 * h:64 * h + 64], src[h]).then_inc(sem("lru_landed"), 16)
            pool.wait_ge(evac["dve"], plan.jobs["norm8.1"][4])
            pool.dma_start(wrt, a["w_router_3"][0].rearrange("(k p) e -> p k e", p=P)).then_inc(sem("router_landed"), 16)
            pool.wait_ge(sem("block_done"), 3)
            pool.dma_start(out[0].rearrange("(t p) n -> p t n", p=P), xn[:, :, :]).then_inc(sem("out_stored"), 16)
            pool.wait_ge(sem("out_stored"), 16)

        @block.scalar
        def _(act):
            own = Ops(act, "act_own")
            fed = [0]

            def make_head(c):
                act.wait_ge(landed[c.raw], c.landed())
                wait(act, chunk_used, c.count(-SPL))
                act.activation(head[:, c.split, :], raw[:, c.raw, :], ACT.Copy).then_inc(heads_done, 1)

            def feed(upto):
                while fed[0] < min(upto, MOE0 + 2):
                    make_head(At(fed[0]))
                    fed[0] += 1

            def job(name):
                feed(last_chunk(name) + 1 + AHEAD)
                act.wait_ge(chunk_used, last_chunk(name) + 1)
                return bank(name)

            def split(name, lo, hi, ready=None):
                act.wait_ge(sem("hT_ready"), plan.splits[name])
                act.activation(hTh[:, lo:hi, :], hT[:, lo:hi, :], ACT.Copy).then_inc(hth_ready, 1)

            def sqrt_rows(n):
                act.wait_ge(sem("x_ready"), n)
                act.activation(xn[:, 1, :], x[:, 1, :], ACT.Square, accum_out=ss[:, 1:2]).then_inc(sem("tile1_squared"), 1)
                act.wait_ge(sem("mean_square"), n)
                act.activation(rstd, ss, ACT.Sqrt).then_inc(sem("root"), 1)

            def norm(n):
                act.wait_ge(sem("rstd_ready"), n + 1)
                act.activation(xn[:, 1, :], x[:, 1, :], ACT.Copy, scale=rstd[:, 1:2]).then_inc(sem("xn_ready"), 1)
                for j in range(2):
                    split(f"norm{n}.{j}", 4 * j, 4 * j + 4)

            def sines(k):
                act.wait_ge(sem("angles_ready"), k + 1)
                act.activation(trig[:, 1, :], aw[:, 2 * S:3 * S], ACT.Sin)
                act.activation(trig[:, 0, :], aw[:, 3 * S:4 * S], ACT.Sin).then_inc(sem("trig_ready"), 1)

            def condition(k):
                act.wait_ge(sem("cond_ready"), k // 2 + 1)
                if k == 0:
                    own.did(act.activation(cact, pcol("c", 0, 8), ACT.Silu))
                    own.now()
                act.activation(cHL[:, 0:2 * KD:2], cact if k == 0 else pcol("c_2", 0, 8), ACT.Copy).then_inc(sem("cond_head"), 1)

            def mod(k, slices, before_):
                if k == 2:
                    condition(2)
                for j in range(slices):
                    ps = job(f"mod{k}.{j}")
                    wait(act, sem("modrow_used"), before_ + j)
                    act.activation(modrow[0:2, :].rearrange("p (b n) -> p b n", b=2), ps[0:2, :, :], ACT.Copy).then_inc(evac["act"], 1)

            def copy_job(name, dst, func=ACT.Copy, turn=True, scale=1.0):
                ps = job(name)
                act.activation(dst, flat4(ps) if turn else ps[:, :, :], func, scale=scale).then_inc(evac["act"], 1)

            def score_exps(k):
                act.wait_ge(job_done, jobs_done(f"score0.{k}"))
                act.activation(sc0, bank(f"score0.{k}")[:, :, :].rearrange("p r (g n) -> p (r g) n", n=P), ACT.Copy,
                               scale=0.125).then_inc(evac["act"], 1)
                for h, part in enumerate("ab"):
                    name = f"score1{part}.{k}"
                    act.wait_ge(job_done, jobs_done(name))
                    dst = sc1.rearrange("p (r g) s -> p r g s", r=2)[:, :, 2 * h:2 * h + 2, :]
                    act.activation(dst, bank(name)[:, :, :].rearrange("p r (g s) -> p r g s", s=S), ACT.Copy,
                                   scale=0.125).then_inc(evac["act"], 1)
                for q, sc in enumerate((sc0, sc1)):
                    act.wait_ge(sem("max_ready"), 2 * k + q + 1)
                    for m in range(8):
                        ins = act.activation(sc[:, m, :], sc[:, m, :], ACT.Exp, bias=mx[:, 8 * q + m:8 * q + m + 1],
                                             accum_out=su[:, 8 * q + m:8 * q + m + 1])
                    ins.then_inc(sem("exp_ready"), 1)

            def apply_scores(k):
                for j in range(2 if k < 2 else 3):
                    act.wait_ge(job_done, jobs_done(f"turn{k}.{j}"))
                    n = 1 if k < 2 and j == 1 else 2
                    act.activation(aT[:, 2 * j:2 * j + n, :], bank(f"turn{k}.{j}")[:, 0:n, :], ACT.Copy).then_inc(evac["act"], 1)
                act.wait_ge(job_done, jobs_done(f"pv{k}"))
                act.activation(oT[:, :, :], flat4(bank(f"pv{k}")), ACT.Copy).then_inc(evac["act"], 1)

            def mix(k):
                for j in range(2):
                    act.wait_ge(job_done, jobs_done(f"mix{k}.{j}"))
                    act.activation(hT[:, 4 * j:4 * j + 4, :], flat4(bank(f"mix{k}.{j}")), ACT.Copy).then_inc(evac["act"], 1)
                    act.wait_ge(evac["act"], plan.jobs[f"mix{k}.{j}"][4])
                    act.activation(hTh[:, 4 * j:4 * j + 4, :], hT[:, 4 * j:4 * j + 4, :], ACT.Copy).then_inc(hth_ready, 1)

            def silu_gate(c, s, nt, b=0):
                act.wait_ge(chunk_used, c.count())
                src = pair[0][:, 0:T, 0:FB] if nt == T else pair[0][:, b:b + 1, 0:FB]
                act.activation(sg[:, 0:nt, :], src, ACT.Silu).then_inc(sem("silu_ready"), 1)

            def turned_head(s, nt):
                act.wait_ge(turned, s + 1)
                act.activation(aTh[:, :, 0:nt * P], tb[0][:, :].rearrange("p (k s) -> p k s", k=2)[:, :, 0:nt * P],
                               ACT.Copy).then_inc(ath_ready, 1)

            def ffn_step(c, s, nt, b=0):
                make_head(c.next(2))
                turned_head(s, nt)
                make_head(c.next(3))
                make_head(c.next(4))
                silu_gate(c.next(1), s + 1, nt, b)

            def ffn(k, steps):
                c0, s0 = at3[k], STEP0[k]
                feed(c0 + 2 + AHEAD)
                silu_gate(At(c0 + 1), s0, T)
                ffn_step(At(c0 + 2), s0, T)
                with act.Fori(0, (steps - 2) // 2) as i:
                    for j in range(2):
                        ffn_step(At(c0 + 5 + 3 * j, i, RAW), i * 2 + (s0 + 1 + j), T)
                done = 1 + 2 * ((steps - 2) // 2)
                for s in range(done, steps - 1):
                    ffn_step(At(c0 + 2 + 3 * s), s0 + s, T)
                fed[0] = c0 + 2 + 3 * (steps - 1) + AHEAD
                turned_head(s0 + steps - 1, T)

            def gate_job(k, j):
                copy_job(f"gates{k}.{j}", gat[:, :, j * NT:(j + 1) * NT], ACT.Sigmoid, turn=False)

            condition(0)
            feed(SPL)
            act.wait_ge(sem("lam_dots"), 1)
            act.activation(lam4, lam4, ACT.Exp).then_inc(sem("lam_exp"), 1)
            act.wait_ge(sem("lru_decay_in"), 1)
            act.activation(tmp8[:, 8:16], tmp8[:, 0:8], ACT.Exp, scale=-1.0).then_inc(sem("lru_decay_exp"), 1)
            feed(2 * SPL)
            sines(0)
            nn = 0
            for l in range(2):
                mod(*mods[l])
                sqrt_rows(nn + 1)
                norm(nn)
                nn += 1
                act.wait_ge(sem("pads_zero"), 1)
                copy_job(f"ga{l}", upad[:, :, PADS:PADS + S])
                copy_job(f"gb{l}", oT[:, :, :], ACT.Sigmoid)
                copy_job(f"q{l}", qT)
                copy_job(f"k{l}", kT)
                copy_job(f"v{l}", vt, turn=False)
                score_exps(l)
                gate_job(l, 0)
                gate_job(l, 1)
                apply_scores(l)
                gate_job(l, 2)
                act.wait_ge(sem("sub_var"), l + 1)
                act.activation(kq[1], kq[1], ACT.Sqrt).then_inc(sem("sub_root"), 1)
                job(f"gates{l}.3")
                split(f"attn{l}", 0, 4)
                gate_job(l, 3)
                feed(last_chunk(f"yattn{l}.0") + 1 + AHEAD)
                act.wait_ge(sem("ln_var"), l + 1)
                act.activation(kq[1][:, 0, :], kq[1][:, 0, :], ACT.Sqrt).then_inc(sem("ln_root"), 1)
                act.wait_ge(sem("ln_ready"), l + 1)
                for g in range(KW):
                    own.did(act.activation(hT[:, 4 + g, :], conv[:, g, :], ACT.Silu,
                                           scale=pcol("conv_ln_g", 4 * l + g), bias=pcol("conv_ln_b", 4 * l + g)))
                own.now()
                act.activation(hTh[:, 4:8, :], hT[:, 4:8, :], ACT.Copy).then_inc(hth_ready, 1)
                feed(last_chunk(f"yattn{l}.1") + 1 + AHEAD)
                feed(last_chunk(f"yconv{l}.0") + 1 + AHEAD)
                feed(last_chunk(f"yconv{l}.1") + 1 + AHEAD)
                mix(l)
                feed(last_chunk(f"wout{l}.0") + 1 + AHEAD)
                feed(last_chunk(f"wout{l}.1") + 1 + AHEAD)
                sqrt_rows(nn + 1)
                norm(nn)
                nn += 1
                ffn(*DENSE[l])
            roots = nn + 1
            sqrt_rows(roots)
            sines(1)
            mod(*mods[2])
            roots += 1
            sqrt_rows(roots)
            norm(nn)
            nn += 1
            copy_job("up", upad[:, :, PADS:PADS + S])
            copy_job("zp", xn[:, 0, :].rearrange("p (g s) -> p g s", s=S), ACT.Silu)
            copy_job("q2", qT)
            copy_job("k2", kT)
            copy_job("v2", vt, turn=False)
            for j in range(4):
                gate_job(2, j)
            act.wait_ge(sem("pool_ready"), 1)
            copy_job("za", upad[:, :, PADS:PADS + S], ACT.Silu)
            split("conv2", 4, 8)
            feed(last_chunk("yconv2.1") + 1 + AHEAD)
            score_exps(2)
            apply_scores(2)
            split("attn2", 0, 4)
            feed(last_chunk("yattn2.1") + 1 + AHEAD)
            mix(2)
            feed(last_chunk("wout2.1") + 1 + AHEAD)
            roots += 1
            sqrt_rows(roots)
            for l in range(2):
                roots += 1
                sqrt_rows(roots)
                norm(nn)
                nn += 1
                copy_job(f"cg{l}", kq[0])
                copy_job(f"bg{l}", kq[1])
                feed(last_chunk(f"vv{l}") + 1 + AHEAD)
                act.wait_ge(sem("upu_zero"), 1)
                copy_job(f"uu{l}", upu[:, :, 3:3 + S])
                copy_job(f"gg{l}", kq[2], ACT.Gelu_apprx_tanh)
                for i, (name, bias) in enumerate((("lrur", "lru_ba_3"), ("lrui", "lru_bx_3"))):
                    act.wait_ge(job_done, jobs_done(f"{name}{l}"))
                    for g in range(KW):
                        ins = act.activation(aw4[i][:, g, :], flat4(bank(f"{name}{l}"))[:, g, :], ACT.Sigmoid,
                                             bias=pcol(bias, 4 * l + g))
                    ins.then_inc(evac["act"], 1)
                act.wait_ge(sem("ya_read"), l + 1)
                act.wait_ge(evac["act"], plan.jobs[f"lrur{l}"][4])
                for func, dst, done in ((ACT.Exp, lru_a, "lru_exp"), (ACT.Tanh, aw4[2], "lru_tanh")):
                    for g in range(KW):
                        ins = act.activation(dst[:, g, :], aw4[0][:, g, :], func, scale=sp8[:, 4 * l + g:4 * l + g + 1])
                    ins.then_inc(sem(done), 1)
                split(f"lru{l}.0", 0, 4)
                act.wait_ge(sem("b_square"), l + 1)
                act.activation(aw4[2], aw4[2], ACT.Sqrt, scale=-1.0).then_inc(sem("b_root"), 1)
                split(f"lru{l}.1", 4, 8)
                feed(last_chunk(f"wout{3 + l}.1") + 1 + AHEAD)
                roots += 1
                sqrt_rows(roots)
                norm(nn)
                nn += 1
                if l == 0:
                    ffn(*DENSE[2])
            act.wait_ge(sem("gap_ready"), 1)
            act.activation(m2, m2, ACT.Exp).then_inc(sem("gap_exp"), 1)
            feed(MOE0 + 2)

            def gathered_head(count):
                act.wait_ge(sem("gathered"), count)
                act.activation(hTh[:, :, 0:P], xe, ACT.Copy).then_inc(sem("xe_head"), 1)

            def expert(it, window):
                s0 = it * STEPS3 + STEP0[3]
                at = At(MOE0, it, PER)
                make_head(at.next(2))
                make_head(at.next(3))
                act.wait_ge(sem("combine_turned"), it + 1)
                act.activation(pslot, tb[1][:, 0:256], ACT.Copy).then_inc(sem("combine_ready"), 1)
                silu_gate(at.next(1), s0, 1, 0)
                for s in range(STEPS3 - 1):
                    ffn_step(at.next(2 + 3 * s), s0 + s, 1, (s + 1) % 2)
                turned_head(s0 + (STEPS3 - 1), 1)
                make_head(at.next(PER + 1))
                gathered_head(it + (window + 2))
                act.wait_ge(chunk_used, at.next(PER - 1).count())
                act.activation(ysb.rearrange("p (b n) -> p b n", b=2), pair[1][:, :, :], ACT.Copy).then_inc(sem("y_ready"), 1)

            gathered_head(1)
            with act.Fori(0, E) as e:
                expert(e, 0)
            act.wait_ge(sem("windows_ready"), 1)
            more = act.value_load(wins[0:1, 0:1], min_val=0, max_val=1)
            with act.If(more):
                gathered_head(E + 2)
                with act.Fori(0, E) as e:
                    expert(e + E, 1)
            act.wait_ge(sem("last_mean_square"), 1)
            act.activation(rstd, ss, ACT.Sqrt).then_inc(sem("last_root"), 1)

        @block.vector
        def _(dve):
            own = Ops(dve, "dve_own")
            did, now = own.did, own.now
            fed = [0]
            roots = [0]

            def make_rest(c):
                dve.wait_ge(heads_done, c.count())
                dve.tensor_tensor(rest[:, c.split, :], raw[:, c.raw, :], head[:, c.split, :].bitcast(F32),
                                  ALU.subtract).then_inc(rests_done, 1)

            def feed(upto):
                while fed[0] < min(upto, MOE0 + 2):
                    make_rest(At(fed[0]))
                    fed[0] += 1

            def job(name):
                feed(last_chunk(name) + 1 + AHEAD)
                dve.wait_ge(chunk_used, last_chunk(name) + 1)
                return bank(name)

            def split_rest(name, lo, hi):
                dve.wait_ge(hth_ready, plan.splits[name])
                dve.tensor_tensor(hTl[:, lo:hi, :], hT[:, lo:hi, :], hTh[:, lo:hi, :].bitcast(F32),
                                  ALU.subtract).then_inc(htl_ready, 1)

            def rms(eps=1e-6):
                now()
                dve.sem_inc(sem("x_ready"), 1)
                did(dve.tensor_tensor_reduce(xn[:, 0, :], x[:, 0, :], x[:, 0, :], 1.0, 0.0, ALU.mult, ALU.add, ss[:, 0:1]))
                now()
                roots[0] += 1
                dve.wait_ge(sem("tile1_squared"), roots[0])
                dve.tensor_scalar(ss, ss, 1.0 / D, eps, ALU.mult, ALU.add).then_inc(sem("mean_square"), 1)
                dve.wait_ge(sem("root"), roots[0])
                did(dve.reciprocal(rstd, rstd))
                now()

            def norm(n, scale, shift=None):
                rms()
                dve.sem_inc(sem("rstd_ready"), 1)
                dve.tensor_scalar(xn[:, 0, :], x[:, 0, :], rstd[:, 0:1], None, ALU.mult).then_inc(sem("xn_ready"), 1)
                for j in range(2):
                    dve.wait_ge(job_done, jobs_done(f"norm{n}.{j}"))
                    ps = flat4(bank(f"norm{n}.{j}"))
                    for i in range(4):
                        k = 4 * j + i
                        if shift is None:
                            ins = dve.tensor_scalar(hT[:, k, :], ps[:, i, :], scale[:, k:k + 1], None, ALU.mult)
                        else:
                            ins = dve.tensor_scalar(hT[:, k, :], ps[:, i, :], scale[:, k:k + 1], shift[:, k:k + 1], ALU.mult, ALU.add)
                        if i < 3:
                            did(ins)
                    ins.then_inc(evac["dve"], 1)
                    dve.wait_ge(evac["dve"], plan.jobs[f"norm{n}.{j}"][4])
                    dve.sem_inc(sem("hT_ready"), 1)
                    split_rest(f"norm{n}.{j}", 4 * j, 4 * j + 4)

            def last_norm(src_row, dst):
                rms()
                dve.wait_ge(sem("final_g_landed"), 16 * (src_row[0] + 1))
                for t in range(T):
                    ins = dve.scalar_tensor_tensor(out=dst[:, t, :], in0=x[:, t, :], scalar=rstd[:, t:t + 1],
                                                   in1=gbc[:, src_row[1], :], op0=ALU.mult, op1=ALU.mult)
                ins.then_inc(sem("block_done"), 1)
                dve.wait_ge(sem("block_done"), src_row[0] + 1)

            def angles(k):
                r, c_, m, n_int = aw[:, 2 * S:3 * S], aw[:, 3 * S:4 * S], aw[:, 0:S], posi
                did(dve.tensor_scalar(r, angle, freq[:, k:k + 1], None, ALU.mult))
                now()
                did(dve.tensor_scalar(n_int, r, 1.0 / (2 * PI), None, ALU.mult))
                now()
                did(dve.tensor_copy(c_, n_int))
                now()
                for part in (6.28125, 2 * PI - 6.28125):
                    did(dve.scalar_tensor_tensor(out=r, in0=c_, scalar=-part, in1=r, op0=ALU.mult, op1=ALU.add))
                    now()

                def fold(v):
                    for cmp, lim, step in ((ALU.is_gt, PI, -2 * PI), (ALU.is_lt, -PI, 2 * PI)):
                        did(dve.tensor_scalar(m, v, lim, step, cmp, ALU.mult))
                        now()
                        did(dve.tensor_tensor(v, v, m, ALU.add))
                        now()
                    did(dve.tensor_scalar(v, v, 3.1415925, -3.1415925, ALU.min, ALU.max))
                    now()
                fold(r)
                did(dve.tensor_scalar(c_, r, PI / 2, None, ALU.add))
                now()
                fold(c_)
                dve.sem_inc(sem("angles_ready"), 1)

            def condition(k):
                now()
                dve.sem_inc(sem("cond_ready"), 1)
                dve.wait_ge(sem("cond_head"), k // 2 + 1)
                dve.tensor_tensor(cHL[:, 1:2 * KD:2], cact if k == 0 else pcol("c_2", 0, 8),
                                  cHL[:, 0:2 * KD:2].bitcast(F32), ALU.subtract).then_inc(sem("cond_split"), 1)

            def mod(k, slices, before_):
                if k == 2:
                    condition(2)
                for j in range(slices):
                    feed(last_chunk(f"mod{k}.{j}") + 1 + AHEAD)
                    if j in (2, 5):
                        dve.wait_ge(sem("modrow_used"), before_ + j + 1)
                        dve.tensor_scalar(gbc[:, j // 3, :], bank(f"gate{k}.{j}")[:, :, :].rearrange("p b n -> p (b n)"),
                                          1.0 if k < 2 else 0.0, None, ALU.add).then_inc(evac["dve"], 1)
                for i in range(slices // 3):
                    g = col8("norm1_g" if i == 0 else "norm2_g", k) if k < 2 else pcol("g_norm_2", 0, 8)
                    if i == 0:
                        dve.wait_ge(sem("modrow_used"), before_ + slices)
                    did(dve.tensor_copy(sh[:, 8 * i:8 * i + 8], tb[1][:, 24 * i:24 * i + 8]))
                    did(dve.scalar_tensor_tensor(out=gs[:, 8 * i:8 * i + 8], in0=tb[1][:, 24 * i + 8:24 * i + 16], scalar=1.0,
                                                 in1=g, op0=ALU.add, op1=ALU.mult))
                now()
                dve.sem_inc(sem("modcols_read"), 1)

            def conv_taps(l, ks):
                for k in ks:
                    now()
                    for g in range(KW // 2):
                        w_ = pcol("dw_conv_w", 124 * l + 4 * k + g)
                        if k == 0:
                            did(dve.tensor_scalar(conv[:, g, :], upad[:, g, 0:S], w_, pcol("dw_conv_b", 4 * l + g), ALU.mult, ALU.add))
                        else:
                            did(dve.scalar_tensor_tensor(out=conv[:, g, :], in0=upad[:, g, k:k + S], scalar=w_, in1=conv[:, g, :],
                                                         op0=ALU.mult, op1=ALU.add))

            def rope(k):
                tmp = aw4[0]
                dve.wait_ge(sem("trig_ready"), 1 if k < 2 else 2)
                for i, (name, buf) in enumerate((("rotq", qT), ("rotk", kT))):
                    dve.wait_ge(job_done, jobs_done(f"{name}{k}"))
                    dve.tensor_tensor(tmp, flat4(bank(f"{name}{k}")), over(trig[:, 1, :], [P, KW, S], 1), ALU.mult).then_inc(evac["dve"], 1)
                    did(dve.tensor_tensor(buf, buf, over(trig[:, 0, :], [P, KW, S], 1), ALU.mult))
                    now()
                    dve.wait_ge(evac["dve"], plan.jobs[f"{name}{k}"][4])
                    did(dve.tensor_tensor(buf, buf, tmp, ALU.add))
                    now()
                    dve.sem_inc(sem("roped"), 1)

            def mask_and_max(k, q):
                sc, L = (sc0, sc1)[q], P * (q + 1)
                dve.wait_ge(evac["act"], plan.jobs[f"score0.{k}" if q == 0 else f"score1b.{k}"][4])
                diag = sc[:, :, q * P:(q + 1) * P]
                did(dve.tensor_tensor(diag, diag, over(tri, [P, 8, P], 1), ALU.add))
                now()
                did(dve.tensor_reduce(mx[:, 8 * q:8 * q + 8], sc[:, :, 0:L], AX.X, ALU.max))
                now()
                dve.tensor_scalar(mx[:, 8 * q:8 * q + 8], mx[:, 8 * q:8 * q + 8], -1.0, None, ALU.mult).then_inc(sem("max_ready"), 1)

            def probs(k, q):
                sc = (sc0, sc1)[q]
                dve.wait_ge(sem("exp_ready"), 2 * k + q + 1)
                did(dve.reciprocal(rs[:, 0:8], su[:, 8 * q:8 * q + 8]))
                now()
                if k < 2:
                    did(dve.tensor_scalar(rs[:, 4:8], rs[:, 4:8], lamc[:, k:k + 1], None, ALU.mult))
                    now()
                for m in range(4 if k < 2 else 8):
                    did(dve.tensor_scalar(sc[:, m, :], sc[:, m, :], rs[:, m:m + 1], None, ALU.mult))
                now()
                if k < 2:
                    for h in range(4):
                        did(dve.scalar_tensor_tensor(out=sc[:, h, :], in0=sc[:, 4 + h, :], scalar=rs[:, 4 + h:5 + h], in1=sc[:, h, :],
                                                     op0=ALU.mult, op1=ALU.add))
                    now()
                dve.sem_inc(sem("probs_ready"), 1)

            def column_mean_job(name, buf, n, eps=None):
                dve.wait_ge(job_done, jobs_done(name))
                src = flat4(bank(name)) if len(buf.shape) == 3 else bank(name)[:, 0, 0:S]
                if eps is None:
                    dve.tensor_scalar(buf, src, 1.0 / n, None, ALU.mult).then_inc(evac["dve"], 1)
                else:
                    dve.tensor_scalar(buf, src, 1.0 / n, eps, ALU.mult, ALU.add).then_inc(evac["dve"], 1)
                dve.wait_ge(evac["dve"], plan.jobs[name][4])

            def gate_product(name, gate, halves_=(0, 1)):
                for j in halves_:
                    ps = job(f"{name}.{j}")
                    part = gate[:, :, j * NT:(j + 1) * NT]
                    dve.tensor_tensor(part, part, ps[:, :, :], ALU.mult).then_inc(evac["dve"], 1)

            def merge(k, last, gate):
                for j in range(2):
                    gate_product(f"{last}{k}", gate, (j,))
                    dve.wait_ge(evac["dve"], plan.jobs[f"{last}{k}.{j}"][4])
                    part = slice(j * NT, (j + 1) * NT)
                    dve.tensor_tensor(gateA[:, :, part], gateA[:, :, part], gateB[:, :, part], ALU.add).then_inc(sem("merged"), 1)
                for j in range(2):
                    split_rest(f"mix{k}.{j}", 4 * j, 4 * j + 4)

            def add_product(name, gate):
                for j in range(2):
                    ps = job(f"{name}.{j}")
                    part = x[:, :, j * NT:(j + 1) * NT]
                    if gate is None:
                        dve.tensor_tensor(part, part, ps[:, :, :], ALU.add).then_inc(evac["dve"], 1)
                    else:
                        tmp = gateB[:, :, j * NT:(j + 1) * NT]
                        dve.tensor_tensor(tmp, ps[:, :, :], over(gate[:, j * NT:(j + 1) * NT], [P, T, NT], 1),
                                          ALU.mult).then_inc(evac["dve"], 1)
                        dve.wait_ge(evac["dve"], plan.jobs[f"{name}.{j}"][4])
                        did(dve.tensor_tensor(part, part, tmp, ALU.add))
                dve.wait_ge(evac["dve"], plan.jobs[f"{name}.1"][4])

            def gated_hidden(s, nt, b=0):
                dve.wait_ge(sem("silu_ready"), s + 1)
                up = pair[0][:, 0:T, FB:2 * FB] if nt == T else pair[0][:, b:b + 1, FB:2 * FB]
                dve.tensor_tensor(act_[:, 0:nt, :], sg[:, 0:nt, :], up, ALU.mult).then_inc(act_ready, 1)

            def turned_rest(s, nt):
                dve.wait_ge(ath_ready, s + 1)
                dve.tensor_tensor(aTl[:, :, 0:nt * P], tb[0][:, :].rearrange("p (k s) -> p k s", k=2)[:, :, 0:nt * P],
                                  aTh[:, :, 0:nt * P].bitcast(F32), ALU.subtract).then_inc(atl_ready, 1)

            def ffn_step(c, s, nt, b=0):
                make_rest(c.next(2))
                turned_rest(s, nt)
                make_rest(c.next(3))
                make_rest(c.next(4))
                gated_hidden(s + 1, nt, b)

            def ffn(k, steps, gate):
                c0, s0 = at3[k], STEP0[k]
                feed(c0 + 2 + AHEAD)
                gated_hidden(s0, T)
                ffn_step(At(c0 + 2), s0, T)
                with dve.Fori(0, (steps - 2) // 2) as i:
                    for j in range(2):
                        ffn_step(At(c0 + 5 + 3 * j, i, RAW), i * 2 + (s0 + 1 + j), T)
                done = 1 + 2 * ((steps - 2) // 2)
                for s in range(done, steps - 1):
                    ffn_step(At(c0 + 2 + 3 * s), s0 + s, T)
                fed[0] = c0 + 2 + 3 * (steps - 1) + AHEAD
                turned_rest(s0 + steps - 1, T)
                dve.wait_ge(chunk_used, c0 + 3 * steps)
                for t in range(T):
                    y = pair[1 + t][:, :, :].rearrange("p b n -> p (b n)")
                    if gate is None:
                        did(dve.tensor_tensor(x[:, t, :], x[:, t, :], y, ALU.add))
                    else:
                        did(dve.tensor_tensor(xn[:, t, :], y, gate, ALU.mult))
                now()
                dve.sem_inc(sem("ffn_read"), 1)
                if gate is not None:
                    did(dve.tensor_tensor(x[:, :, :], x[:, :, :], xn[:, :, :], ALU.add))

            did(dve.memset(cHL[:, :].bitcast(F32), 0.0))
            dve.wait_ge(sem("params_turned"), 1)
            did(dve.tensor_copy(prm[:, :], tb[0][:, :]))
            now()
            dve.sem_inc(sem("params_ready"), 1)
            condition(0)
            feed(SPL)
            dve.wait_ge(sem("lambdas_landed"), 64)
            for l in range(2):
                for i in range(2):
                    did(dve.tensor_tensor_reduce(lamrow[:, 2 * i, l, 0:64], lamrow[:, 2 * i, l, 0:64], lamrow[:, 2 * i + 1, l, 0:64],
                                                 1.0, 0.0, ALU.mult, ALU.add, lam4[:, 2 * i + l:2 * i + l + 1]))
            now()
            dve.sem_inc(sem("lam_dots"), 1)
            dve.wait_ge(sem("lam_exp"), 1)
            did(dve.tensor_tensor(lam4[:, 0:2], lam4[:, 2:4], lam4[:, 0:2], ALU.subtract))
            now()
            for l in range(2):
                did(dve.tensor_scalar(lam4[:, l:l + 1], lam4[:, l:l + 1], -lam_init[l], None, ALU.add))
            now()
            dve.sem_inc(sem("lam_rows"), 1)
            for l in range(2):
                did(dve.tensor_scalar(lamc[:, 2 + l:3 + l], pcol("subln_g", l), 1.0 - lam_init[l], None, ALU.mult))
            lam = pcol("lru_lambda_3", 0, 8)
            az, ez, s_, s2, p_ = (tmp8[:, 8 * i:8 * i + 8] for i in (0, 1, 2, 3, 0))
            did(dve.tensor_scalar(s2, lam, -1.0, None, ALU.mult))
            now()
            did(dve.tensor_tensor(az, s2, lam, ALU.max))
            now()
            dve.sem_inc(sem("lru_decay_in"), 1)
            dve.wait_ge(sem("lru_decay_exp"), 1)
            did(dve.tensor_scalar(s_, ez, 2.0, None, ALU.add))
            now()
            did(dve.reciprocal(s_, s_))
            now()
            did(dve.tensor_tensor(s_, s_, ez, ALU.mult))
            now()
            did(dve.tensor_tensor(s2, s_, s_, ALU.mult))
            now()
            did(dve.tensor_scalar(p_, s2, 1.0 / 17, 1.0 / 15, ALU.mult, ALU.add))
            for n in (13, 11, 9, 7, 5, 3, 1):
                now()
                did(dve.tensor_tensor(p_, p_, s2, ALU.mult))
                now()
                did(dve.tensor_scalar(p_, p_, 1.0 / n, None, ALU.add))
            now()
            did(dve.tensor_tensor(p_, p_, s_, ALU.mult))
            did(dve.tensor_scalar(s2, lam, -1.0, 0.0, ALU.mult, ALU.max))
            now()
            did(dve.scalar_tensor_tensor(out=p_, in0=p_, scalar=2.0, in1=s2, op0=ALU.mult, op1=ALU.add))
            now()
            did(dve.tensor_scalar(sp8, p_, -8.0, None, ALU.mult))
            feed(2 * SPL)
            dve.wait_ge(sem("positions_landed"), 16)
            did(dve.tensor_copy(angle, posi))
            now()
            angles(0)
            dve.wait_ge(sem("x_landed"), 16)
            nn = 0
            for l in range(2):
                mod(*mods[l])
                if l == 0:
                    dve.wait_ge(sem("lam_spread"), 1)
                    did(dve.tensor_copy(lamc[:, 0:2], tb[1][:, 100:102]))
                norm(nn, gs[:, 0:8], sh[:, 0:8])
                nn += 1
                feed(last_chunk(f"gb{l}") + 1 + AHEAD)
                dve.wait_ge(evac["act"], plan.jobs[f"gb{l}"][4])
                did(dve.tensor_tensor(upad[:, :, PADS:], upad[:, :, PADS:], oT[:, :, :], ALU.mult))
                now()
                dve.sem_inc(sem("u_ready"), 1)
                feed(last_chunk(f"q{l}") + AHEAD)
                conv_taps(l, range(0, 5))
                feed(last_chunk(f"q{l}") + 1 + AHEAD)
                feed(last_chunk(f"k{l}") + AHEAD)
                conv_taps(l, range(5, 10))
                feed(last_chunk(f"k{l}") + 1 + AHEAD)
                rope(l)
                feed(last_chunk(f"v{l}") + AHEAD)
                conv_taps(l, range(10, 13))
                feed(last_chunk(f"v{l}") + 1 + AHEAD)
                mask_and_max(l, 0)
                mask_and_max(l, 1)
                conv_taps(l, range(13, 15))
                probs(l, 0)
                feed(last_chunk(f"gates{l}.0") + AHEAD)
                probs(l, 1)
                feed(last_chunk(f"gates{l}.0") + 1 + AHEAD)
                conv_taps(l, range(15, 18))
                feed(last_chunk(f"gates{l}.1") + AHEAD)
                conv_taps(l, range(18, 23))
                feed(last_chunk(f"gates{l}.1") + 1 + AHEAD)
                dve.wait_ge(evac["act"], plan.jobs[f"pv{l}"][4])
                did(dve.tensor_tensor(kq[0], oT[:, :, :], oT[:, :, :], ALU.mult))
                now()
                dve.sem_inc(sem("squares_ready"), 1)
                conv_taps(l, range(23, 26))
                feed(last_chunk(f"gates{l}.2") + AHEAD)
                conv_taps(l, range(26, 28))
                feed(last_chunk(f"gates{l}.2") + 1 + AHEAD)
                column_mean_job(f"subln{l}", kq[1], P, 1e-5)
                dve.sem_inc(sem("sub_var"), 1)
                conv_taps(l, range(28, CONV_K))
                now()
                dve.sem_inc(sem("squares_ready"), 1)
                dve.wait_ge(sem("sub_root"), l + 1)
                did(dve.reciprocal(kq[1], kq[1]))
                now()
                did(dve.scalar_tensor_tensor(out=hT[:, 0:4, :].rearrange("p k s -> p (k s)"), in0=oT[:, :, :].rearrange("p k s -> p (k s)"),
                                             scalar=lamc[:, 2 + l:3 + l], in1=qkv[:, 1, :], op0=ALU.mult, op1=ALU.mult))
                now()
                dve.sem_inc(sem("hT_ready"), 1)
                feed(last_chunk(f"gates{l}.3") + 1 + AHEAD)
                split_rest(f"attn{l}", 0, 4)
                column_mean_job(f"lnmean{l}", kq[0][:, 0, :], W)
                did(dve.tensor_tensor(conv, conv, over(kq[0][:, 0, :], [P, KW, S], 1), ALU.subtract))
                now()
                did(dve.tensor_tensor(kq[2], conv, conv, ALU.mult))
                now()
                dve.sem_inc(sem("squares_ready"), 1)
                gate_product(f"yattn{l}", gateA, (0,))
                column_mean_job(f"lnvar{l}", kq[1][:, 0, :], W, 1e-5)
                dve.sem_inc(sem("ln_var"), 1)
                dve.wait_ge(sem("ln_root"), l + 1)
                did(dve.reciprocal(kq[1][:, 0, :], kq[1][:, 0, :]))
                now()
                did(dve.tensor_tensor(conv, conv, over(kq[1][:, 0, :], [P, KW, S], 1), ALU.mult))
                now()
                dve.sem_inc(sem("ln_ready"), 1)
                dve.sem_inc(sem("hT_ready"), 1)
                split_rest(f"conv{l}", 4, 8)
                gate_product(f"yattn{l}", gateA, (1,))
                merge(l, "yconv", gateB)
                dve.sem_inc(sem("hT_ready"), 1)
                dve.sem_inc(sem("hT_ready"), 1)
                add_product(f"wout{l}", gbc[:, 0, :])
                norm(nn, gs[:, 8:16], sh[:, 8:16])
                nn += 1
                ffn(*DENSE[l], gbc[:, 1, :])
            last_norm((0, 0), x)
            dve.wait_ge(sem("pool_landed"), 48)
            angles(1)
            mod(*mods[2])
            norm(nn, gs[:, 0:8], sh[:, 0:8])
            nn += 1
            for name in ("up", "zp", "q2", "k2"):
                feed(last_chunk(name) + 1 + AHEAD)
            rope(2)
            feed(last_chunk("v2") + 1 + AHEAD)
            dve.wait_ge(evac["act"], plan.jobs["zp"][4])
            src = upad[:, :, PADS:]
            for level in range(4):
                dst, h = POOLBUF[level % 2], 2 ** level
                did(dve.tensor_copy(dst[:, level:, 0:h], src[:, level:, 0:h]))
                did(dve.tensor_tensor(dst[:, level:, h:], src[:, level:, h:], src[:, level:, 0:S - h], ALU.add))
                now()
                src = dst
            for g in range(4):
                did(dve.tensor_tensor(dpool[:, g, :], POOLBUF[g % 2][:, g, :], invcnt[:, g, :], ALU.mult))
            now()
            did(dve.tensor_tensor(dpool, dpool, upad[:, :, PADS:], ALU.subtract))
            now()
            dve.sem_inc(sem("pool_ready"), 1)
            for name in ["gates2.0", "gates2.1", "gates2.2", "gates2.3", "za"]:
                feed(last_chunk(name) + 1 + AHEAD)
            dve.wait_ge(job_done, jobs_done("pool"))
            for g in range(KW):
                ins = dve.scalar_tensor_tensor(out=hT[:, 4 + g, :], in0=flat4(bank("pool"))[:, g, :], scalar=pcol("pool_scale_2", g),
                                               in1=xn[:, 0, g * S:(g + 1) * S], op0=ALU.mult, op1=ALU.mult)
            ins.then_inc(evac["dve"], 1)
            dve.wait_ge(evac["dve"], plan.jobs["pool"][4])
            dve.sem_inc(sem("hT_ready"), 1)
            split_rest("conv2", 4, 8)
            gate_product("yconv2", gateA)
            for q in range(T):
                mask_and_max(2, q)
            for q in range(T):
                probs(2, q)
            dve.wait_ge(evac["act"], plan.jobs["pv2"][4])
            did(dve.tensor_tensor(hT[:, 0:4, :], oT[:, :, :], upad[:, :, PADS:], ALU.mult))
            now()
            dve.sem_inc(sem("hT_ready"), 1)
            split_rest("attn2", 0, 4)
            merge(2, "yattn", gateB)
            dve.sem_inc(sem("hT_ready"), 1)
            dve.sem_inc(sem("hT_ready"), 1)
            add_product("wout2", gbc[:, 0, :])
            last_norm((1, 1), x)
            did(dve.memset(upu[:, :, 0:3], 0.0))
            now()
            dve.sem_inc(sem("upu_zero"), 1)
            for l in range(2):
                norm(nn, col8("norm_mix_3", l))
                nn += 1
                feed(last_chunk(f"bg{l}") + 1 + AHEAD)
                ps = job(f"vv{l}")
                dve.wait_ge(evac["act"], plan.jobs[f"cg{l}"][4])
                dve.tensor_tensor(upad[:, :, PADS:], flat4(ps), kq[0], ALU.mult).then_inc(evac["dve"], 1)
                dve.wait_ge(evac["dve"], plan.jobs[f"vv{l}"][4])
                feed(last_chunk(f"uu{l}") + 1 + AHEAD)
                y = hT[:, 0:4, :]
                ya = aw4[2]
                for k in range(3):
                    now()
                    for g in range(KW):
                        w_, src = pcol("conv_w_3", 12 * l + 4 * k + g), upad[:, g, PADS - 2 + k:PADS - 2 + k + S]
                        if k == 0:
                            did(dve.tensor_scalar(ya[:, g, :], src, w_, None, ALU.mult))
                        else:
                            did(dve.scalar_tensor_tensor(out=ya[:, g, :], in0=src, scalar=w_, in1=ya[:, g, :], op0=ALU.mult, op1=ALU.add))
                now()
                feed(last_chunk(f"gg{l}") + 1)
                dve.wait_ge(evac["act"], plan.jobs[f"uu{l}"][4])
                for k in range(4):
                    now()
                    for g in range(KW):
                        w_, src = pcol("lru_conv_w_3", 16 * l + 4 * k + g), upu[:, g, k:k + S]
                        if k == 0:
                            did(dve.tensor_scalar(oT[:, g, :], src, w_, pcol("lru_conv_b_3", 4 * l + g), ALU.mult, ALU.add))
                        else:
                            did(dve.scalar_tensor_tensor(out=oT[:, g, :], in0=src, scalar=w_, in1=oT[:, g, :], op0=ALU.mult, op1=ALU.add))
                now()
                dve.sem_inc(sem("uc_ready"), 1)
                feed(last_chunk(f"gg{l}") + 1 + AHEAD)
                did(dve.tensor_tensor(y, ya, kq[1], ALU.mult))
                now()
                dve.sem_inc(sem("hT_ready"), 1)
                dve.sem_inc(sem("ya_read"), 1)
                dve.wait_ge(evac["act"], plan.jobs[f"lrui{l}"][4])
                did(dve.tensor_tensor(aw4[1], aw4[1], oT[:, :, :], ALU.mult))
                now()
                dve.wait_ge(sem("lru_exp"), l + 1)
                did(dve.tensor_tensor(oT[:, :, :], lru_a, lru_a, ALU.mult))
                now()
                dve.wait_ge(sem("lru_tanh"), l + 1)
                did(dve.scalar_tensor_tensor(out=aw[:, 2048:3072], in0=oT[:, :, :].rearrange("p g s -> p (g s)"), scalar=1.0,
                                             in1=aw[:, 2048:3072], op0=ALU.add, op1=ALU.mult))
                now()
                dve.sem_inc(sem("b_square"), 1)
                split_rest(f"lru{l}.0", 0, 4)
                dve.wait_ge(sem("b_root"), l + 1)
                did(dve.tensor_tensor(aw4[1], aw4[1], aw4[2], ALU.mult))
                now()
                for g in range(KW):
                    did(dve.tensor_tensor_scan(oT[:, g, :], lru_a[:, g, :], aw4[1][:, g, :], 0.0, ALU.mult, ALU.add))
                now()
                dve.wait_ge(evac["act"], plan.jobs[f"gg{l}"][4])
                did(dve.tensor_tensor(hT[:, 4:8, :], oT[:, :, :], kq[2], ALU.mult))
                now()
                dve.sem_inc(sem("hT_ready"), 1)
                split_rest(f"lru{l}.1", 4, 8)
                add_product(f"wout{3 + l}", None)
                norm(nn, col8("norm_ffn_3", l))
                nn += 1
                if l == 0:
                    ffn(*DENSE[2], None)
            dve.wait_ge(sem("logits_done"), 1)
            for t in range(T):
                did(dve.tensor_copy(lg[:, t, :], tb[1][:, 8 * t:8 * t + 8]))
            now()
            i8 = iota[:, 0:E]
            picks = ((m1, sel), (m2, o8))
            for n, (m, pick) in enumerate(picks):
                did(dve.tensor_reduce(m, lg, AX.X, ALU.max))
                now()
                did(dve.tensor_tensor(w8, lg, over(m, [P, T, E], 2), ALU.is_equal))
                now()
                did(dve.scalar_tensor_tensor(out=w8, in0=w8, scalar=-99.0, in1=over(i8, [P, T, E], 1), op0=ALU.mult, op1=ALU.add))
                now()
                did(dve.tensor_reduce(rstd, w8, AX.X, ALU.min))
                now()
                did(dve.tensor_tensor(pick, w8, over(rstd, [P, T, E], 2), ALU.is_equal))
                now()
                if n == 0:
                    did(dve.scalar_tensor_tensor(out=lg, in0=pick, scalar=-3.0e38, in1=lg, op0=ALU.mult, op1=ALU.add))
                    now()
            did(dve.tensor_tensor(m2, m2, m1, ALU.subtract))
            now()
            dve.sem_inc(sem("gap_ready"), 1)
            dve.wait_ge(sem("gap_exp"), 1)
            did(dve.tensor_scalar(m1, m2, 1.0, None, ALU.add))
            now()
            did(dve.reciprocal(m1, m1))
            now()
            did(dve.tensor_tensor(m2, m2, m1, ALU.mult))
            now()
            for t in range(T):
                did(dve.tensor_scalar(comb[:, t, :], sel[:, t, :], m1[:, t:t + 1], None, ALU.mult))
            now()
            for t in range(T):
                did(dve.scalar_tensor_tensor(out=comb[:, t, :], in0=o8[:, t, :], scalar=m2[:, t:t + 1], in1=comb[:, t, :], op0=ALU.mult, op1=ALU.add))
            did(dve.tensor_tensor(sel, sel, o8, ALU.add))
            now()
            dve.sem_inc(sem("chosen"), 1)
            dve.wait_ge(sem("ranks_done"), 1)
            did(dve.tensor_copy(pos.rearrange("p t e -> p (t e)"), tb[1][:, 32:48]))
            did(dve.tensor_reduce(rstd[:, 0:1], tb[1][:, 48:56], AX.X, ALU.max))
            now()
            did(dve.tensor_scalar(wins[0:1, 0:1], rstd[0:1, 0:1], float(P), None, ALU.is_gt))
            now()
            dve.sem_inc(sem("windows_ready"), 1)
            feed(MOE0 + 2)

            def pick(column):
                for t in range(T):
                    ins = dve.tensor_scalar(ptok[:, t, :], iota, column(128 + E * t), column(160 + E * t), ALU.is_equal, ALU.mult)
                ins.then_inc(sem("picks_ready"), 1)

            def gathered_rest(count):
                dve.wait_ge(sem("gather_done"), count)
                dve.tensor_tensor(xe, pair[2][:, :, :].rearrange("p b (k s) -> p (b k) s", s=P),
                                  over(col8("norm_ffn_3", 1), [P, KD, P], 2), ALU.mult).then_inc(sem("gathered"), 1)
                dve.wait_ge(sem("xe_head"), count)
                dve.tensor_tensor(hTl[:, :, 0:P], xe, hTh[:, :, 0:P].bitcast(F32), ALU.subtract).then_inc(sem("xe_rest"), 1)

            def expert(it, e, window):
                s0 = it * STEPS3 + STEP0[3]
                for t in range(T):
                    ins = dve.tensor_scalar(pcomb[:, t, :], iota, pos[:, t, bass.ds(e, 1)], comb[:, t, bass.ds(e, 1)], ALU.is_equal, ALU.mult)
                ins.then_inc(sem("combine_picked"), 1)
                pick(lambda c: sm[:, bass.ds(e + (c + 1), 1)])
                at = At(MOE0, it, PER)
                make_rest(at.next(2))
                make_rest(at.next(3))
                gated_hidden(s0, 1, 0)
                for s in range(STEPS3 - 1):
                    ffn_step(at.next(2 + 3 * s), s0 + s, 1, (s + 1) % 2)
                turned_rest(s0 + (STEPS3 - 1), 1)
                make_rest(at.next(PER + 1))
                gathered_rest(it + (window + 2))
                for t in range(T):
                    dve.wait_ge(sem("scattered"), it * 2 + (t + 1))
                    dve.tensor_tensor(x[:, t, :], x[:, t, :], pair[2 - t][:, :, :].rearrange("p b n -> p (b n)"),
                                      ALU.add).then_inc(sem("scatter_added"), 1)

            pick(lambda c: sm[:, c:c + 1])
            gathered_rest(1)
            dve.sem_inc(sem("scatter_added"), 2)
            with dve.Fori(0, E) as e:
                expert(e, e, 0)
            more = dve.value_load(wins[0:1, 0:1], min_val=0, max_val=1)
            with dve.If(more):
                dve.wait_ge(sem("scatter_added"), 2 * E + 2)
                dve.tensor_scalar(pos.rearrange("p t e -> p (t e)"), pos.rearrange("p t e -> p (t e)"), -float(P), None,
                                  ALU.add).then_inc(sem("window_moved"), 1)
                dve.wait_ge(sem("window_moved"), 1)
                pick(lambda c: sm[:, c:c + 1])
                gathered_rest(E + 2)
                with dve.Fori(0, E) as e:
                    expert(e + E, e, 1)
            dve.wait_ge(sem("scatter_added"), more * (2 * E) + (2 * E + 2))
            for t in range(T):
                did(dve.tensor_tensor_reduce(xn[:, t, :], x[:, t, :], x[:, t, :], 1.0, 0.0, ALU.mult, ALU.add, ss[:, t:t + 1]))
            now()
            dve.tensor_scalar(ss, ss, 1.0 / D, 1e-6, ALU.mult, ALU.add).then_inc(sem("last_mean_square"), 1)
            dve.wait_ge(sem("last_root"), 1)
            did(dve.reciprocal(rstd, rstd))
            now()
            dve.wait_ge(sem("final_g_landed"), 48)
            for t in range(T):
                ins = dve.scalar_tensor_tensor(out=xn[:, t, :], in0=x[:, t, :], scalar=rstd[:, t:t + 1], in1=gbc[:, 1, :],
                                               op0=ALU.mult, op1=ALU.mult)
            ins.then_inc(sem("block_done"), 1)

        @block.tensor
        def _(pe):
            def free(name):
                b = plan.before(name)
                if b:
                    pe.wait_ge(evac[b[0]], b[1])

            def three(out_, lh, ll, rh, rl, start, stop):
                pe.matmul(out_, lh, rh, start=start, stop=False, skip_group_check=True)
                pe.matmul(out_, lh, rl, start=False, stop=False, skip_group_check=True)
                return pe.matmul(out_, ll, rh, start=False, stop=stop, skip_group_check=True)

            def linear(name, cols, k0=0, turn=False, splits=()):
                for j in range(cols // NT):
                    job_ = f"{name}.{j}" if cols > NT else name
                    n, c0, nch = plan.jobs[job_][0:3]
                    free(job_)
                    ps = pair[n % 3]
                    for ch in range(nch):
                        c = At(c0 + ch)
                        if j == 0 and ch < len(splits):
                            ready(splits[ch])
                        pe.wait_ge(rests_done, c.count())
                        for k in range(4):
                            kk = k0 + 4 * ch + k
                            first, last = ch == 0 and k == 0, ch == nch - 1 and k == 3
                            if turn:
                                for i in range(4):
                                    wcols = slice(k * NT + i * P, k * NT + (i + 1) * P)
                                    ins = three(flat4(ps)[:, i, :], head[:, c.split, wcols], rest[:, c.split, wcols],
                                                hTh[:, kk, :], hTl[:, kk, :], first and i % 2 == 0, last)
                            else:
                                wcols = slice(k * NT, (k + 1) * NT)
                                for t in range(T):
                                    toks = slice(t * P, (t + 1) * P)
                                    ins = three(ps[:, t, :], hTh[:, kk, toks], hTl[:, kk, toks],
                                                head[:, c.split, wcols], rest[:, c.split, wcols], first, last)
                        ins.then_inc(chunk_used, 1)

            def mod_finish(k, j, before_):
                pe.wait_ge(evac["act"], plan.jobs[f"mod{k}.{j}"][4])
                pe.wait_ge(sem("bias_row"), 16 * (before_ + j + 1))
                if j in (2, 5):
                    free(f"gate{k}.{j}")
                    for b in range(2):
                        ins = pe.matmul(bank(f"gate{k}.{j}")[:, b, :], ones[0:3, :], modrow[0:3, b * NT:(b + 1) * NT], start=True, stop=True)
                else:
                    if j == 0 and k > 0:
                        pe.wait_ge(sem("modcols_read"), k)
                    if j == 0 and k == 0:
                        pe.wait_ge(sem("params_ready"), 1)
                    for i in range(KD):
                        ins = pe.matmul(tb[1][:, 8 * j + i:8 * j + i + 1], modrow[0:3, i * P:(i + 1) * P], ones[0:3, 0:1], start=True, stop=True)
                ins.then_inc(sem("modrow_used"), 1)
                if j in (2, 5):
                    pe.wait_ge(sem("modrow_used"), before_ + j + 1)
                    pe.sem_inc(job_done, 1)

            def mod(k, slices, before_):
                pe.wait_ge(sem("cond_split"), k // 2 + 1)
                for j in range(slices):
                    n, c0, nch = plan.jobs[f"mod{k}.{j}"][0:3]
                    free(f"mod{k}.{j}")
                    ps = pair[n % 3]
                    for ch in range(nch):
                        c = At(c0 + ch)
                        pe.wait_ge(rests_done, c.count())
                        for i in range(4):
                            kk = 4 * (ch % 2) + i
                            for w_ in (head, rest):
                                ins = pe.matmul(ps[0:66, ch // 2, :], cHL[:, 2 * kk:2 * kk + 66], w_[:, c.split, i * NT:(i + 1) * NT],
                                                start=kk == 0 and w_ is head, stop=kk == 7 and w_ is rest)
                        ins.then_inc(chunk_used, 1)
                        if ch == 0 and j > 0:
                            mod_finish(k, j - 1, before_)
                mod_finish(k, slices - 1, before_)

            def turn4(name, src):
                free(name)
                for i in range(4):
                    for t in range(T):
                        ins = pe.transpose(flat4(bank(name))[:, i, t * P:(t + 1) * P], src(i, t), ident)
                ins.then_inc(job_done, 1)

            def norm(n):
                pe.wait_ge(sem("xn_ready"), 2 * n + 2)
                for j in range(2):
                    turn4(f"norm{n}.{j}", lambda i, t: xn[:, t, (4 * j + i) * P:(4 * j + i + 1) * P])

            def ready(name):
                pe.wait_ge(htl_ready, plan.splits[name])

            combos = ((0, 0), (1, 0), (1, 1))

            def rotate(k):
                for name, job_, buf in (("rotq", f"q{k}", qT), ("rotk", f"k{k}", kT)):
                    free(f"{name}{k}")
                    pe.wait_ge(evac["act"], plan.jobs[job_][4])
                    for g in range(KW):
                        ins = pe.matmul(flat4(bank(f"{name}{k}"))[:, g, :], rot, buf[:, g, :], start=True, stop=True)
                    ins.then_inc(job_done, 1)

            def scores(k):
                pe.wait_ge(sem("roped"), 2 * k + 2)
                for name, q, gg in ((f"score0.{k}", 0, range(4)), (f"score1a.{k}", 1, (0, 1)), (f"score1b.{k}", 1, (2, 3))):
                    free(name)
                    L = P * (q + 1)
                    for i, g in enumerate(gg):
                        for r in range(2):
                            rows = slice(64 * r, 64 * r + 64)
                            ins = pe.matmul(bank(name)[:, r, i * L:(i + 1) * L], qT[rows, g, q * P:(q + 1) * P], kT[rows, g, 0:L],
                                            start=True, stop=True)
                    ins.then_inc(job_done, 1)

            def apply_scores(k):
                groups = [(ci, r) for ci in range(3) for r in range(1 if k < 2 else 2)]
                for j in range(2 if k < 2 else 3):
                    free(f"turn{k}.{j}")
                    for b, (ci, r) in enumerate(groups[2 * j:2 * j + 2]):
                        q, kt = combos[ci]
                        pe.wait_ge(sem("probs_ready"), 2 * k + q + 1)
                        for h in range(4):
                            ins = pe.transpose(bank(f"turn{k}.{j}")[:, b, h * P:(h + 1) * P], (sc0, sc1)[q][:, 4 * r + h, kt * P:(kt + 1) * P], ident)
                    ins.then_inc(job_done, 1)
                free(f"pv{k}")
                pe.wait_ge(evac["act"], plan.jobs[f"turn{k}.{1 if k < 2 else 2}"][4])
                ps = flat4(bank(f"pv{k}"))
                for g in range(4):
                    for r in range(1 if k < 2 else 2):
                        rows = slice(0, P) if k < 2 else slice(64 * r, 64 * r + 64)
                        vcols = slice(g * P, (g + 1) * P) if k < 2 else slice((2 * g + r) * 64, (2 * g + r + 1) * 64)
                        for ci, (q, kt) in enumerate(combos):
                            src = aT[:, ci if k < 2 else 2 * ci + r, g * P:(g + 1) * P]
                            ins = pe.matmul(ps[rows, g, q * P:(q + 1) * P], vt[:, kt, vcols], src, start=kt == 0, stop=kt == q)
                ins.then_inc(job_done, 1)

            def mix(k):
                for j in range(2):
                    pe.wait_ge(sem("merged"), 2 * k + j + 1)
                    turn4(f"mix{k}.{j}", lambda i, t: gateA[:, t, (4 * j + i) * P:(4 * j + i + 1) * P])
                linear(f"wout{k}", D, splits=(f"mix{k}.0", f"mix{k}.1"))

            def gate_up(c, s, half, nt, b, wait_for):
                if half == 0:
                    wait(pe, act_ready, wait_for)
                pe.wait_ge(rests_done, c.count())
                wh = head[:, c.split, :].rearrange("p (m k n) -> p m k n", m=2, k=4)
                wl = rest[:, c.split, :].rearrange("p (m k n) -> p m k n", m=2, k=4)
                for k in range(4):
                    for t in range(nt):
                        toks = slice(t * P, (t + 1) * P)
                        ins = three(pair[0][:, b + t, :].rearrange("p (m n) -> p m n", m=2), hTh[:, 4 * half + k, toks], hTl[:, 4 * half + k, toks],
                                    wh[:, :, k, :], wl[:, :, k, :], half == 0 and k == 0, half == 1 and k == 3)
                        if k == 3 and t == nt - 1:
                            ins.then_inc(chunk_used, 1)

            def turn_hidden(s, nt):
                pe.wait_ge(act_ready, s + 1)
                wait(pe, atl_ready, s)
                for t in range(nt):
                    for k in range(2):
                        ins = pe.transpose(tb[0][:, k * S + t * P:k * S + (t + 1) * P], act_[:, t, k * P:(k + 1) * P], ident)
                ins.then_inc(turned, 1)

            def down(c, s, nt, first, last):
                pe.wait_ge(rests_done, c.count())
                pe.wait_ge(atl_ready, s + 1)
                for k in range(2):
                    for t in range(nt):
                        toks = slice(t * P, (t + 1) * P)
                        for n in range(2):
                            wcols = slice(k * D + n * NT, k * D + (n + 1) * NT)
                            ins = three(pair[1 + t][:, n, :], aTh[:, k, toks], aTl[:, k, toks], head[:, c.split, wcols],
                                        rest[:, c.split, wcols], first and k == 0, last and k == 1)
                ins.then_inc(chunk_used, 1)

            def ffn_step(c, s, nt, first, b=0, lag=0):
                gate_up(c, s + 1, 0, nt, b, s + 1 - lag)
                turn_hidden(s, nt)
                gate_up(c.next(1), s + 1, 1, nt, b, None)
                down(c.next(2), s, nt, first, False)

            def ffn(k, steps, splits):
                c0, s0 = at3[k], STEP0[k]
                for eng in ("act", "dve"):
                    pe.wait_ge(evac[eng], counts_at[k][eng])
                ready(splits[0])
                gate_up(At(c0), s0, 0, T, 0, s0)
                ready(splits[1])
                gate_up(At(c0 + 1), s0, 1, T, 0, None)
                ffn_step(At(c0 + 2), s0, T, True)
                with pe.Fori(0, (steps - 2) // 2) as i:
                    for j in range(2):
                        ffn_step(At(c0 + 5 + 3 * j, i, RAW), i * 2 + (s0 + 1 + j), T, False)
                done = 1 + 2 * ((steps - 2) // 2)
                for s in range(done, steps - 1):
                    ffn_step(At(c0 + 2 + 3 * s), s0 + s, T, False)
                turn_hidden(s0 + steps - 1, T)
                c = At(c0 + 2 + 3 * (steps - 1))
                down(c, s0 + steps - 1, T, False, True)
                pe.wait_ge(sem("ffn_read"), k + 1)

            def sum_over_partitions(name, buf, n):
                free(name)
                if n == 1:
                    for b in range(2):
                        ins = pe.matmul(bank(name)[:, b, :], ones[:, :], buf[:, b * NT:(b + 1) * NT], start=True, stop=True)
                else:
                    for g in range(n):
                        ins = pe.matmul(bank(name)[:, 0, 0:S], ones[:, :], buf[:, g, :], start=g == 0, stop=g == n - 1)
                ins.then_inc(job_done, 1)

            pe.wait_ge(sem("const_landed"), 16)
            pe.wait_ge(sem("ones_ready"), 1)
            pe.wait_ge(sem("params_landed"), 16)
            for i in range(PARAM_TILES):
                ins = pe.transpose(tb[0][:, i * P:(i + 1) * P], praw[:, i, :], ident)
            ins.then_inc(sem("params_turned"), 1)
            nn = 0
            for l in range(2):
                mod(*mods[l])
                if l == 0:
                    pe.wait_ge(sem("lam_rows"), 1)
                    pe.wait_ge(sem("modcols_read"), 1)
                    pe.matmul(tb[1][:, 100:102], ones[0:1, :], lam4[:, 0:2], start=True, stop=True).then_inc(sem("lam_spread"), 1)
                norm(nn)
                linear(f"ga{l}", 512, turn=True, splits=(f"norm{nn}.0", f"norm{nn}.1"))
                nn += 1
                linear(f"gb{l}", 512, turn=True)
                linear(f"q{l}", 512, turn=True)
                linear(f"k{l}", 512, turn=True)
                rotate(l)
                linear(f"v{l}", 512)
                scores(l)
                linear(f"gates{l}.0", NT)
                linear(f"gates{l}.1", NT)
                apply_scores(l)
                linear(f"gates{l}.2", NT)
                pe.wait_ge(sem("squares_ready"), 3 * l + 1)
                sum_over_partitions(f"subln{l}", qkv[:, 0, :], 1)
                linear(f"gates{l}.3", NT)
                pe.wait_ge(sem("squares_ready"), 3 * l + 2)
                pe.wait_ge(sem("conv_half_done"), l + 1)
                sum_over_partitions(f"lnmean{l}", conv, KW)
                linear(f"yattn{l}.0", NT, splits=(f"attn{l}",))
                pe.wait_ge(sem("squares_ready"), 3 * l + 3)
                sum_over_partitions(f"lnvar{l}", kq[2], KW)
                linear(f"yattn{l}.1", NT)
                linear(f"yconv{l}", D, k0=4, splits=(f"conv{l}",))
                mix(l)
                norm(nn)
                ffn(*DENSE[l], splits=(f"norm{nn}.0", f"norm{nn}.1"))
                nn += 1
            mod(*mods[2])
            norm(nn)
            linear("up", 512, turn=True, splits=(f"norm{nn}.0", f"norm{nn}.1"))
            nn += 1
            for name in ("zp", "q2", "k2"):
                linear(name, 512, turn=True)
            rotate(2)
            linear("v2", 512)
            for j in range(4):
                linear(f"gates2.{j}", NT)
            linear("za", 512, turn=True)
            pe.wait_ge(sem("pool_ready"), 1)
            pe.wait_ge(sem("pool_landed"), 48)
            free("pool")
            for g in range(KW):
                ins = pe.matmul(flat4(bank("pool"))[:, g, :], wgrp[:, g, :], dpool[:, g, :], start=True, stop=True)
            ins.then_inc(job_done, 1)
            linear("yconv2", D, k0=4, splits=("conv2",))
            scores(2)
            apply_scores(2)
            linear("yattn2", D, splits=("attn2",))
            mix(2)
            for l in range(2):
                norm(nn)
                for name in ("cg", "bg", "vv", "uu", "gg"):
                    linear(f"{name}{l}", 512, turn=True, splits=(f"norm{nn}.0", f"norm{nn}.1") if name == "cg" else ())
                nn += 1
                pe.wait_ge(sem("uc_ready"), l + 1)
                pe.wait_ge(sem("lru_landed"), 64 * (l + 1))
                for i, name in enumerate(("lrur", "lrui")):
                    free(f"{name}{l}")
                    for g in range(KW):
                        ins = pe.matmul(flat4(bank(f"{name}{l}"))[:, g, :], wbd[:, i, g, :], oT[:, g, :], start=True, stop=True)
                    ins.then_inc(job_done, 1)
                linear(f"wout{3 + l}", D, splits=(f"lru{l}.0", f"lru{l}.1"))
                norm(nn)
                if l == 0:
                    ffn(*DENSE[2], splits=(f"norm{nn}.0", f"norm{nn}.1"))
                    nn += 1
            pe.wait_ge(evac["dve"], plan.jobs["norm8.1"][4])
            pe.wait_ge(sem("router_landed"), 16)
            for t in range(T):
                for k in range(KD):
                    ins = pe.matmul(tb[1][:, E * t:E * t + E], hT[:, k, t * P:(t + 1) * P], wrt[:, k, :], start=k == 0, stop=k == KD - 1)
            ins.then_inc(sem("logits_done"), 1)
            pe.wait_ge(sem("chosen"), 1)
            pe.matmul(tb[1][:, 32:40], before, sel[:, 0, :], start=True, stop=True)
            pe.matmul(tb[1][:, 40:48], ones[:, :], sel[:, 0, :], start=True, stop=False)
            pe.matmul(tb[1][:, 40:48], before, sel[:, 1, :], start=False, stop=True)
            pe.matmul(tb[1][:, 48:56], ones[:, :], sel[:, 0, :], start=True, stop=False)
            pe.matmul(tb[1][:, 48:56], ones[:, :], sel[:, 1, :], start=False, stop=True).then_inc(sem("ranks_done"), 1)
            pe.wait_ge(htl_ready, plan.splits["norm8.1"])
            pe.wait_ge(sem("windows_ready"), 1)

            def gather(count):
                pe.wait_ge(sem("picks_ready"), count)
                for k in range(KD):
                    for t in range(T):
                        ins = pe.matmul(pair[2][:, k // 4, (k % 4) * P:(k % 4 + 1) * P], xn[:, t, k * P:(k + 1) * P], ptok[:, t, :],
                                        start=t == 0, stop=t == 1)
                ins.then_inc(sem("gather_done"), 1)

            def expert(it, window):
                s0 = it * STEPS3 + STEP0[3]
                at = At(MOE0, it, PER)
                pe.wait_ge(sem("xe_rest"), it + (window + 1))
                gate_up(at, s0, 0, 1, 0, s0 - 1)
                pe.wait_ge(sem("combine_picked"), it + 1)
                for t in range(T):
                    ins = pe.transpose(tb[1][:, t * P:(t + 1) * P], pcomb[:, t, :], ident)
                ins.then_inc(sem("combine_turned"), 1)
                gate_up(at.next(1), s0, 1, 1, 0, None)
                pe.wait_ge(sem("scatter_added"), it * 2 + 2)
                for s in range(STEPS3 - 1):
                    ffn_step(at.next(2 + 3 * s), s0 + s, 1, s == 0, (s + 1) % 2, 1)
                turn_hidden(s0 + (STEPS3 - 1), 1)
                gather(it + (window + 2))
                down(at.next(PER - 1), s0 + (STEPS3 - 1), 1, False, True)
                pe.wait_ge(sem("y_ready"), it + 1)
                pe.wait_ge(sem("gathered"), it + (window + 2))
                for t in range(T):
                    for n in range(2):
                        ins = pe.matmul(pair[2 - t][:, n, :], pslot[:, t * P:(t + 1) * P], ysb[:, n * NT:(n + 1) * NT], start=True, stop=True)
                    ins.then_inc(sem("scattered"), 1)

            gather(1)
            with pe.Fori(0, E) as e:
                expert(e, 0)
            more = pe.value_load(wins[0:1, 0:1], min_val=0, max_val=1)
            with pe.If(more):
                pe.wait_ge(sem("scatter_added"), 2 * E + 2)
                gather(E + 2)
                with pe.Fori(0, E) as e:
                    expert(e + E, 1)


INPUTS = ["x", "positions", "ada_w", "ada_b", "w_in", "lambda_q1", "lambda_k1", "lambda_q2", "lambda_k2",
          "w_attn_o", "w_conv_o", "w_out", "w_ffn_in", "w_ffn_out", "final_g", "w_ada_2", "b_ada_2", "w_in_2",
          "w_pool_grp_2", "w_pool_up_2", "w_attn_up_2", "w_out_2", "g_final_2", "norm_final_3", "w_in_3",
          "lru_wa_3", "lru_wx_3", "w_out_3", "ffn_w_gate_3", "ffn_w_up_3", "ffn_w_down_3", "w_router_3",
          "moe_w_gate_3", "moe_w_up_3", "moe_w_down_3"]


def kernel(**inputs):
    import numpy as np
    import concourse.bacc as bacc
    from concourse.bass_utils import run_bass_kernel_spmd as run

    nc = bacc.Bacc("TRN2", target_bir_lowering=False, num_devices=1)
    square, rows = shape_constants()
    given = {name: np.ascontiguousarray(inputs[name]) for name in INPUTS}
    table = [np.ascontiguousarray(inputs[name]).reshape(-1, P) for name, _ in PARAM_ROWS]
    table.append(np.zeros((PARAM_TILES * P - sum(n for _, n in PARAM_ROWS), P), np.float32))
    given["params"] = np.concatenate(table)
    given["square"], given["rows"] = square, rows
    arrays = {f"in_{name}": v for name, v in given.items()}
    a = {name: nc.dram_tensor(f"in_{name}", v.shape, mybir.dt.from_np(v.dtype), kind="ExternalInput").ap()
         for name, v in given.items()}
    out = nc.dram_tensor("result", (1, S, D), F32, kind="ExternalOutput").ap()
    build(nc, a, out)
    r = run(nc, [arrays], core_ids=[0])
    return r.results[0]["result"]
```
